# Optimizing a Trainium2 kernel written in Bass

```python
import jax, jax.numpy as jnp
from jax import lax
import numpy as np

D_MODEL = 1024
BATCH = 1
SEQ = 1024
DEPTH = 1

SB_HEADS = 16
SB_HEAD_DIM = 64
SB_WIDTH = SB_HEADS * SB_HEAD_DIM
SB_BLOCK = 128
GLA_HEADS = 4
GLA_KEY_WIDTH = D_MODEL // 2
GLA_VALUE_WIDTH = D_MODEL
GLA_DK = GLA_KEY_WIDTH // GLA_HEADS
GLA_DV = GLA_VALUE_WIDTH // GLA_HEADS
GLA_GATE_RANK = 16
GLA_GATE_TAU = 16.0
GLA_CHUNK = 64
D_FF = -(-8 * D_MODEL // (3 * 256)) * 256
RMS_EPS = 1e-6
IN_SIZES = (SB_WIDTH, SB_WIDTH, SB_WIDTH,
            GLA_KEY_WIDTH, GLA_KEY_WIDTH, GLA_VALUE_WIDTH, GLA_VALUE_WIDTH, GLA_GATE_RANK,
            D_MODEL, D_MODEL)
IN_WIDTH = sum(IN_SIZES)

kernel_name = "hybrid_stickbreak_gla_gated_block"

def rms_norm(x, g):
    xf = x.astype(jnp.float32)
    y = xf * lax.rsqrt(jnp.mean(xf * xf, axis=-1, keepdims=True) + RMS_EPS)
    return (y * g.astype(jnp.float32)).astype(x.dtype)

def stick_breaking_attention(q, k, v):
    b, h, s, dh = q.shape
    nb = s // SB_BLOCK
    scale = dh ** -0.5
    kf = k.astype(jnp.float32)
    vf = v.astype(jnp.float32)
    key_pos = jnp.arange(s)

    def block(i):
        start = i * SB_BLOCK
        qb = lax.dynamic_slice_in_dim(q, start, SB_BLOCK, axis=2).astype(jnp.float32)
        z = jnp.einsum('bhtd,bhsd->bhts', qb, kf) * scale
        q_pos = start + jnp.arange(SB_BLOCK)
        mask = key_pos[None, :] < q_pos[:, None]
        log_not = jnp.where(mask, jax.nn.log_sigmoid(-z), 0.0)
        after = lax.cumsum(log_not, axis=3, reverse=True) - log_not
        w = jnp.where(mask, jnp.exp(jax.nn.log_sigmoid(z) + after), 0.0)
        return jnp.einsum('bhts,bhsd->bhtd', w, vf)

    o = lax.map(block, jnp.arange(nb))
    o = jnp.transpose(o, (1, 0, 3, 2, 4)).reshape(b, s, h * dh)
    return o.astype(v.dtype)

def gla_chunked(q, k, v, log_a):
    b, h, s, dk = q.shape
    dv = v.shape[-1]
    nc = s // GLA_CHUNK

    def to_chunks(t):
        t = t.astype(jnp.float32)
        return jnp.moveaxis(t.reshape(b, h, nc, GLA_CHUNK, t.shape[-1]), 2, 0)

    qc = to_chunks(q * (dk ** -0.5))
    kc = to_chunks(k)
    vc = to_chunks(v)
    gc = to_chunks(log_a)
    causal = jnp.tril(jnp.ones((GLA_CHUNK, GLA_CHUNK), dtype=bool))

    def step(state, inp):
        qi, ki, vi, gi = inp
        cum = jnp.cumsum(gi, axis=2)
        o_inter = jnp.einsum('bhck,bhkv->bhcv', qi * jnp.exp(cum), state)
        diff = cum[:, :, :, None, :] - cum[:, :, None, :, :]
        decay = jnp.where(causal[:, :, None], jnp.exp(jnp.minimum(diff, 0.0)), 0.0)
        scores = jnp.einsum('bhik,bhjk,bhijk->bhij', qi, ki, decay)
        o_intra = jnp.einsum('bhij,bhjv->bhiv', scores, vi)
        last = cum[:, :, -1:, :]
        state = (state * jnp.exp(last[:, :, 0, :])[..., None]
                 + jnp.einsum('bhck,bhcv->bhkv', ki * jnp.exp(last - cum), vi))
        return state, o_inter + o_intra

    state0 = jnp.zeros((b, h, dk, dv), jnp.float32)
    _, o = lax.scan(step, state0, (qc, kc, vc, gc))
    o = jnp.moveaxis(o, 0, 2).reshape(b, h, s, dv)
    return jnp.transpose(o, (0, 2, 1, 3)).astype(v.dtype)

def setup_inputs(seed: int = 0) -> dict:
    key = jax.random.key(seed)
    ks = jax.random.split(key, 16)
    f32 = jnp.float32
    nrm = lambda k, shape, fan_in: jax.random.normal(k, shape, f32) * (fan_in ** -0.5)
    gain = lambda k, shape: 1.0 + 0.02 * jax.random.normal(k, shape, f32)
    return {
        "x": jax.random.normal(ks[0], (BATCH, SEQ, D_MODEL), f32),
        "norm1_g": gain(ks[1], (DEPTH, D_MODEL)),
        "w_in": nrm(ks[2], (DEPTH, D_MODEL, IN_WIDTH), D_MODEL),
        "sb_q_norm_g": gain(ks[3], (DEPTH, SB_HEAD_DIM)),
        "sb_k_norm_g": gain(ks[4], (DEPTH, SB_HEAD_DIM)),
        "gla_gate_w2": nrm(ks[5], (DEPTH, GLA_GATE_RANK, GLA_KEY_WIDTH), GLA_GATE_RANK),
        "gla_gate_b": 0.1 * jax.random.normal(ks[6], (DEPTH, GLA_KEY_WIDTH), f32),
        "gla_out_norm_g": gain(ks[7], (DEPTH, GLA_DV)),
        "w_branch_sb": nrm(ks[8], (DEPTH, SB_WIDTH, D_MODEL), SB_WIDTH),
        "w_branch_gla": nrm(ks[9], (DEPTH, GLA_VALUE_WIDTH, D_MODEL), GLA_VALUE_WIDTH),
        "w_out": nrm(ks[10], (DEPTH, D_MODEL, D_MODEL), D_MODEL),
        "norm2_g": gain(ks[11], (DEPTH, D_MODEL)),
        "w_ffn_gate": nrm(ks[12], (DEPTH, D_MODEL, D_FF), D_MODEL),
        "w_ffn_up": nrm(ks[13], (DEPTH, D_MODEL, D_FF), D_MODEL),
        "w_ffn_down": nrm(ks[14], (DEPTH, D_FF, D_MODEL), D_FF),
    }

def reference(x, norm1_g, w_in, sb_q_norm_g, sb_k_norm_g, gla_gate_w2, gla_gate_b,
              gla_out_norm_g, w_branch_sb, w_branch_gla, w_out, norm2_g,
              w_ffn_gate, w_ffn_up, w_ffn_down):
    b, s, _ = x.shape
    split_points = [int(v) for v in np.cumsum(IN_SIZES)[:-1]]
    for l in range(DEPTH):
        h = rms_norm(x, norm1_g[l])
        proj = h @ w_in[l]
        (sb_q, sb_k, sb_v, gla_q, gla_k, gla_v, gla_r, gla_lr,
         gate_sb, gate_gla) = jnp.split(proj, split_points, axis=-1)

        heads_sb = lambda t: jnp.transpose(t.reshape(b, s, SB_HEADS, SB_HEAD_DIM), (0, 2, 1, 3))
        q_a = heads_sb(rms_norm(sb_q.reshape(b, s, SB_HEADS, SB_HEAD_DIM), sb_q_norm_g[l]).reshape(b, s, SB_WIDTH))
        k_a = heads_sb(rms_norm(sb_k.reshape(b, s, SB_HEADS, SB_HEAD_DIM), sb_k_norm_g[l]).reshape(b, s, SB_WIDTH))
        o_sb = stick_breaking_attention(q_a, k_a, heads_sb(sb_v))

        gate_logit = (gla_lr @ gla_gate_w2[l] + gla_gate_b[l]).astype(jnp.float32)
        log_a = jax.nn.log_sigmoid(gate_logit) / GLA_GATE_TAU
        heads_k = lambda t: jnp.transpose(t.reshape(b, s, GLA_HEADS, GLA_DK), (0, 2, 1, 3))
        v_b = jnp.transpose(gla_v.reshape(b, s, GLA_HEADS, GLA_DV), (0, 2, 1, 3))
        o_b = gla_chunked(heads_k(gla_q), heads_k(gla_k), v_b, heads_k(log_a))
        o_gla = rms_norm(o_b, gla_out_norm_g[l]).reshape(b, s, GLA_VALUE_WIDTH) * jax.nn.silu(gla_r)

        merged = (jax.nn.sigmoid(gate_sb) * (o_sb @ w_branch_sb[l])
                  + jax.nn.sigmoid(gate_gla) * (o_gla @ w_branch_gla[l]))
        x = x + merged @ w_out[l]

        h2 = rms_norm(x, norm2_g[l])
        x = x + (jax.nn.silu(h2 @ w_ffn_gate[l]) * (h2 @ w_ffn_up[l])) @ w_ffn_down[l]
    return x


_drawn_inputs = setup_inputs


def setup_inputs(seed=0):
    import zlib

    import numpy as np

    out = dict(_drawn_inputs(seed))
    spreads = {}
    factors = {'norm1_g': 3.243,
     'sb_q_norm_g': 22.578,
     'sb_k_norm_g': 29.11,
     'gla_gate_b': 3.792,
     'gla_out_norm_g': 8.0,
     'norm2_g': 11.349}
    for name, (base, spread) in spreads.items():
        noise = np.random.default_rng([zlib.crc32(name.encode()), seed]).standard_normal(out[name].shape)
        drawn = base * np.exp(spread * noise) if base else spread * noise
        out[name] = __import__('jax').numpy.asarray(drawn.astype(out[name].dtype))
    for name, factor in factors.items():
        out[name] = (out[name] * factor).astype(out[name].dtype)
    return out
```

```python
from contextlib import ExitStack

import numpy as np
import concourse.bass as bass
from concourse import mybir

F32 = mybir.dt.float32
F32R = mybir.dt.float32r
I32 = mybir.dt.int32
BF16 = mybir.dt.bfloat16
ALU = mybir.AluOpType
ACT = mybir.ActivationFunctionType
AX_X = mybir.AxisListType.X
ds = bass.ds

P = 128
S = 1024
D = 1024
KT = D // P
TT = S // P
HALF = 512
NH = S // HALF
EPS = 1e-6

SB_HEADS, SB_DH = 16, 64
PAIRS = SB_HEADS * SB_DH // P
GLA_HEADS, GLA_DK, GLA_DV = 4, 128, 256
LR = 16
TAU = 16.0
FF = 2816

SBQ, SBK, SBV = 0, 1024, 2048
GLQ, GLK, GLV, GLR, GLLR = 3072, 3584, 4096, 5120, 6144
GATE = 6160


def need(eng, sem, value):
    if isinstance(value, int) and value <= 0:
        return
    eng.wait_ge(sem, value)


class Chain:

    def __init__(self, eng, sem):
        self.eng, self.sem, self.base, self.n = eng, sem, 0, 0

    def enter(self, base):
        self.base, self.n = base, 0

    def link(self, ins):
        self.n += 1
        ins.then_inc(self.sem, 1)
        self.eng.wait_ge(self.sem, self.base + self.n)


def rounds(eng, count, body):
    with eng.Fori(0, count - 1, 1) as i:
        body(i, False)
    body(count - 1, True)


class Weights:

    def __init__(self, nc, ctx, name, ring):
        self.nc, self.ring = nc, ring
        sb = lambda n, dt: ctx.enter_context(nc.sbuf_tensor(f"{name}_{n}", [P, ring, D], dt))
        sem = lambda n: ctx.enter_context(nc.semaphore(f"{name}_{n}"))
        self.ones = ctx.enter_context(nc.sbuf_tensor(f"{name}_ones", [P, 64], F32))
        self.raw, self.hi, self.lo = sb("raw", F32), sb("hi", F32R), sb("lo", F32R)
        self.loaded = [sem(f"loaded{i}") for i in range(ring)]
        self.rounded = sem("rounded")
        self.ready = sem("ready")

    def prime_pool(self, pool):
        self.nc.gpsimd.memset(self.ones[:], 1.0).then_inc(self.rounded, 1)
        pool.wait_ge(self.rounded, 1)
        pool.sem_inc(self.ready, self.ring)

    def take(self, pe, lot, step):
        pe.wait_ge(self.ready, self.ring + lot + step + 1)

    def load(self, sp, lot, step, src):
        s = step % self.ring
        need(sp, self.ready, lot + step + 1)
        dst = self.raw[:, s, :].rearrange("p (k c) -> p k c", k=src.shape[1])
        sp.dma_start(dst, src).then_inc(self.loaded[s], 16)

    def split(self, pool, lot, step, done=None):
        s = step % self.ring
        raw, hi, lo = self.raw[:, s, :], self.hi[:, s, :], self.lo[:, s, :]
        pool.wait_ge(self.loaded[s], (lot // self.ring + step // self.ring + 1) * 16)
        if done is not None:
            pool.wait_ge(*done)
        self.nc.gpsimd.tensor_tensor(hi[:, 0:64], raw[:, 0:64], self.ones[:], ALU.mult)
        self.nc.gpsimd.tensor_scalar(hi[:, 64:D], raw[:, 64:D], 1.0, 0.0, ALU.mult, ALU.add).then_inc(self.rounded, 1)
        pool.wait_ge(self.rounded, lot + step + 2)
        self.nc.gpsimd.tensor_tensor(lo, raw, hi, ALU.subtract).then_inc(self.ready, 1)

    def tile(self, step):
        s = step % self.ring
        view = lambda t: t[:, s, :].rearrange("p (k c) -> p k c", k=KT)
        return view(self.hi), view(self.lo)


def weight_cols(w, col):
    return w.rearrange("(k p) c -> p k c", p=P)[:, :, ds(col, P)]


def project_part(nc, acc, wt, xt, half, part, parts):
    (w_hi, w_lo), (x_hi, x_lo) = wt, xt
    steps = [(a, b, k) for a, b in ((w_hi, x_hi), (w_hi, x_lo), (w_lo, x_hi)) for k in range(KT)]
    per = len(steps) // parts
    ins = None
    for n in range(part * per, (part + 1) * per):
        a, b, k = steps[n]
        ins = nc.tensor.matmul(acc, a[:, k, :], b[:, k, half * HALF:(half + 1) * HALF],
                               start=(n == 0), stop=(n == len(steps) - 1))
    return ins




def constants(nc, ctx):
    sb = lambda n, shape, dt: ctx.enter_context(nc.sbuf_tensor(n, shape, dt))
    c = {
        "ident": sb("ident", [P, P], F32), "ident_b": sb("ident_b", [P, P], BF16),
        "not_before": sb("not_before", [P, P], BF16), "head_mean": sb("head_mean", [P, P], F32),
    }
    made = ctx.enter_context(nc.semaphore("const_made"))
    with nc.Block() as block:
        @block.gpsimd
        def _(pool):
            chain = Chain(pool, made)
            for name in ("ident", "ident_b", "not_before", "head_mean"):
                chain.link(nc.gpsimd.memset(c[name][:], 0.0))
            for r in range(0, P, SB_DH):
                chain.link(nc.gpsimd.memset(c["head_mean"][r:r + SB_DH, r:r + SB_DH], 1.0 / SB_DH))
            for name in ("ident", "ident_b"):
                chain.link(nc.gpsimd.affine_select(out=c[name][:], in_=c[name][:], compare_op=ALU.not_equal,
                                                   fill=1.0, base=0, pattern=[[-1, P]], channel_multiplier=1))
            chain.link(nc.gpsimd.affine_select(out=c["not_before"][:], in_=c["not_before"][:],
                                               compare_op=ALU.is_gt, fill=-1e30, base=0, pattern=[[-1, P]],
                                               channel_multiplier=1))
    return c


def rsqrt(nc, chain, ms, y, u):
    chain.link(nc.vector.tensor_scalar(y.bitcast(I32), ms.bitcast(I32), -0.5, 1597463007.0, ALU.mult, ALU.add))
    for _ in range(3):
        chain.link(nc.vector.tensor_tensor(u, y, y, ALU.mult))
        chain.link(nc.vector.tensor_tensor(u, u, ms, ALU.mult))
        chain.link(nc.vector.tensor_scalar(u, u, -0.5, 1.5, ALU.mult, ALU.add))
        chain.link(nc.vector.tensor_tensor(y, y, u, ALU.mult))


def norm_transposed(nc, c, name, src, x, gain, hT):
    h_hi, h_lo = hT
    with ExitStack() as ctx:
        sb = lambda n, shape, dt: ctx.enter_context(nc.sbuf_tensor(f"{name}_{n}", shape, dt))
        sem = lambda n: ctx.enter_context(nc.semaphore(f"{name}_{n}"))
        g_all = sb("g_all", [P, D], F32)
        h = sb("h", [P, 2, D], F32)
        junk = sb("junk", [P, D], F32)
        ssq = sb("ssq", [P, TT], F32)
        work = sb("work", [P, 3, TT], F32)
        bank = [ctx.enter_context(nc.psum_tensor(f"{name}_t{i}", [P, 4, P], F32)) for i in range(4)]
        x_loaded = [sem(f"x_loaded{i}") for i in range(TT)]
        g_loaded = sem("g_loaded")
        ssq_ready = sem("ssq_ready")
        dve_step = sem("dve_step")
        h_ready = sem("h_ready")
        t_done = sem("t_done")
        hi_done = sem("hi_done")
        lo_done = sem("lo_done")
        with nc.Block() as block:
            @block.sync
            def _(sp):
                sp.dma_start(g_all[:], gain[0].partition_broadcast(P)).then_inc(g_loaded, 16)
                if src is not None:
                    for i in range(TT):
                        sp.dma_start(x[:, i, :], src[i * P:(i + 1) * P, :]).then_inc(x_loaded[i], 16)

            @block.scalar
            def _(act):
                for i in range(TT):
                    if src is not None:
                        act.wait_ge(x_loaded[i], 16)
                    if i:
                        act.wait_ge(ssq_ready, i)
                    nc.scalar.activation(junk[:], x[:, i, :], ACT.Square,
                                         accum_out=ssq[:, i:i + 1]).then_inc(ssq_ready, 1)
                with act.Fori(0, TT // 2, 1) as i:
                    for u in range(4):
                        act.wait_ge(t_done, 4 * i + u + 1)
                        nc.scalar.copy(h_hi[:, 4 * (u % 2):4 * (u % 2) + 4, ds(i * 2 * P + (u // 2) * P, P)],
                                       bank[u][:]).then_inc(hi_done, 1)

            @block.vector
            def _(dve):
                chain = Chain(dve, dve_step)
                dve.sem_inc(lo_done, 4)
                dve.wait_ge(ssq_ready, TT)
                chain.link(nc.vector.tensor_scalar(work[:, 0, :], ssq[:], 1.0 / D, EPS, ALU.mult, ALU.add))
                rsqrt(nc, chain, work[:, 0, :], work[:, 1, :], work[:, 2, :])
                dve.wait_ge(g_loaded, 16)
                rstd = work[:, 1, :]

                def normalise(i, b):
                    nc.vector.scalar_tensor_tensor(h[:, b, :], x[:, ds(2 * i + b, 1), :].rearrange("p a d -> p (a d)"),
                                                   rstd[:, ds(2 * i + b, 1)], g_all[:],
                                                   ALU.mult, ALU.mult).then_inc(h_ready, 1)

                normalise(0, 0)
                normalise(0, 1)

                def lows(i, b):
                    for u in (2 * b, 2 * b + 1):
                        dve.wait_ge(hi_done, 4 * i + u + 1)
                        at = (slice(None), slice(4 * (u % 2), 4 * (u % 2) + 4), ds(i * 2 * P + (u // 2) * P, P))
                        nc.vector.tensor_tensor(h_lo[at], bank[u][:], h_hi[at], ALU.subtract).then_inc(lo_done, 1)

                def body(i, last):
                    for b in range(2):
                        lows(i, b)
                        if not last:
                            normalise(i + 1, b)
                rounds(dve, TT // 2, body)

            @block.tensor
            def _(pe):
                with pe.Fori(0, TT // 2, 1) as i:
                    for u in range(4):
                        b, half = u // 2, u % 2
                        if half == 0:
                            pe.wait_ge(h_ready, 2 * i + b + 1)
                        pe.wait_ge(lo_done, 4 * i + u + 1)
                        for q in range(4):
                            k = 4 * half + q
                            ins = nc.tensor.transpose(bank[u][:, q, :], h[:, b, k * P:(k + 1) * P], c["ident"][:])
                        ins.then_inc(t_done, 1)


SLOTS = 32
SCORE_SLOT = [0, 1, 2, 3, 4, 5, 6, 8, 10, 12, 14, 15, 16, 17, 18, 20]
SCORE_STEPS = [(hh, tb) for hh in range(2) for tb in range(TT)]
WEIGHT_STEPS = [(hh, g, j) for hh in range(2) for g in range(NH) for j in range(4 * g + 4)]
WEIGHT_SLOT = 7
NSC, NWT = len(SCORE_STEPS), len(WEIGHT_STEPS)
STACKS = 12
SB_CHAIN = 12


def stick_breaking(nc, c, hT, w_in, qk_gains, osb_t, gates_t):
    with ExitStack() as ctx:
        sb = lambda n, shape, dt: ctx.enter_context(nc.sbuf_tensor(f"sb_{n}", shape, dt))
        ps = lambda n, shape: ctx.enter_context(nc.psum_tensor(f"sb_{n}", shape, F32))
        sem = lambda n: ctx.enter_context(nc.semaphore(f"sb_{n}"))
        W = Weights(nc, ctx, "sbw", 2)
        qs = [sb(f"qs{e}", [P, S], F32R) for e in range(2)]
        kh = [sb(f"kh{e}", [P, S], F32R) for e in range(2)]
        kl = [sb(f"kl{e}", [P, S], F32R) for e in range(2)]
        qk = sb("qk", [P, 2, S], F32)
        ms = sb("ms", [P, 2, S], F32)
        rs = sb("rs", [P, 2, S], F32)
        sq = sb("sq", [P, NH, HALF], F32)
        gv = sb("gv", [P, 2], F32)
        vt = sb("vt", [P, S], F32)
        v_hi = sb("v_hi", [P, TT, P], F32R)
        v_lo = sb("v_lo", [P, TT, P], F32R)
        rest = sb("rest", [P, 2, S + 1], F32)
        beta = sb("beta", [P, 2, S], F32)
        rows = [sb(f"rows{g}", [P, 4, HALF * (g + 1)], F32) for g in range(NH)]
        wt_hi = sb("wt_hi", [P, 2, HALF], F32R)
        wt_lo = sb("wt_lo", [P, 2, HALF], F32R)
        ot = sb("ot", [P, S], F32)
        gst = sb("gst", [P, HALF], F32)
        G = [ps(f"g{h}", [P, HALF]) for h in range(NH)]
        Z = [ps(f"z{b}", [P, S]) for b in range(2)]
        T = ps("t", [P, HALF])
        O = ps("o", [P, HALF])

        g_loaded, gv_made = sem("g_loaded"), sem("gv_made")
        g_done = [sem(f"g_done{h}") for h in range(NH)]
        g_free = [sem(f"g_free{h}") for h in range(NH)]
        sq_ready = sem("sq_ready")
        rs_log, rs_ready = sem("rs_log"), sem("rs_ready")
        stacked = sem("stacked")
        z_done = sem("z_done")
        z_free = sem("z_free")
        row_ready = sem("row_ready")
        scanned = sem("scanned")
        t_done = sem("t_done")
        hi_ready = sem("hi_ready")
        lo_ready = sem("lo_ready")
        av_done = sem("av_done")
        o_free = sem("o_free")
        ot_out = sem("ot_out")
        gs_out = sem("gs_out")
        dve_step = sem("dve_step")

        units = lambda it: 4 * it
        g_uses = lambda it: 5 + 6 * it
        t_uses = lambda it: 2 + (NWT + 2) * it
        LAST_GATES = 3

        def slot_of_unit(s):
            return s // 8, s % 8

        with nc.Block() as block:
            @block.sync
            def _(sp):
                for half in range(2):
                    for x in range(2):
                        sp.dma_start(gv[half * SB_DH:(half + 1) * SB_DH, x:x + 1],
                                     qk_gains[x].rearrange("a d -> d a")).then_inc(g_loaded, 16)

                def stacks(it):
                    sp.wait_ge(dve_step, SB_CHAIN * (it + 2))
                    need(sp, z_done, NSC * (it + 1))
                    for e in range(2):
                        rows_e = slice(e * SB_DH, (e + 1) * SB_DH)
                        for top in range(2):
                            to = slice(top * SB_DH, (top + 1) * SB_DH)
                            for dst, src, x in ((qs[e], (ms, rs)[top], 0), (kh[e], ms, 1), (kl[e], rs, 1)):
                                sp.dma_start(dst[to, :].bitcast(F32), src[rows_e, x, :]).then_inc(stacked, 16)

                for step, col in enumerate((SBQ, SBK, SBV)):
                    W.load(sp, 0, step, weight_cols(w_in, col))
                stacks(-1)
                W.load(sp, 0, 3, weight_cols(w_in, SBQ + P))
                W.load(sp, 0, 4, weight_cols(w_in, SBK + P))

                def body(it, last):
                    if last:
                        W.load(sp, units(it), 5, weight_cols(w_in, GATE + (PAIRS - 1 + 2) * P))
                        sp.wait_ge(ot_out, 16 * PAIRS)
                        return
                    W.load(sp, units(it), 5, weight_cols(w_in, it * P + (SBV + P)))
                    W.load(sp, units(it), 6, weight_cols(w_in, it * P + GATE))
                    stacks(it)

                def next_pair(it):
                    W.load(sp, units(it + 1), 3, weight_cols(w_in, it * P + (SBQ + 2 * P)))
                    W.load(sp, units(it + 1), 4, weight_cols(w_in, it * P + (SBK + 2 * P)))

                with sp.Fori(0, PAIRS - 2, 1) as it:
                    body(it, False)
                    next_pair(it)
                body(PAIRS - 2, False)
                for n in range(2):
                    W.load(sp, units(PAIRS - 1), 3 + n, weight_cols(w_in, GATE + (PAIRS - 1 + n) * P))
                body(PAIRS - 1, True)
                sp.wait_ge(gs_out, 16 * NH * (PAIRS - 1 + LAST_GATES))

            @block.gpsimd
            def _(pool):
                W.prime_pool(pool)
                W.split(pool, 0, 0)
                W.split(pool, 0, 1)
                W.split(pool, 0, 2, (g_done[1], 1))

                def body(it, last):
                    for step, uses in zip(range(3, 6 if last else 7), (-1, 0, 1, 3)):
                        W.split(pool, units(it), step, (g_done[1], g_uses(it) + uses))
                rounds(pool, PAIRS, body)

            @block.tensor
            def _(pe):
                pe.sem_inc(av_done, 2)

                def fill(it_units, step, eighth, use):
                    half, part = eighth // 4, eighth % 4
                    if eighth == 0:
                        W.take(pe, it_units, step)
                    if part == 0:
                        pe.wait_ge(g_free[half], use + 1)
                    ins = project_part(nc, G[half][:], W.tile(step), hT, half, part, 4)
                    if part == 3:
                        ins.then_inc(g_done[half], 1)

                def mean_squares(prep, x, half, use):
                    pe.wait_ge(sq_ready, 4 * prep + 2 * x + half + 1)
                    pe.wait_ge(g_free[half], use + 1)
                    nc.tensor.matmul(G[half][:], c["head_mean"][:], sq[:, half, :],
                                     start=True, stop=True).then_inc(g_done[half], 1)

                def transpose_v(part, use, copied):
                    pe.wait_ge(g_free[part], copied)
                    need(pe, lo_ready, use)
                    for q in range(4):
                        j = 4 * part + q
                        ins = nc.tensor.transpose(T[:, q * P:(q + 1) * P], vt[:, j * P:(j + 1) * P], c["ident"][:])
                    ins.then_inc(t_done, 1)

                for step in range(3):
                    for eighth in range(8):
                        fill(0, step, eighth, (0, 2, 4)[step])
                    if step < 2:
                        for half in range(NH):
                            mean_squares(0, step, half, 2 * step + 1)
                for part in range(2):
                    transpose_v(part, part, 6)

                def scores(it, n):
                    e, tb = SCORE_STEPS[n]
                    if n == 0:
                        pe.wait_ge(stacked, 16 * STACKS * (it + 1))
                    pe.wait_ge(z_free, NSC * it + n + 1)
                    z, width = Z[n % 2], (tb + 1) * P
                    q = qs[e][:, tb * P:(tb + 1) * P]
                    for a in range(0, width, HALF):
                        b = min(a + HALF, width)
                        nc.tensor.matmul(z[:, a:b], q, kh[e][:, a:b], start=True, stop=False)
                        ins = nc.tensor.matmul(z[:, a:b], q, kl[e][:, a:b], start=False, stop=(b < width))
                    nc.tensor.matmul(z[:, width - P:width], c["ident_b"][:], c["not_before"][:],
                                     start=False, stop=True).then_inc(z_done, 1)

                def transposes(it, m):
                    e, g, j = WEIGHT_STEPS[m]
                    first = max(j, 4 * g)
                    if j == 0:
                        pe.wait_ge(row_ready, 2 + NSC * it + 8 * e + 4 * g + 4)
                    pe.wait_ge(lo_ready, t_uses(it) + m)
                    for tb in range(first, 4 * g + 4):
                        ins = nc.tensor.transpose(T[:, (tb - 4 * g) * P:(tb - 4 * g + 1) * P],
                                                  rows[g][:, tb - 4 * g, j * P:(j + 1) * P], c["ident"][:])
                    ins.then_inc(t_done, 1)

                def weigh(it, m):
                    e, g, j = WEIGHT_STEPS[m]
                    a = max(j - 4 * g, 0) * P
                    if j == 0:
                        pe.wait_ge(o_free, 4 * it + 2 * e + g + 1)
                    pe.wait_ge(lo_ready, t_uses(it) + m + 1)
                    v = slice(e * SB_DH, (e + 1) * SB_DH)
                    o, hi, lo = O[0:SB_DH, a:HALF], wt_hi[:, m % 2, a:HALF], wt_lo[:, m % 2, a:HALF]
                    last = j == 4 * g + 3
                    nc.tensor.matmul(o, v_hi[:, j, v], hi, start=(j == 0), stop=False)
                    nc.tensor.matmul(o, v_lo[:, j, v], hi, start=False, stop=False)
                    nc.tensor.matmul(o, v_hi[:, j, v], lo, start=False, stop=last).then_inc(av_done, 1)

                def body(it, last):
                    fills = LAST_GATES if last else 4
                    for s in range(SLOTS):
                        m = s - WEIGHT_SLOT
                        if 0 <= m < NWT:
                            transposes(it, m)
                        if s in SCORE_SLOT:
                            scores(it, SCORE_SLOT.index(s))
                        u, eighth = slot_of_unit(s)
                        if u < fills:
                            fill(units(it), 3 + u, eighth, g_uses(it) + (u if last else (0, 2, 4, 5)[u]))
                        if not last and s in (6, 10, 14, 18):
                            i = (6, 10, 14, 18).index(s)
                            mean_squares(it + 1, i // 2, i % 2, g_uses(it) + 2 * (i // 2) + 1)
                        if 0 <= m - 1 < NWT:
                            weigh(it, m - 1)
                    if not last:
                        for part in range(2):
                            transpose_v(part, t_uses(it) + NWT + part, g_uses(it) + 6)
                rounds(pe, PAIRS, body)

            @block.scalar
            def _(act):
                for sem_ in (z_free, z_free, o_free):
                    act.sem_inc(sem_, 1)

                def square(x, half, use):
                    act.wait_ge(g_free[half], use + 2)
                    nc.scalar.activation(sq[:, half, :], qk[:, x, half * HALF:(half + 1) * HALF],
                                         ACT.Square).then_inc(sq_ready, 1)

                def first_rs(prep, uses):
                    for half in range(NH):
                        act.wait_ge(g_free[half], 1 + uses)
                    need(act, stacked, 16 * STACKS * prep)
                    for x in range(2):
                        nc.scalar.activation(rs[:, x, :], ms[:, x, :], ACT.Ln).then_inc(rs_log, 1)
                    for x in range(2):
                        act.wait_ge(rs_log, 2 * prep + x + 1)
                        nc.scalar.activation(rs[:, x, :], rs[:, x, :], ACT.Exp, scale=-0.5).then_inc(rs_ready, 1)

                def copy_vt(half, use):
                    act.wait_ge(g_done[half], use + 1)
                    nc.scalar.copy(vt[:, half * HALF:(half + 1) * HALF], G[half][:]).then_inc(g_free[half], 1)

                def v_high(part, use):
                    act.wait_ge(t_done, use + 1)
                    nc.scalar.copy(v_hi[:, 4 * part:4 * part + 4, :], T[:].rearrange("p (j n) -> p j n", j=4)
                                   ).then_inc(hi_ready, 1)

                def gate(n_done, half, use, row):
                    act.wait_ge(g_done[half], use + 1)
                    need(act, gs_out, 16 * (NH * n_done + half))
                    nc.scalar.activation(gst[:], G[half][:], ACT.Sigmoid).then_inc(g_free[half], 1)
                    act.wait_ge(g_free[half], use + 2)
                    act.dma_start(gates_t[ds(row, P), half * HALF:(half + 1) * HALF],
                                  gst[:]).then_inc(gs_out, 16)

                for x in range(2):
                    for half in range(NH):
                        square(x, half, 2 * x)
                for half in range(NH):
                    copy_vt(half, 4)
                first_rs(0, 4)
                for part in range(2):
                    v_high(part, part)

                def sigmoids(it, n):
                    e, tb = SCORE_STEPS[n]
                    act.wait_ge(z_done, NSC * it + n + 1)
                    act.wait_ge(row_ready, NSC * it + n + 1)
                    width = (tb + 1) * P
                    nc.scalar.activation(rest[:, n % 2, 0:width], Z[n % 2][:, 0:width], ACT.Sigmoid,
                                         scale=-(SB_DH ** -0.5))
                    nc.scalar.activation(beta[:, n % 2, 0:width], Z[n % 2][:, 0:width], ACT.Sigmoid,
                                         scale=SB_DH ** -0.5).then_inc(z_free, 1)

                def wt_high(it, m):
                    e, g, j = WEIGHT_STEPS[m]
                    a = max(j - 4 * g, 0) * P
                    act.wait_ge(t_done, t_uses(it) + m + 1)
                    act.wait_ge(av_done, NWT * it + m + 1)
                    nc.scalar.copy(wt_hi[:, m % 2, a:HALF], T[:, a:HALF]).then_inc(hi_ready, 1)

                def copy_o(it, e, g):
                    m = WEIGHT_STEPS.index((e, g, 4 * g + 3))
                    act.wait_ge(av_done, 2 + NWT * it + m + 1)
                    if e == 0 and g == 0:
                        act.wait_ge(ot_out, 16 * it)
                    nc.scalar.copy(ot[e * SB_DH:(e + 1) * SB_DH, g * HALF:(g + 1) * HALF],
                                   O[0:SB_DH, :]).then_inc(o_free, 1)

                def body(it, last):
                    for s in range(SLOTS):
                        m = s - WEIGHT_SLOT
                        if 0 <= m < NWT:
                            wt_high(it, m)
                        if s in SCORE_SLOT:
                            sigmoids(it, SCORE_SLOT.index(s))
                        if not last:
                            if s in (5, 9, 13, 17):
                                i = (5, 9, 13, 17).index(s)
                                square(i // 2, i % 2, g_uses(it) + 2 * (i // 2))
                            if s in (20, 24):
                                copy_vt((s - 20) // 4, g_uses(it) + 4)
                            if s == 21:
                                first_rs(it + 1, g_uses(it) + 4)
                            if s == 28:
                                gate(it, 0, g_uses(it) + 5, it * P)
                        elif s in (4, 8, 12, 16, 20, 24):
                            i = (s - 4) // 4
                            gate(PAIRS - 1 + i // 2, i % 2, g_uses(it) + i // 2, (PAIRS - 1 + i // 2) * P)
                        if 0 <= m - 1 < NWT and WEIGHT_STEPS[m - 1][2] == 4 * WEIGHT_STEPS[m - 1][1] + 3:
                            copy_o(it, *WEIGHT_STEPS[m - 1][:2])
                    act.wait_ge(o_free, 4 * it + 5)
                    act.dma_start(osb_t[ds(it * P, P), :], ot[:]).then_inc(ot_out, 16)
                    if not last:
                        gate(it, 1, g_uses(it) + 5, it * P)
                        for part in range(2):
                            v_high(part, t_uses(it) + NWT + part)
                rounds(act, PAIRS, body)

            @block.vector
            def _(dve):
                chain = Chain(dve, dve_step)
                for sem_ in (g_free[0], g_free[1], row_ready, row_ready):
                    dve.sem_inc(sem_, 1)
                nc.vector.memset(rest[:], 1.0)
                dve.wait_ge(g_loaded, 64)
                nc.vector.tensor_scalar(gv[:], gv[:], -0.5, None, ALU.mult).then_inc(gv_made, 1)
                dve.wait_ge(gv_made, 1)

                def copy_raw(x, half, use):
                    dve.wait_ge(g_done[half], use + 1)
                    nc.vector.tensor_copy(qk[:, x, half * HALF:(half + 1) * HALF], G[half][:]
                                          ).then_inc(g_free[half], 1)

                def copy_ms(prep, x, half, use):
                    dve.wait_ge(g_done[half], use + 1)
                    if x == 0 and half == 0:
                        need(dve, stacked, 16 * STACKS * prep)
                    nc.vector.tensor_scalar(ms[:, x, half * HALF:(half + 1) * HALF], G[half][:], EPS, None,
                                            ALU.add).then_inc(g_free[half], 1)

                def normalise(prep, x):
                    u = sq[:].rearrange("p a b -> p (a b)")
                    m, r, q = ms[:, x, :], rs[:, x, :], qk[:, x, :]
                    if x == 0:
                        chain.enter(SB_CHAIN * prep)
                    dve.wait_ge(rs_ready, 2 * prep + x + 1)
                    chain.link(nc.vector.tensor_tensor(u, r, r, ALU.mult))
                    chain.link(nc.vector.tensor_tensor(u, u, m, ALU.mult))
                    chain.link(nc.vector.scalar_tensor_tensor(u, u, 3.0, r, ALU.subtract, ALU.mult))
                    chain.link(nc.vector.scalar_tensor_tensor(q, q, gv[:, x:x + 1], u, ALU.mult, ALU.mult))
                    chain.link(nc.vector.tensor_copy(m.bitcast(F32R), q))
                    chain.link(nc.vector.tensor_tensor(r.bitcast(F32R), q, m, ALU.subtract))
                    assert x == 0 or chain.n == SB_CHAIN

                def v_low(part, use):
                    dve.wait_ge(hi_ready, use + 1)
                    at = v_lo[:, 4 * part:4 * part + 4, :], v_hi[:, 4 * part:4 * part + 4, :]
                    nc.vector.tensor_tensor(at[0], T[:].rearrange("p (j n) -> p j n", j=4), at[1],
                                            ALU.subtract).then_inc(lo_ready, 1)

                for x in range(2):
                    for half in range(NH):
                        copy_raw(x, half, 2 * x)
                    for half in range(NH):
                        copy_ms(0, x, half, 2 * x + 1)
                normalise(0, 0)
                normalise(0, 1)
                for part in range(2):
                    v_low(part, part)

                def row(it, n):
                    e, tb = SCORE_STEPS[n]
                    g, width, b = tb // 4, (tb + 1) * P, n % 2
                    dve.wait_ge(z_free, 2 + NSC * it + n + 1)
                    back = rest[:, b, width - 1::-1] if width == S + 1 else rest[:, b, 0:width][:, ::-1]
                    nc.vector.tensor_tensor_scan(back, back, back, 1.0, ALU.mult, ALU.bypass).then_inc(scanned, 1)
                    dve.wait_ge(scanned, NSC * it + n + 1)
                    nc.vector.tensor_tensor(rows[g][:, tb - 4 * g, 0:width], beta[:, b, 0:width],
                                            rest[:, b, 1:width + 1], ALU.mult).then_inc(row_ready, 1)

                def wt_low(it, m):
                    e, g, j = WEIGHT_STEPS[m]
                    a = max(j - 4 * g, 0) * P
                    dve.wait_ge(hi_ready, t_uses(it) + m + 1)
                    nc.vector.tensor_tensor(wt_lo[:, m % 2, a:HALF], T[:, a:HALF], wt_hi[:, m % 2, a:HALF],
                                            ALU.subtract).then_inc(lo_ready, 1)

                def body(it, last):
                    for s in range(SLOTS):
                        m = s - WEIGHT_SLOT
                        if 0 <= m < NWT:
                            wt_low(it, m)
                        if s - 1 in SCORE_SLOT:
                            row(it, SCORE_SLOT.index(s - 1))
                        if not last:
                            if s in (4, 8, 12, 16):
                                i = (s - 4) // 4
                                copy_raw(i // 2, i % 2, g_uses(it) + 2 * (i // 2))
                            if s in (7, 11, 15, 19):
                                i = (s - 7) // 4
                                copy_ms(it + 1, i // 2, i % 2, g_uses(it) + 2 * (i // 2) + 1)
                            if s in (23, 25):
                                normalise(it + 1, (s - 23) // 2)
                    if not last:
                        for part in range(2):
                            v_low(part, t_uses(it) + NWT + part)
                rounds(dve, PAIRS, body)


GLA_SLOTS = 48
CHUNKS = S // P
LEVELS = 8
GLA_UNITS = 6
GLA_TASKS = 9
GLA_T = CHUNKS + 8
GLA_CHAIN = 15
N_MADE = 3 + 3 * (LEVELS - 1) + 1


def linear_attention(nc, c, hT, w_in, w2, gate_b, out_gain, ogla_t, gates_t):
    with ExitStack() as ctx:
        sb = lambda n, shape, dt=F32: ctx.enter_context(nc.sbuf_tensor(f"gla_{n}", shape, dt))
        ps = lambda n, shape: ctx.enter_context(nc.psum_tensor(f"gla_{n}", shape, F32))
        sem = lambda n: ctx.enter_context(nc.semaphore(f"gla_{n}"))
        W = Weights(nc, ctx, "glaw", 2)
        lr_raw, lr_hi, lr_lo = sb("lr_raw", [P, KT, LR]), sb("lr_hi", [P, KT, LR], F32R), sb("lr_lo", [P, KT, LR], F32R)
        lr_t = sb("lr_t", [LR, S])
        w2_all, w2_h = sb("w2_all", [LR, GLA_HEADS * GLA_DK]), sb("w2_h", [LR, GLA_DK])
        gb_all, gb_h = sb("gb_all", [P, GLA_HEADS]), sb("gb_h", [P, 1])
        og = sb("og", [P, 2])
        mask = sb("mask", [P, LEVELS, P])
        keep = sb("keep", [P, S], BF16)
        q_new, k_new = sb("q_new", [P, S]), sb("k_new", [P, S])
        q_diag, k_diag = sb("q_diag", [P, S]), sb("k_diag", [P, S])
        X = sb("x", [P, LEVELS - 1, S])
        q_in, k_out = sb("q_in", [P, S]), sb("k_out", [P, S])
        C = sb("c", [P, S])
        E = sb("e", [P, 2, S])
        dec = sb("dec", [P, CHUNKS])
        vt = sb("vt", [P, 2, S])
        V = sb("v", [P, CHUNKS, GLA_DV])
        RT = sb("rt", [P, 2, S])
        masked = E[:, 0, :].rearrange("p (l i) -> p l i", l=LEVELS)
        sc = sb("sc", [P, 2, P])
        kt = sb("kt", [P, 2, P])
        state = sb("state", [P, GLA_DV])
        obuf = sb("obuf", [P, CHUNKS, GLA_DV])
        junk = E[:, 1, 0:GLA_DV]
        ssq, stat = sb("ssq", [P, CHUNKS]), sb("stat", [P, 3, CHUNKS])
        gst = sb("gst", [P, HALF])
        G = [ps(f"g{h}", [P, HALF]) for h in range(NH)]
        SC = ps("s", [P, LEVELS, P])
        O = [ps(f"o{b}", [P, HALF]) for b in range(2)]
        ST = ps("st", [P, HALF])
        T = ps("t", [P, HALF])

        small_loaded = sem("small_loaded")
        made = sem("made")
        lr_split = sem("lr_split")
        g_done = [sem(f"g_done{h}") for h in range(NH)]
        g_free = [sem(f"g_free{h}") for h in range(NH)]
        r_sig = sem("r_sig")
        w2_ready = sem("w2_ready")
        s_done, s_free = sem("s_done"), sem("s_free")
        abs_ready, log_ready = sem("abs_ready"), sem("log_ready")
        d_ready, e_ready = sem("d_ready"), sem("e_ready")
        f_ready = sem("f_ready")
        sc_ready = sem("sc_ready")
        t_done, t_free = sem("t_done"), sem("t_free")
        o_done, o_free = sem("o_done"), sem("o_free")
        ssq_ready = sem("ssq_ready")
        st_done, st_free = sem("st_done"), sem("st_free")
        on_ready = sem("on_ready")
        gst_out = sem("gst_out")
        gate_out = [sem(f"gate_out{h}") for h in range(NH)]
        dve_step = sem("dve_step")

        g_uses = lambda it: 7 + GLA_UNITS * it
        t_uses = lambda it: 4 + GLA_T * it
        s_uses = lambda it: 1 + (CHUNKS + 1) * it
        N_LAST_GATES = 6

        def blocks(t, half):
            return t.rearrange("p (b a h) -> p b a h", a=2, h=half)

        with nc.Block() as block:
            @block.sync
            def _(sp):
                sp.dma_start(lr_raw[:], w_in.rearrange("(k p) c -> p k c", p=P)[:, :, GLLR:GLLR + LR]
                             ).then_inc(small_loaded, 16)
                sp.dma_start(w2_all[:], w2).then_inc(small_loaded, 16)
                for dst, src in ((gb_all, gate_b), (og, out_gain)):
                    for n in range(dst.shape[1]):
                        sp.dma_start(dst[:, n:n + 1], src[:, n * P:(n + 1) * P].rearrange("a p -> p a")
                                     ).then_inc(small_loaded, 16)

                cols = [(GLQ, GLA_DK), (GLK, GLA_DK), (GLV, GLA_DV), (GLV + P, GLA_DV), (GLR, GLA_DV), (GLR + P, GLA_DV)]
                for n, (col, _) in enumerate(cols):
                    W.load(sp, 0, n, weight_cols(w_in, col))

                def body(it, last):
                    for n, (col, width) in enumerate(cols):
                        src = GATE + (10 + n) * P if last else it * width + (col + width)
                        W.load(sp, GLA_UNITS * it, GLA_UNITS + n, weight_cols(w_in, src))
                rounds(sp, GLA_HEADS, body)
                sp.wait_ge(gst_out, 16 * 4 * GLA_HEADS)
                for half in range(NH):
                    sp.wait_ge(gate_out[half], 16 * N_LAST_GATES)

            @block.gpsimd
            def _(pool):
                W.prime_pool(pool)
                W.split(pool, 0, 0)
                W.split(pool, 0, 1)
                chain = Chain(pool, made)
                chain.link(nc.gpsimd.memset(mask[:], 0.0))
                chain.link(nc.gpsimd.memset(keep[:], 1.0))
                chain.link(nc.gpsimd.memset(keep[:].rearrange("p (c t) -> p c t", t=P)[:, :, 0:1], 0.0))
                for lv in range(LEVELS - 1):
                    half = 1 << lv
                    second = blocks(mask[:, lv, :], half)[:, :, 1, :]
                    chain.link(nc.gpsimd.memset(second, 1.0))
                    pattern = lambda sign: [[sign * 2 * half, P // (2 * half)], [0, half]]
                    chain.link(nc.gpsimd.affine_select(out=second, in_=second, compare_op=ALU.is_ge, fill=0.0,
                                                       base=0, pattern=pattern(-1), channel_multiplier=1))
                    chain.link(nc.gpsimd.affine_select(out=second, in_=second, compare_op=ALU.is_ge, fill=0.0,
                                                       base=half - 1, pattern=pattern(1), channel_multiplier=-1))
                diag = mask[:, LEVELS - 1, :]
                chain.link(nc.gpsimd.affine_select(out=diag, in_=diag, compare_op=ALU.not_equal, fill=1.0,
                                                   base=0, pattern=[[-1, P]], channel_multiplier=1))
                assert chain.n == N_MADE
                for n in range(2, GLA_UNITS):
                    W.split(pool, 0, n, (g_done[1], n))

                def body(it, last):
                    for n in range(GLA_UNITS):
                        W.split(pool, GLA_UNITS * it, GLA_UNITS + n, (g_done[1], GLA_UNITS * it + (GLA_UNITS + n)))
                rounds(pool, GLA_HEADS, body)

            @block.tensor
            def _(pe):
                def fill(lot, step, eighth, use):
                    half, part = eighth // 4, eighth % 4
                    if eighth == 0:
                        W.take(pe, lot, step)
                    if part == 0:
                        pe.wait_ge(g_free[half], use + 1)
                    ins = project_part(nc, G[half][:], W.tile(step), hT, half, part, 4)
                    if part == 3:
                        ins.then_inc(g_done[half], 1)

                def transpose_v(n, use):
                    d, cg = n // 2, n % 2
                    pe.wait_ge(t_free, use)
                    for q in range(4):
                        j = 4 * cg + q
                        ins = nc.tensor.transpose(T[:, q * P:(q + 1) * P], vt[:, d, j * P:(j + 1) * P], c["ident"][:])
                    ins.then_inc(t_done, 1)

                def logits(prep, use):
                    pe.wait_ge(w2_ready, prep + 1)
                    pe.wait_ge(s_free, use + 1)
                    flat = SC[:].rearrange("p l i -> p (l i)")
                    for half in range(NH):
                        at = slice(half * HALF, (half + 1) * HALF)
                        ins = nc.tensor.matmul(flat[:, at], w2_h[:], lr_t[:, at], start=True, stop=True)
                    ins.then_inc(s_done, 1)

                pe.wait_ge(lr_split, 2)
                for half in range(NH):
                    pe.wait_ge(g_free[half], 1)
                    steps = [(a, b, k) for a, b in ((lr_hi, hT[0]), (lr_hi, hT[1]), (lr_lo, hT[0])) for k in range(KT)]
                    for n, (a, b, k) in enumerate(steps):
                        ins = nc.tensor.matmul(G[half][0:LR, :], a[:, k, :], b[:, k, half * HALF:(half + 1) * HALF],
                                               start=(n == 0), stop=(n == len(steps) - 1))
                    ins.then_inc(g_done[half], 1)
                for n in range(GLA_UNITS):
                    for eighth in range(8):
                        fill(0, n, eighth, 1 + n)
                    if n == 1:
                        for half in range(NH):
                            pe.wait_ge(g_free[half], 2)
                        logits(0, 0)
                    if n == 4:
                        for half in range(NH):
                            pe.wait_ge(g_free[half], 6)
                        for m in range(4):
                            if m:
                                transpose_v(m, m)
                            else:
                                for q in range(4):
                                    ins = nc.tensor.transpose(T[:, q * P:(q + 1) * P], vt[:, 0, q * P:(q + 1) * P],
                                                              c["ident"][:])
                                ins.then_inc(t_done, 1)

                def scores(it, ch):
                    if ch == 0:
                        pe.wait_ge(f_ready, GLA_TASKS * (it + 1))
                    at = slice(ch * P, (ch + 1) * P)
                    pe.wait_ge(t_free, t_uses(it) + ch)
                    nc.tensor.transpose(T[:, 0:P], k_out[:, at], c["ident"][:]).then_inc(t_done, 1)
                    pe.wait_ge(s_free, s_uses(it) + ch + 1)
                    for lv in range(LEVELS - 1):
                        nc.tensor.matmul(SC[:, lv, :], X[:, lv, at], X[:, lv, at], start=True, stop=True)
                    nc.tensor.matmul(SC[:, LEVELS - 1, :], k_diag[:, at], q_diag[:, at],
                                     start=True, stop=True).then_inc(s_done, 1)

                def outputs(it, ch):
                    at, o = slice(ch * P, (ch + 1) * P), O[ch % 2][:, 0:GLA_DV]
                    pe.wait_ge(o_free, CHUNKS * it + ch + 1)
                    if ch:
                        pe.wait_ge(st_free, (CHUNKS - 1) * it + ch + 1)
                        nc.tensor.matmul(o, q_in[:, at], state[:], start=True, stop=False)
                    pe.wait_ge(sc_ready, CHUNKS * it + ch + 1)
                    nc.tensor.matmul(o, sc[:, ch % 2, :], V[:, ch, :], start=(ch == 0), stop=True).then_inc(o_done, 1)
                    if ch < CHUNKS - 1:
                        pe.wait_ge(t_free, t_uses(it) + ch + 1)
                        pe.wait_ge(st_free, (CHUNKS - 1) * it + ch + 1)
                        nc.tensor.matmul(ST[:, 0:GLA_DV], kt[:, ch % 2, :], V[:, ch, :],
                                         start=True, stop=True).then_inc(st_done, 1)

                def transpose_o(it, n):
                    d, cg = n // 2, n % 2
                    if n == 0:
                        pe.wait_ge(on_ready, it + 1)
                    pe.wait_ge(t_free, t_uses(it) + CHUNKS + n)
                    for q in range(4):
                        ins = nc.tensor.transpose(T[:, q * P:(q + 1) * P], obuf[:, 4 * cg + q, d * P:(d + 1) * P],
                                                  c["ident"][:])
                    ins.then_inc(t_done, 1)

                def body(it, last):
                    for s in range(GLA_SLOTS):
                        if s < 3 * CHUNKS and s % 3 == 0:
                            scores(it, s // 3)
                        if s < 3 * CHUNKS and s % 3 == 2:
                            outputs(it, s // 3)
                        if s in (27, 28, 29, 30):
                            transpose_o(it, s - 27)
                        if not last:
                            if s == 25:
                                logits(it + 1, s_uses(it) + CHUNKS)
                            if s in (33, 34, 35, 36):
                                if s == 33:
                                    for half in range(NH):
                                        pe.wait_ge(g_free[half], g_uses(it) + 5)
                                transpose_v(s - 33, t_uses(it) + CHUNKS + 4 + s - 33)
                        fill(GLA_UNITS * it, GLA_UNITS + s // 8, s % 8, g_uses(it) + s // 8)
                rounds(pe, GLA_HEADS, body)

            @block.scalar
            def _(act):
                for _ in range(2):
                    act.sem_inc(o_free, 1)

                def copy_vt(d, half, use):
                    act.wait_ge(g_done[half], use + 1)
                    nc.scalar.copy(vt[:, d, half * HALF:(half + 1) * HALF], G[half][:]).then_inc(g_free[half], 1)

                def sigmoid_r(d, half, use):
                    act.wait_ge(g_done[half], use + 1)
                    nc.scalar.activation(RT[:, d, half * HALF:(half + 1) * HALF], G[half][:],
                                         ACT.Sigmoid).then_inc(r_sig, 1)

                def copy_v(n, use):
                    d, cg = n // 2, n % 2
                    act.wait_ge(t_done, use + 1)
                    nc.scalar.copy(V[:, 4 * cg:4 * cg + 4, d * P:(d + 1) * P],
                                   T[:].rearrange("p (j n) -> p j n", j=4)).then_inc(t_free, 1)

                def log_sigmoid(prep, use):
                    act.wait_ge(s_done, use + 1)
                    e, flat = E[:, 0, :], SC[:].rearrange("p l i -> p (l i)")
                    nc.scalar.activation(e, flat, ACT.Abs, bias=gb_h[:]).then_inc(abs_ready, 1)
                    act.wait_ge(abs_ready, 2 * prep + 1)
                    nc.scalar.activation(e, e, ACT.Exp, scale=-1.0).then_inc(abs_ready, 1)
                    act.wait_ge(abs_ready, 2 * prep + 2)
                    nc.scalar.activation(e, e, ACT.Ln, bias=1.0).then_inc(log_ready, 1)

                def exponential(prep, task):
                    act.wait_ge(d_ready, GLA_TASKS * prep + task + 1)
                    e = E[:, task % 2, :]
                    if task == 0:
                        nc.scalar.activation(dec[:], C[:].rearrange("p (c t) -> p c t", t=P)[:, :, P - 1],
                                             ACT.Exp, scale=1.0 / TAU)
                    nc.scalar.activation(e, C[:] if task == 0 else e, ACT.Exp,
                                         scale=1.0 / TAU).then_inc(e_ready, 1)

                for half in range(NH):
                    act.wait_ge(g_done[half], 1)
                    nc.scalar.copy(lr_t[:, half * HALF:(half + 1) * HALF], G[half][0:LR, :]).then_inc(g_free[half], 1)
                log_sigmoid(0, 0)
                for task in range(GLA_TASKS):
                    exponential(0, task)
                for d in range(2):
                    for half in range(NH):
                        copy_vt(d, half, 3 + d)
                for n in range(4):
                    if n == 2:
                        for half in range(NH):
                            sigmoid_r(0, half, 5)
                    copy_v(n, n)
                for half in range(NH):
                    sigmoid_r(1, half, 6)

                def copy_kt(it, ch):
                    act.wait_ge(t_done, t_uses(it) + ch + 1)
                    nc.scalar.copy(kt[:, ch % 2, :], T[:, 0:P]).then_inc(t_free, 1)

                def copy_o(it, ch):
                    act.wait_ge(o_done, CHUNKS * it + ch + 1)
                    nc.scalar.copy(obuf[:, ch, :], O[ch % 2][:, 0:GLA_DV]).then_inc(o_free, 1)
                    act.wait_ge(o_free, CHUNKS * it + ch + 3)
                    need(act, ssq_ready, CHUNKS * it + ch)
                    nc.scalar.activation(junk, obuf[:, ch, :], ACT.Square,
                                         accum_out=ssq[:, ch:ch + 1]).then_inc(ssq_ready, 1)

                def send_gate(n, half, use):
                    at = slice(half * HALF, (half + 1) * HALF)
                    act.wait_ge(g_done[half], use + 1)
                    need(act, gate_out[half], 16 * n)
                    nc.scalar.activation(q_new[:, at], G[half][:], ACT.Sigmoid).then_inc(g_free[half], 1)
                    act.wait_ge(g_free[half], use + 2)
                    act.dma_start(gates_t[(10 + n) * P:(11 + n) * P, at], q_new[:, at]).then_inc(gate_out[half], 16)

                def send_o(it, n):
                    d, cg = n // 2, n % 2
                    act.wait_ge(t_free, t_uses(it) + CHUNKS + n + 1)
                    act.dma_start(ogla_t[ds(it * GLA_DV + d * P, P), cg * HALF:(cg + 1) * HALF],
                                  gst[:]).then_inc(gst_out, 16)

                def body(it, last):
                    for s in range(GLA_SLOTS):
                        if s < 3 * CHUNKS and s % 3 == 0:
                            copy_kt(it, s // 3)
                        if 3 <= s <= 3 * CHUNKS and s % 3 == 0:
                            copy_o(it, s // 3 - 1)
                        if s in (28, 29, 30, 31):
                            send_o(it, s - 28)
                        if not last:
                            if s in (20, 24, 28, 32):
                                i = (s - 20) // 4
                                copy_vt(i // 2, i % 2, g_uses(it) + 2 + i // 2)
                            if s == 26:
                                log_sigmoid(it + 1, s_uses(it) + CHUNKS)
                            if s in (33, 34, 35, 36):
                                copy_v(s - 33, t_uses(it) + CHUNKS + 4 + s - 33)
                            if s in (31, 32, 34, 37, 38, 39, 41, 42, 43):
                                exponential(it + 1, (31, 32, 34, 37, 38, 39, 41, 42, 43).index(s))
                            if s in (36, 40, 44):
                                i = (s - 36) // 4
                                sigmoid_r(i // 2, i % 2, g_uses(it) + 4 + i // 2)
                        elif s >= 4 and s % 4 == 0:
                            i = s // 4 - 1
                            send_gate(i // 2, i % 2, g_uses(it) + i // 2)
                    if last:
                        send_gate(N_LAST_GATES - 1, 1, g_uses(it) + N_LAST_GATES - 1)
                    else:
                        sigmoid_r(1, 1, g_uses(it) + 5)
                rounds(act, GLA_HEADS, body)

            @block.vector
            def _(dve):
                chain = Chain(dve, dve_step)
                for sem_ in (g_free[0], g_free[1], s_free, st_free):
                    dve.sem_inc(sem_, 1)
                dve.wait_ge(small_loaded, 16 * (2 + GLA_HEADS + 2))
                nc.vector.tensor_copy(lr_hi[:], lr_raw[:]).then_inc(lr_split, 1)
                dve.wait_ge(lr_split, 1)
                nc.vector.tensor_tensor(lr_lo[:], lr_raw[:], lr_hi[:], ALU.subtract).then_inc(lr_split, 1)
                dve.wait_ge(made, N_MADE)

                def copy_q(half, use):
                    dve.wait_ge(g_done[half], use + 1)
                    nc.vector.tensor_scalar(q_new[:, half * HALF:(half + 1) * HALF], G[half][:], GLA_DK ** -0.5,
                                            None, ALU.mult).then_inc(g_free[half], 1)

                def copy_k(half, use):
                    dve.wait_ge(g_done[half], use + 1)
                    nc.vector.tensor_copy(k_new[:, half * HALF:(half + 1) * HALF], G[half][:]
                                          ).then_inc(g_free[half], 1)

                def head_gate(prep):
                    nc.vector.tensor_copy(w2_h[:], w2_all[:, ds(prep * GLA_DK, GLA_DK)])
                    nc.vector.tensor_copy(gb_h[:], gb_all[:, ds(prep, 1)]).then_inc(w2_ready, 1)

                def cumulate(prep, use):
                    dve.wait_ge(s_done, use + 1)
                    dve.wait_ge(abs_ready, 2 * prep + 1)
                    dve.wait_ge(w2_ready, prep + 1)
                    flat = SC[:].rearrange("p l i -> p (l i)")
                    e0, e1 = E[:, 0, :], E[:, 1, :]
                    nc.vector.tensor_scalar(e1, flat, gb_h[:], 0.0, ALU.add, ALU.min).then_inc(s_free, 1)
                    dve.wait_ge(log_ready, prep + 1)
                    dve.wait_ge(s_free, use + 2)
                    chain.link(nc.vector.tensor_tensor(e1, e1, e0, ALU.subtract))
                    nc.vector.tensor_tensor_scan(C[:], keep[:], e1, 0.0, ALU.mult, ALU.add).then_inc(d_ready, 1)
                    dve.wait_ge(d_ready, GLA_TASKS * prep + 1)

                def exponents(prep, task):
                    e = E[:, task % 2, :]
                    if task >= 2:
                        dve.wait_ge(f_ready, GLA_TASKS * prep + task - 1)
                    if task == 1:
                        view = lambda t: t.rearrange("p (c t) -> p c t", t=P)
                        nc.vector.tensor_tensor(view(e), view(C[:])[:, :, P - 1:P].to_broadcast([P, CHUNKS, P]),
                                                view(C[:]), ALU.subtract).then_inc(d_ready, 1)
                        return
                    half = 1 << (task - 2)
                    cb, eb = blocks(C[:], half), blocks(e, half)
                    mid = cb[:, :, 0, half - 1:half].to_broadcast([P, S // (2 * half), half])
                    nc.vector.tensor_tensor(eb[:, :, 0, :], mid, cb[:, :, 0, :], ALU.subtract)
                    nc.vector.tensor_tensor(eb[:, :, 1, :], cb[:, :, 1, :], mid, ALU.subtract).then_inc(d_ready, 1)

                def factors(prep, task):
                    dve.wait_ge(e_ready, GLA_TASKS * prep + task + 1)
                    e = E[:, task % 2, :]
                    if task == 0:
                        ins = nc.vector.tensor_tensor(q_in[:], q_new[:], e, ALU.mult)
                    elif task == 1:
                        ins = nc.vector.tensor_tensor(k_out[:], k_new[:], e, ALU.mult)
                    else:
                        half = 1 << (task - 2)
                        eb, xb = blocks(e, half), blocks(X[:, task - 2, :], half)
                        nc.vector.tensor_tensor(xb[:, :, 0, :], eb[:, :, 0, :], blocks(k_new[:], half)[:, :, 0, :], ALU.mult)
                        ins = nc.vector.tensor_tensor(xb[:, :, 1, :], eb[:, :, 1, :], blocks(q_new[:], half)[:, :, 1, :],
                                                      ALU.mult)
                    ins.then_inc(f_ready, 1)

                def diagonal():
                    nc.vector.tensor_copy(q_diag[:], q_new[:])
                    nc.vector.tensor_copy(k_diag[:], k_new[:])

                def gate_r(d, half, use, count):
                    dve.wait_ge(r_sig, count + 1)
                    r = RT[:, d, half * HALF:(half + 1) * HALF]
                    nc.vector.scalar_tensor_tensor(r, G[half][:], og[:, d:d + 1], r, ALU.mult,
                                                   ALU.mult).then_inc(g_free[half], 1)

                head_gate(0)
                for half in range(NH):
                    copy_q(half, 1)
                for half in range(NH):
                    copy_k(half, 2)
                chain.enter(0)
                cumulate(0, 0)
                diagonal()
                for task in range(GLA_TASKS):
                    if task + 1 < GLA_TASKS:
                        exponents(0, task + 1)
                    factors(0, task)
                for d in range(2):
                    for half in range(NH):
                        gate_r(d, half, 5 + d, 2 * d + half)
                first = chain.n

                def mask_scores(it, ch):
                    dve.wait_ge(s_done, s_uses(it) + ch + 1)
                    nc.vector.tensor_tensor(masked, SC[:], mask[:], ALU.mult).then_inc(s_free, 1)
                    dve.wait_ge(s_free, s_uses(it) + ch + 2)
                    nc.vector.tensor_reduce(sc[:, ch % 2, :], masked.rearrange("p l i -> p i l"), AX_X,
                                            ALU.add).then_inc(sc_ready, 1)

                def update(it, ch):
                    dve.wait_ge(st_done, (CHUNKS - 1) * it + ch + 1)
                    if ch == 0:
                        ins = nc.vector.tensor_copy(state[:], ST[:, 0:GLA_DV])
                    else:
                        dve.wait_ge(st_free, (CHUNKS - 1) * it + ch + 1)
                        ins = nc.vector.scalar_tensor_tensor(state[:], state[:], dec[:, ch:ch + 1], ST[:, 0:GLA_DV],
                                                             ALU.mult, ALU.add)
                    ins.then_inc(st_free, 1)

                def normalise(it):
                    dve.wait_ge(ssq_ready, CHUNKS * (it + 1))
                    ms, y, u = stat[:, 0, :], stat[:, 1, :], stat[:, 2, :]
                    chain.link(nc.vector.tensor_scalar(ms, ssq[:], 1.0 / GLA_DV, EPS, ALU.mult, ALU.add))
                    rsqrt(nc, chain, ms, y, u)
                    for ch in range(CHUNKS):
                        ins = nc.vector.tensor_scalar(obuf[:, ch, :], obuf[:, ch, :], y[:, ch:ch + 1], None, ALU.mult)
                    ins.then_inc(on_ready, 1)

                def gate_o(it, n):
                    d, cg = n // 2, n % 2
                    dve.wait_ge(t_done, t_uses(it) + CHUNKS + n + 1)
                    need(dve, gst_out, 16 * (4 * it + n))
                    nc.vector.tensor_tensor(gst[:], T[:], RT[:, d, cg * HALF:(cg + 1) * HALF], ALU.mult
                                            ).then_inc(t_free, 1)

                def body(it, last):
                    chain.enter(GLA_CHAIN * it + first)
                    for s in range(GLA_SLOTS):
                        if s < 3 * (CHUNKS - 1) + 1 and s % 3 == 0 and s:
                            update(it, s // 3 - 1)
                        if s < 3 * CHUNKS and s % 3 == 0:
                            mask_scores(it, s // 3)
                        if s == 25:
                            normalise(it)
                        if s in (27, 28, 29, 30):
                            gate_o(it, s - 27)
                        if not last:
                            if s in (4, 8):
                                copy_q(s // 4 - 1, g_uses(it))
                            if s in (12, 16):
                                copy_k(s // 4 - 3, g_uses(it) + 1)
                            if s == 24:
                                head_gate(it + 1)
                            if s == 31:
                                cumulate(it + 1, s_uses(it) + CHUNKS)
                                exponents(it + 1, 1)
                                diagonal()
                            if s == 32:
                                factors(it + 1, 0)
                                exponents(it + 1, 2)
                            if s in (34, 37, 38, 39, 41, 42, 43):
                                task = (34, 37, 38, 39, 41, 42, 43).index(s) + 1
                                factors(it + 1, task)
                                if task + 2 < GLA_TASKS:
                                    exponents(it + 1, task + 2)
                            if s in (36, 40, 44):
                                i = (s - 36) // 4
                                gate_r(i // 2, i % 2, g_uses(it) + 4 + i // 2, 4 * it + 4 + i)
                    if not last:
                        factors(it + 1, GLA_TASKS - 1)
                        gate_r(1, 1, g_uses(it) + 5, 4 * it + 7)
                        assert chain.n == GLA_CHAIN, chain.n
                rounds(dve, GLA_HEADS, body)


def branches(nc, o_t, gates_t, weights, merged_t):
    with ExitStack() as ctx:
        sb = lambda n, shape, dt=F32: ctx.enter_context(nc.sbuf_tensor(f"br_{n}", shape, dt))
        sem = lambda n: ctx.enter_context(nc.semaphore(f"br_{n}"))
        W = Weights(nc, ctx, "brw", 2)
        parts = [[sb(f"o{b}_{part}", [P, KT, S], F32R) for part in ("hi", "lo")] for b in range(2)]
        stage = sb("stage", [P, 2, S])
        sig = sb("sig", [P, 2, S])
        merged = sb("merged", [P, S])
        term = sb("term", [P, 2, HALF])
        acc = [[ctx.enter_context(nc.psum_tensor(f"br_acc{b}{h}", [P, HALF], F32)) for h in range(NH)] for b in range(2)]
        loaded = [sem(f"loaded{i}") for i in range(2)]
        hi_done, lo_done = sem("hi_done"), sem("lo_done")
        sig_loaded, out_done = sem("sig_loaded"), sem("out_done")
        acc_done = sem("acc_done")
        acc_free = sem("acc_free")
        m_ready = sem("m_ready")
        row_tiles = [(b, k) for b in range(2) for k in range(KT)]
        with nc.Block() as block:
            @block.sync
            def _(sp):
                def load_sig(j):
                    sp.dma_start(sig[:], gates_t.rearrange("(b r) t -> r b t", b=2)[ds(j * P, P), :, :]
                                 ).then_inc(sig_loaded, 16)

                W.load(sp, 0, 0, weight_cols(weights[0], 0))
                W.load(sp, 0, 1, weight_cols(weights[1], 0))
                for n, (b, k) in enumerate(row_tiles):
                    if n >= 2:
                        sp.wait_ge(lo_done, n - 1)
                    sp.dma_start(stage[:, n % 2, :], o_t[b][k * P:(k + 1) * P, :]).then_inc(loaded[n % 2], 16)
                load_sig(0)

                def body(j, last):
                    if not last:
                        for b in range(2):
                            W.load(sp, 2 * j, 2 + b, weight_cols(weights[b], j * P + P))
                    for half in range(NH):
                        sp.wait_ge(m_ready, NH * j + half + 1)
                        sp.dma_start(merged_t[ds(j * P, P), half * HALF:(half + 1) * HALF],
                                     merged[:, half * HALF:(half + 1) * HALF]).then_inc(out_done, 16)
                    if not last:
                        load_sig(j + 1)
                rounds(sp, KT, body)
                sp.wait_ge(out_done, 16 * NH * KT)

            @block.gpsimd
            def _(pool):
                W.prime_pool(pool)
                W.split(pool, 0, 0)
                W.split(pool, 0, 1)

                def body(j, last):
                    for b in range(2):
                        W.split(pool, 2 * j, 2 + b, (acc_done, 4 * j + 2 * b + 2))
                with pool.Fori(0, KT - 1, 1) as j:
                    body(j, False)

            @block.scalar
            def _(act):
                for n, (b, k) in enumerate(row_tiles):
                    act.wait_ge(loaded[n % 2], 16 * (n // 2 + 1))
                    nc.scalar.copy(parts[b][0][:, k, :], stage[:, n % 2, :]).then_inc(hi_done, 1)

            @block.vector
            def _(dve):
                dve.sem_inc(acc_free, 4)
                for n, (b, k) in enumerate(row_tiles):
                    dve.wait_ge(hi_done, n + 1)
                    nc.vector.tensor_tensor(parts[b][1][:, k, :], stage[:, n % 2, :], parts[b][0][:, k, :],
                                            ALU.subtract).then_inc(lo_done, 1)

                def body(j, last):
                    dve.wait_ge(sig_loaded, 16 * (j + 1))
                    for b in range(2):
                        for half in range(NH):
                            at = slice(half * HALF, (half + 1) * HALF)
                            dve.wait_ge(acc_done, 4 * j + 2 * b + half + 1)
                            if b == 0:
                                need(dve, out_done, 16 * NH * j)
                            dst = merged[:, at] if b == 0 else term[:, half, :]
                            nc.vector.tensor_tensor(dst, acc[b][half][:], sig[:, b, at], ALU.mult).then_inc(acc_free, 1)
                            if b == 1:
                                dve.wait_ge(acc_free, 4 + 4 * j + 3 + half)
                                nc.vector.tensor_tensor(merged[:, at], merged[:, at], term[:, half, :],
                                                        ALU.add).then_inc(m_ready, 1)
                rounds(dve, KT, body)

            @block.tensor
            def _(pe):
                def body(j, last):
                    for b in range(2):
                        W.take(pe, 2 * j, b)
                        if isinstance(j, int) or True:
                            pe.wait_ge(lo_done, KT * (b + 1))
                        for half in range(NH):
                            pe.wait_ge(acc_free, 4 * j + 2 * b + half + 1)
                            project_part(nc, acc[b][half][:], W.tile(b), parts[b], half, 0, 1).then_inc(acc_done, 1)
                rounds(pe, KT, body)


def output_projection(nc, merged_t, x, w_out, y):
    PAIR = 2 * P
    with ExitStack() as ctx:
        sb = lambda n, shape, dt=F32: ctx.enter_context(nc.sbuf_tensor(f"op_{n}", shape, dt))
        sem = lambda n: ctx.enter_context(nc.semaphore(f"op_{n}"))
        W = Weights(nc, ctx, "opw", 4)
        m_hi, m_lo = sb("m_hi", [P, KT, S], F32R), sb("m_lo", [P, KT, S], F32R)
        stage = sb("stage", [P, 2, S])
        bank = [ctx.enter_context(nc.psum_tensor(f"op_acc{i}", [P, HALF], F32)) for i in range(4)]
        loaded = [sem(f"loaded{i}") for i in range(2)]
        hi_done, lo_done = sem("hi_done"), sem("lo_done")
        x_loaded = sem("x_loaded")
        acc_done, acc_free = sem("acc_done"), sem("acc_free")
        with nc.Block() as block:
            @block.sync
            def _(sp):
                for n in range(2):
                    W.load(sp, 0, n, weight_cols(w_out, n * P))
                for n in range(KT):
                    if n >= 2:
                        sp.wait_ge(lo_done, n - 1)
                    sp.dma_start(stage[:, n % 2, :], merged_t[n * P:(n + 1) * P, :]).then_inc(loaded[n % 2], 16)
                for i in range(TT):
                    sp.dma_start(y[:, i, :], x[i * P:(i + 1) * P, :]).then_inc(x_loaded, 16)
                for n in range(2, 8):
                    W.load(sp, 0, n, weight_cols(w_out, n * P))

            @block.gpsimd
            def _(pool):
                W.prime_pool(pool)
                for n in range(8):
                    W.split(pool, 0, n, (acc_done, TT * ((n - 4) // 2 + 1)) if n >= 4 else None)

            @block.scalar
            def _(act):
                for n in range(KT):
                    act.wait_ge(loaded[n % 2], 16 * (n // 2 + 1))
                    nc.scalar.copy(m_hi[:, n, :], stage[:, n % 2, :]).then_inc(hi_done, 1)

            @block.vector
            def _(dve):
                dve.sem_inc(acc_free, 4)
                for n in range(KT):
                    dve.wait_ge(hi_done, n + 1)
                    nc.vector.tensor_tensor(m_lo[:, n, :], stage[:, n % 2, :], m_hi[:, n, :],
                                            ALU.subtract).then_inc(lo_done, 1)
                dve.wait_ge(x_loaded, 16 * TT)
                with dve.Fori(0, D // PAIR, 1) as p:
                    for t in range(TT):
                        dve.wait_ge(acc_done, TT * p + t + 1)
                        at = y[:, t, ds(p * PAIR, PAIR)]
                        nc.vector.tensor_tensor(at, bank[t % 4][:, 0:PAIR], at, ALU.add).then_inc(acc_free, 1)

            @block.tensor
            def _(pe):
                pe.wait_ge(lo_done, KT)
                with pe.Fori(0, 2, 1) as p2:
                    for j in range(2):
                        for n in range(2):
                            W.take(pe, 4 * p2, 2 * j + n)
                        hi, lo = (w[:, 2 * j:2 * j + 2, :].rearrange("p s (k c) -> p k s c", k=KT) for w in (W.hi, W.lo))
                        for t in range(TT):
                            pe.wait_ge(acc_free, 2 * TT * p2 + TT * j + t + 1)
                            steps = [(a, b, k) for a, b in ((m_hi, hi), (m_hi, lo), (m_lo, hi)) for k in range(KT)]
                            out = bank[t % 4][:, 0:PAIR].rearrange("p (s c) -> p s c", s=2)
                            for n, (a, b, k) in enumerate(steps):
                                ins = nc.tensor.matmul(out, a[:, k, t * P:(t + 1) * P], b[:, k],
                                                       start=(n == 0), stop=(n == len(steps) - 1))
                            ins.then_inc(acc_done, 1)


def feed_forward(nc, hT, w_gate, w_up, w_down, y, out):
    CHUNK = 2
    N = FF // P // CHUNK
    OUTS = TT * NH
    ROUND = 4 * CHUNK + OUTS
    with ExitStack() as ctx:
        sb = lambda n, shape, dt=F32: ctx.enter_context(nc.sbuf_tensor(f"ff_{n}", shape, dt))
        sem = lambda n: ctx.enter_context(nc.semaphore(f"ff_{n}"))
        W = Weights(nc, ctx, "ffw", 3)
        hid_hi = sb("hid_hi", [P, 2, CHUNK, S], F32R)
        hid_lo = sb("hid_lo", [P, 2, CHUNK, S], F32R)
        act_buf = sb("act", [P, NH, HALF])
        ps = lambda n: ctx.enter_context(nc.psum_tensor(f"ff_{n}", [P, HALF], F32))
        gate, up = [ps(f"gate{h}") for h in range(NH)], [ps(f"up{h}") for h in range(NH)]
        down = [ps(f"down{i}") for i in range(4)]
        pe_done = sem("pe_done")
        sig_done = sem("sig_done")
        silu_done = sem("silu_done")
        gu_free = sem("gu_free")
        hi_done, lo_done = sem("hi_done"), sem("lo_done")
        d_free = sem("d_free")
        out_done = sem("out_done")
        base = lambda c: 8 + ROUND * c
        tiles = lambda k: 12 * k

        def steps(eng, prologue, step):
            prologue()
            with eng.Fori(0, (N - 1) // 2, 1) as k:
                for j in range(2):
                    step(k, j, False)
            step((N - 1) // 2, 0, True)

        with nc.Block() as block:
            @block.sync
            def _(sp):
                def units(k, first, col):
                    for n, w in enumerate((w_gate, w_up, w_gate, w_up)):
                        W.load(sp, tiles(k), first + n, weight_cols(w, col + (n // 2) * P))

                def step(k, j, last):
                    if not last:
                        units(k, 4 + 6 * j, k * (4 * P) + (j + 1) * 2 * P)
                    for f in range(CHUNK):
                        row = k * (4 * P) + (2 * j + f) * P
                        W.load(sp, tiles(k), 4 + 6 * j + f + (0 if last else 4),
                               w_down[ds(row, P), :].rearrange("p (k c) -> p k c", k=KT))
                steps(sp, lambda: units(0, 0, 0), step)
                for t in range(TT):
                    sp.wait_ge(d_free, 4 + OUTS * (N - 1) + NH * (t + 1))
                    sp.dma_start(out[t * P:(t + 1) * P, :], y[:, t, :]).then_inc(out_done, 16)
                sp.wait_ge(out_done, 16 * TT)

            @block.gpsimd
            def _(pool):
                W.prime_pool(pool)

                def prologue():
                    for n in range(3):
                        W.split(pool, 0, n)
                    W.split(pool, 0, 3, (pe_done, 2))

                def step(k, j, last):
                    c = 2 * k + j
                    done = [base(c) - 4, base(c), base(c), base(c) + 2, base(c) + 4, base(c) + 6]
                    for n in range(2 if last else 6):
                        W.split(pool, tiles(k), 4 + 6 * j + n, (pe_done, done[n]))
                steps(pool, prologue, step)

            @block.tensor
            def _(pe):
                def units(k, first, chunk):
                    for n in range(4):
                        W.take(pe, tiles(k), first + n)
                        for half in range(NH):
                            f = n // 2
                            if n % 2 == 0:
                                pe.wait_ge(gu_free, 2 * (2 * chunk + f) + half + 1)
                            acc = (gate, up)[n % 2][half]
                            project_part(nc, acc[:], W.tile(first + n), hT, half, 0, 1).then_inc(pe_done, 1)

                def step(k, j, last):
                    c = 2 * k + j
                    if not last:
                        units(k, 4 + 6 * j, c + 1)
                    first = 4 + 6 * j + (0 if last else 4)
                    for f in range(CHUNK):
                        W.take(pe, tiles(k), first + f)
                    pe.wait_ge(lo_done, 2 * CHUNK * (c + 1))
                    w = [(W.hi[:, (first + f) % 3, :], W.lo[:, (first + f) % 3, :]) for f in range(CHUNK)]
                    for o in range(OUTS):
                        t, nh = o // NH, o % NH
                        pe.wait_ge(d_free, OUTS * c + o + 1)
                        rows, cols = slice(t * P, (t + 1) * P), slice(nh * HALF, (nh + 1) * HALF)
                        for n in range(3 * CHUNK):
                            f, kind = n // 3, n % 3
                            h = (hid_hi, hid_hi, hid_lo)[kind][:, j, f, rows]
                            ins = nc.tensor.matmul(down[o % 4][:], h, w[f][(0, 1, 0)[kind]][:, cols],
                                                   start=(n == 0), stop=(n == 3 * CHUNK - 1))
                        ins.then_inc(pe_done, 1)
                steps(pe, lambda: units(0, 0, 0), step)

            @block.scalar
            def _(act):
                def units(at, chunk, buf):
                    for f in range(CHUNK):
                        for half in range(NH):
                            num = 2 * CHUNK * chunk + 2 * f + half
                            act.wait_ge(pe_done, at + 4 * f + half + 1)
                            need(act, lo_done, num - 1)
                            nc.scalar.activation(act_buf[:, half, :], gate[half][:], ACT.Sigmoid).then_inc(sig_done, 1)
                            act.wait_ge(gu_free, num + 3)
                            nc.scalar.copy(hid_hi[:, buf, f, half * HALF:(half + 1) * HALF], act_buf[:, half, :]
                                           ).then_inc(hi_done, 1)

                def step(k, j, last):
                    if not last:
                        units(base(2 * k + j), 2 * k + (j + 1), (j + 1) % 2)
                steps(act, lambda: units(0, 0, 0), step)

            @block.vector
            def _(dve):
                dve.sem_inc(gu_free, 2)
                dve.sem_inc(d_free, 4)

                def units(at, chunk, buf):
                    for f in range(CHUNK):
                        for half in range(NH):
                            num, a = 2 * CHUNK * chunk + 2 * f + half, act_buf[:, half, :]
                            dve.wait_ge(sig_done, num + 1)
                            nc.vector.tensor_tensor(a, gate[half][:], a, ALU.mult).then_inc(silu_done, 1)
                            dve.wait_ge(silu_done, num + 1)
                            dve.wait_ge(pe_done, at + 4 * f + 2 + half + 1)
                            nc.vector.tensor_tensor(a, up[half][:], a, ALU.mult).then_inc(gu_free, 1)
                            dve.wait_ge(hi_done, num + 1)
                            cols = slice(half * HALF, (half + 1) * HALF)
                            nc.vector.tensor_tensor(hid_lo[:, buf, f, cols], a, hid_hi[:, buf, f, cols],
                                                    ALU.subtract).then_inc(lo_done, 1)

                def step(k, j, last):
                    c = 2 * k + j
                    if not last:
                        units(base(c), 2 * k + (j + 1), (j + 1) % 2)
                    first = base(c) + (0 if last else 4 * CHUNK)
                    for o in range(OUTS):
                        t, nh = o // NH, o % NH
                        at = y[:, t, nh * HALF:(nh + 1) * HALF]
                        dve.wait_ge(pe_done, first + o + 1)
                        nc.vector.tensor_tensor(at, down[o % 4][:], at, ALU.add).then_inc(d_free, 1)
                steps(dve, lambda: units(0, 0, 0), step)


def layer(nc, x, norm1_g, w_in, sb_q_norm_g, sb_k_norm_g, gla_gate_w2, gla_gate_b, gla_out_norm_g,
          w_branch_sb, w_branch_gla, w_out, norm2_g, w_ffn_gate, w_ffn_up, w_ffn_down, out):
    scratch = lambda n, rows: nc.dram_tensor(n, [rows, S], F32, kind="Internal").ap()
    osb_t, ogla_t, merged_t = scratch("osb_t", D), scratch("ogla_t", D), scratch("merged_t", D)
    gates_t = scratch("gates_t", 2 * D)
    with ExitStack() as ctx:
        c = constants(nc, ctx)
        with ExitStack() as heads:
            hT = [heads.enter_context(nc.sbuf_tensor(f"h1_{n}", [P, KT, S], F32R)) for n in ("hi", "lo")]
            with ExitStack() as first:
                x_sb = first.enter_context(nc.sbuf_tensor("x_sb", [P, TT, D], F32))
                norm_transposed(nc, c, "norm1", x[0], x_sb, norm1_g, hT)
            linear_attention(nc, c, hT, w_in[0], gla_gate_w2[0], gla_gate_b, gla_out_norm_g, ogla_t, gates_t)
            stick_breaking(nc, c, hT, w_in[0], (sb_q_norm_g, sb_k_norm_g), osb_t, gates_t)
        branches(nc, (osb_t, ogla_t), gates_t, (w_branch_sb[0], w_branch_gla[0]), merged_t)
        y = ctx.enter_context(nc.sbuf_tensor("y", [P, TT, D], F32))
        output_projection(nc, merged_t, x[0], w_out[0], y)
        hT = [ctx.enter_context(nc.sbuf_tensor(f"h2_{n}", [P, KT, S], F32R)) for n in ("hi", "lo")]
        norm_transposed(nc, c, "norm2", None, y, norm2_g, hT)
        feed_forward(nc, hT, w_ffn_gate[0], w_ffn_up[0], w_ffn_down[0], y, out[0])


_INS = ["x", "norm1_g", "w_in", "sb_q_norm_g", "sb_k_norm_g", "gla_gate_w2", "gla_gate_b", "gla_out_norm_g",
        "w_branch_sb", "w_branch_gla", "w_out", "norm2_g", "w_ffn_gate", "w_ffn_up", "w_ffn_down"]


def kernel(**inputs):
    import concourse.bacc as bacc
    from concourse.bass_utils import run_bass_kernel_spmd

    nc = bacc.Bacc("TRN2", target_bir_lowering=False, num_devices=1)
    arrays = {n: np.ascontiguousarray(inputs[n]) for n in _INS}
    args = [nc.dram_tensor(n, a.shape, mybir.dt.from_np(a.dtype), kind="ExternalInput").ap()
            for n, a in arrays.items()]
    out = nc.dram_tensor("out", [1, S, D], F32, kind="ExternalOutput").ap()
    layer(nc, *args, out)
    result = run_bass_kernel_spmd(nc, [arrays], core_ids=[0])
    return result.results[0]["out"]
```

```python
from contextlib import ExitStack

import numpy as np
import concourse.bass as bass
from concourse import mybir

F32 = mybir.dt.float32
F32R = mybir.dt.float32r
I32 = mybir.dt.int32
BF16 = mybir.dt.bfloat16
ALU = mybir.AluOpType
ACT = mybir.ActivationFunctionType
AX_X = mybir.AxisListType.X
ds = bass.ds

P = 128
S = 1024
D = 1024
KT = D // P
TT = S // P
HALF = 512
NH = S // HALF
EPS = 1e-6

SB_HEADS, SB_DH = 16, 64
PAIRS = SB_HEADS * SB_DH // P
GLA_HEADS, GLA_DK, GLA_DV = 4, 128, 256
LR = 16
TAU = 16.0
FF = 2816

SBQ, SBK, SBV = 0, 1024, 2048
GLQ, GLK, GLV, GLR, GLLR = 3072, 3584, 4096, 5120, 6144
GATE = 6160


def need(eng, sem, value):
    if isinstance(value, int) and value <= 0:
        return
    eng.wait_ge(sem, value)


class Chain:

    def __init__(self, eng, sem):
        self.eng, self.sem, self.base, self.n = eng, sem, 0, 0

    def enter(self, base):
        self.base, self.n = base, 0

    def link(self, ins):
        self.n += 1
        ins.then_inc(self.sem, 1)
        self.eng.wait_ge(self.sem, self.base + self.n)


def rounds(eng, count, body):
    with eng.Fori(0, count - 1, 1) as i:
        body(i, False)
    body(count - 1, True)


class Weights:

    def __init__(self, nc, ctx, name, ring):
        self.nc, self.ring = nc, ring
        sb = lambda n, dt: ctx.enter_context(nc.sbuf_tensor(f"{name}_{n}", [P, ring, D], dt))
        sem = lambda n: ctx.enter_context(nc.semaphore(f"{name}_{n}"))
        self.ones = ctx.enter_context(nc.sbuf_tensor(f"{name}_ones", [P, 64], F32))
        self.raw, self.hi, self.lo = sb("raw", F32), sb("hi", F32R), sb("lo", F32R)
        self.loaded = [sem(f"loaded{i}") for i in range(ring)]
        self.rounded = sem("rounded")
        self.ready = sem("ready")

    def prime_pool(self, pool):
        self.nc.gpsimd.memset(self.ones[:], 1.0).then_inc(self.rounded, 1)
        pool.wait_ge(self.rounded, 1)
        pool.sem_inc(self.ready, self.ring)

    def take(self, pe, lot, step):
        pe.wait_ge(self.ready, self.ring + lot + step + 1)

    def load(self, sp, lot, step, src):
        s = step % self.ring
        need(sp, self.ready, lot + step + 1)
        dst = self.raw[:, s, :].rearrange("p (k c) -> p k c", k=src.shape[1])
        sp.dma_start(dst, src).then_inc(self.loaded[s], 16)

    def split(self, pool, lot, step, done=None):
        s = step % self.ring
        raw, hi, lo = self.raw[:, s, :], self.hi[:, s, :], self.lo[:, s, :]
        pool.wait_ge(self.loaded[s], (lot // self.ring + step // self.ring + 1) * 16)
        if done is not None:
            pool.wait_ge(*done)
        self.nc.gpsimd.tensor_tensor(hi[:, 0:64], raw[:, 0:64], self.ones[:], ALU.mult)
        self.nc.gpsimd.tensor_scalar(hi[:, 64:D], raw[:, 64:D], 1.0, 0.0, ALU.mult, ALU.add).then_inc(self.rounded, 1)
        pool.wait_ge(self.rounded, lot + step + 2)
        self.nc.gpsimd.tensor_tensor(lo, raw, hi, ALU.subtract).then_inc(self.ready, 1)

    def tile(self, step):
        s = step % self.ring
        view = lambda t: t[:, s, :].rearrange("p (k c) -> p k c", k=KT)
        return view(self.hi), view(self.lo)


def weight_cols(w, col):
    return w.rearrange("(k p) c -> p k c", p=P)[:, :, ds(col, P)]


def project_part(nc, acc, wt, xt, half, part, parts):
    (w_hi, w_lo), (x_hi, x_lo) = wt, xt
    steps = [(a, b, k) for a, b in ((w_hi, x_hi), (w_hi, x_lo), (w_lo, x_hi)) for k in range(KT)]
    per = len(steps) // parts
    ins = None
    for n in range(part * per, (part + 1) * per):
        a, b, k = steps[n]
        ins = nc.tensor.matmul(acc, a[:, k, :], b[:, k, half * HALF:(half + 1) * HALF],
                               start=(n == 0), stop=(n == len(steps) - 1))
    return ins




def constants(nc, ctx):
    sb = lambda n, shape, dt: ctx.enter_context(nc.sbuf_tensor(n, shape, dt))
    c = {
        "ident": sb("ident", [P, P], F32), "ident_b": sb("ident_b", [P, P], BF16),
        "not_before": sb("not_before", [P, P], BF16), "head_mean": sb("head_mean", [P, P // SB_DH], F32),
    }
    made = ctx.enter_context(nc.semaphore("const_made"))
    with nc.Block() as block:
        @block.gpsimd
        def _(pool):
            chain = Chain(pool, made)
            for name in ("ident", "ident_b", "not_before", "head_mean"):
                chain.link(nc.gpsimd.memset(c[name][:], 0.0))
            for r in range(0, P, SB_DH):
                chain.link(nc.gpsimd.memset(c["head_mean"][r:r + SB_DH, r // SB_DH:r // SB_DH + 1], 1.0 / SB_DH))
            for name in ("ident", "ident_b"):
                chain.link(nc.gpsimd.affine_select(out=c[name][:], in_=c[name][:], compare_op=ALU.not_equal,
                                                   fill=1.0, base=0, pattern=[[-1, P]], channel_multiplier=1))
            chain.link(nc.gpsimd.affine_select(out=c["not_before"][:], in_=c["not_before"][:],
                                               compare_op=ALU.is_gt, fill=-1e30, base=0, pattern=[[-1, P]],
                                               channel_multiplier=1))
    return c


def rsqrt_guess(nc, chain, ms, y):
    chain.link(nc.vector.tensor_scalar(y.bitcast(I32), ms.bitcast(I32), -0.5, 1597463007.0, ALU.mult, ALU.add))
    chain.link(nc.vector.tensor_scalar(ms, ms, -0.5, None, ALU.mult))


def rsqrt_newton(nc, chain, ms, y, u):
    chain.link(nc.vector.tensor_tensor(u, y, y, ALU.mult))
    chain.link(nc.vector.tensor_tensor(u, u, ms, ALU.mult))
    chain.link(nc.vector.scalar_tensor_tensor(y, u, 1.5, y, ALU.add, ALU.mult))


def rsqrt(nc, chain, ms, y, u):
    rsqrt_guess(nc, chain, ms, y)
    for _ in range(3):
        rsqrt_newton(nc, chain, ms, y, u)


def norm_transposed(nc, c, name, src, x, gain, hT):
    h_hi, h_lo = hT
    with ExitStack() as ctx:
        sb = lambda n, shape, dt: ctx.enter_context(nc.sbuf_tensor(f"{name}_{n}", shape, dt))
        sem = lambda n: ctx.enter_context(nc.semaphore(f"{name}_{n}"))
        g_all = sb("g_all", [P, D], F32)
        h = sb("h", [P, 2, D], F32)
        junk = sb("junk", [P, D], F32)
        ssq = sb("ssq", [P, TT], F32)
        work = sb("work", [P, 3, TT], F32)
        bank = [ctx.enter_context(nc.psum_tensor(f"{name}_t{i}", [P, 4, P], F32)) for i in range(4)]
        x_loaded = [sem(f"x_loaded{i}") for i in range(TT)]
        g_loaded = sem("g_loaded")
        ssq_ready = sem("ssq_ready")
        dve_step = sem("dve_step")
        h_ready = sem("h_ready")
        t_done = sem("t_done")
        hi_done = sem("hi_done")
        lo_done = sem("lo_done")
        with nc.Block() as block:
            @block.sync
            def _(sp):
                sp.dma_start(g_all[:], gain[0].partition_broadcast(P)).then_inc(g_loaded, 16)
                if src is not None:
                    for i in range(TT):
                        sp.dma_start(x[:, i, :], src[i * P:(i + 1) * P, :]).then_inc(x_loaded[i], 16)

            @block.scalar
            def _(act):
                for i in range(TT):
                    if src is not None:
                        act.wait_ge(x_loaded[i], 16)
                    if i:
                        act.wait_ge(ssq_ready, i)
                    nc.scalar.activation(junk[:], x[:, i, :], ACT.Square,
                                         accum_out=ssq[:, i:i + 1]).then_inc(ssq_ready, 1)
                with act.Fori(0, TT // 2, 1) as i:
                    for u in range(4):
                        act.wait_ge(t_done, 4 * i + u + 1)
                        nc.scalar.copy(h_hi[:, 4 * (u % 2):4 * (u % 2) + 4, ds(i * 2 * P + (u // 2) * P, P)],
                                       bank[u][:]).then_inc(hi_done, 1)

            @block.vector
            def _(dve):
                chain = Chain(dve, dve_step)
                dve.sem_inc(lo_done, 4)
                dve.wait_ge(ssq_ready, TT)
                chain.link(nc.vector.tensor_scalar(work[:, 0, :], ssq[:], 1.0 / D, EPS, ALU.mult, ALU.add))
                rsqrt(nc, chain, work[:, 0, :], work[:, 1, :], work[:, 2, :])
                dve.wait_ge(g_loaded, 16)
                rstd = work[:, 1, :]

                def normalise(i, b):
                    nc.vector.scalar_tensor_tensor(h[:, b, :], x[:, ds(2 * i + b, 1), :].rearrange("p a d -> p (a d)"),
                                                   rstd[:, ds(2 * i + b, 1)], g_all[:],
                                                   ALU.mult, ALU.mult).then_inc(h_ready, 1)

                normalise(0, 0)
                normalise(0, 1)

                def lows(i, b):
                    for u in (2 * b, 2 * b + 1):
                        dve.wait_ge(hi_done, 4 * i + u + 1)
                        at = (slice(None), slice(4 * (u % 2), 4 * (u % 2) + 4), ds(i * 2 * P + (u // 2) * P, P))
                        nc.vector.tensor_tensor(h_lo[at], bank[u][:], h_hi[at], ALU.subtract).then_inc(lo_done, 1)

                def body(i, last):
                    for b in range(2):
                        lows(i, b)
                        if not last:
                            normalise(i + 1, b)
                rounds(dve, TT // 2, body)

            @block.tensor
            def _(pe):
                with pe.Fori(0, TT // 2, 1) as i:
                    for u in range(4):
                        b, half = u // 2, u % 2
                        if half == 0:
                            pe.wait_ge(h_ready, 2 * i + b + 1)
                        pe.wait_ge(lo_done, 4 * i + u + 1)
                        for q in range(4):
                            k = 4 * half + q
                            ins = nc.tensor.transpose(bank[u][:, q, :], h[:, b, k * P:(k + 1) * P], c["ident"][:])
                        ins.then_inc(t_done, 1)


SLOTS = 32
SCORE_SLOT = [0, 1, 2, 3, 4, 5, 6, 8, 10, 11, 12, 13, 14, 15, 16, 17]
SCORE_STEPS = [(hh, tb) for hh in range(2) for tb in range(TT)]
WEIGHT_STEPS = [(hh, g, j) for hh in range(2) for g in range(NH) for j in range(4 * g + 4)]
WEIGHT_SLOT = 7
NSC, NWT = len(SCORE_STEPS), len(WEIGHT_STEPS)
STACKS = 12
SB_CHAIN = 22
MS_SLOT = [6, 10, 13, 17]
V_SLOT = [25, 27]
SPREAD_SLOT = [14, 18]


def stick_breaking(nc, c, hT, w_in, qk_gains, osb_t, gates_t):
    with ExitStack() as ctx:
        sb = lambda n, shape, dt: ctx.enter_context(nc.sbuf_tensor(f"sb_{n}", shape, dt))
        ps = lambda n, shape: ctx.enter_context(nc.psum_tensor(f"sb_{n}", shape, F32))
        sem = lambda n: ctx.enter_context(nc.semaphore(f"sb_{n}"))
        W = Weights(nc, ctx, "sbw", 2)
        qs = [sb(f"qs{e}", [P, S], F32R) for e in range(2)]
        kh = [sb(f"kh{e}", [P, S], F32R) for e in range(2)]
        kl = [sb(f"kl{e}", [P, S], F32R) for e in range(2)]
        k_new = sb("k_new", [P, S], F32)
        q_st = sb("q_st", [P, 2, S], F32R)
        k_st = sb("k_st", [P, 2, S], F32R)
        sq = sb("sq", [P, NH, HALF], F32)
        gains = sb("gains", [P, 2], F32)
        ms = sb("ms", [P, 2, TT * 2], F32)
        rms = sb("rms", [P, 2, TT * 2], F32)
        tmp = sb("tmp", [P, TT * 2], F32)
        k_rs = sb("k_rs", [P, TT, P], F32)
        q_scale = sb("q_scale", [P, 2, TT * 2], F32)
        vt = sb("vt", [P, S], F32)
        v = sb("v", [P, TT, 2, 2, SB_DH], F32R)
        rest = sb("rest", [P, 2, S + 1], F32)
        beta = sb("beta", [P, 2, S], F32)
        rows = [sb(f"rows{g}", [P, 4, HALF * (g + 1)], F32) for g in range(NH)]
        wt_hi = sb("wt_hi", [P, 2, HALF], F32R)
        wt_lo = sb("wt_lo", [P, 2, HALF], F32R)
        o_low = sb("o_low", [SB_DH, HALF], F32)
        ot = sb("ot", [P, S], F32)
        G = [ps(f"g{h}", [P, HALF]) for h in range(NH)]
        Z = [ps(f"z{b}", [P, S]) for b in range(2)]
        T = ps("t", [P, HALF])
        O = ps("o", [P, HALF])

        g_loaded, gains_made = sem("g_loaded"), sem("gains_made")
        g_done = [sem(f"g_done{h}") for h in range(NH)]
        g_free = [sem(f"g_free{h}") for h in range(NH)]
        sq_ready = sem("sq_ready")
        k_rs_ready = sem("k_rs_ready")
        q_scale_ready = sem("q_scale_ready")
        q_high, k_high = sem("q_high"), sem("k_high")
        split_done = sem("split_done")
        half_copied = sem("half_copied")
        stacked = sem("stacked")
        z_done = sem("z_done")
        z_free = sem("z_free")
        row_ready = sem("row_ready")
        scanned = sem("scanned")
        t_done = sem("t_done")
        hi_ready = sem("hi_ready")
        lo_ready = sem("lo_ready")
        vt_done = sem("vt_done")
        v_high = sem("v_high")
        v_ready = sem("v_ready")
        av_done = sem("av_done")
        o_free = sem("o_free")
        ot_out = sem("ot_out")
        gs_out = sem("gs_out")
        dve_step = sem("dve_step")

        units = lambda it: 4 * it
        g_uses = lambda it: 6 + 7 * it
        t_uses = lambda it: NWT * it
        LAST_GATES = 3

        def rows_used(it, e, tb):
            before = WEIGHT_STEPS.index((0, tb // 4, tb)) + 1
            return t_uses(it) + before + (NWT if e == 1 else NWT // 2)

        def slot_of_unit(s):
            return s // 8, s % 8

        with nc.Block() as block:
            @block.sync
            def _(sp):
                for half in range(2):
                    for x in range(2):
                        sp.dma_start(gains[half * SB_DH:(half + 1) * SB_DH, x:x + 1],
                                     qk_gains[x].rearrange("a d -> d a")).then_inc(g_loaded, 16)

                def stacks(it):
                    sp.wait_ge(split_done, NH * (it + 2))
                    need(sp, z_done, NSC * (it + 1))
                    for e in range(2):
                        rows_e = slice(e * SB_DH, (e + 1) * SB_DH)
                        for top in range(2):
                            to = slice(top * SB_DH, (top + 1) * SB_DH)
                            for dst, src, x in ((qs[e], q_st, top), (kh[e], k_st, 0), (kl[e], k_st, 1)):
                                sp.dma_start(dst[to, :].bitcast(F32), src[rows_e, x, :].bitcast(F32)).then_inc(stacked, 16)

                for step, col in enumerate((SBK, SBQ, SBV)):
                    W.load(sp, 0, step, weight_cols(w_in, col))
                W.load(sp, 0, 3, weight_cols(w_in, SBK + P))
                stacks(-1)
                W.load(sp, 0, 4, weight_cols(w_in, SBQ + P))

                def send_gate(half, use, row):
                    sp.wait_ge(g_free[half], use + 2)
                    sp.dma_start(gates_t[ds(row, P), half * HALF:(half + 1) * HALF], sq[:, half, :]
                                 ).then_inc(gs_out, 16)

                def send_o(it):
                    sp.wait_ge(o_free, 4 * it + 5)
                    sp.dma_start(osb_t[ds(it * P, P), :], ot[:]).then_inc(ot_out, 16)

                def body(it, k_next, q_next):
                    W.load(sp, units(it), 5, weight_cols(w_in, it * P + (SBV + P)))
                    W.load(sp, units(it), 6, weight_cols(w_in, it * P + GATE))
                    W.load(sp, units(it), 7, weight_cols(w_in, k_next))
                    stacks(it)
                    W.load(sp, units(it), 8, weight_cols(w_in, q_next))
                    send_gate(0, g_uses(it) + 6, it * P)
                    send_gate(1, g_uses(it) + 6, it * P)
                    send_o(it)

                last_gates = [GATE + (PAIRS - 1 + n) * P for n in range(LAST_GATES)]
                with sp.Fori(0, PAIRS - 2, 1) as it:
                    body(it, it * P + (SBK + 2 * P), it * P + (SBQ + 2 * P))
                body(PAIRS - 2, last_gates[0], last_gates[1])
                W.load(sp, units(PAIRS - 1), 5, weight_cols(w_in, last_gates[2]))
                for n in range(LAST_GATES):
                    for half in range(NH):
                        send_gate(half, g_uses(PAIRS - 1) + n, (PAIRS - 1 + n) * P)
                send_o(PAIRS - 1)
                sp.wait_ge(ot_out, 16 * (PAIRS + 1))
                sp.wait_ge(gs_out, 16 * (NH * (PAIRS - 1 + LAST_GATES) + 1))

            @block.gpsimd
            def _(pool):
                W.prime_pool(pool)
                W.split(pool, 0, 0)
                W.split(pool, 0, 1)
                W.split(pool, 0, 2, (g_done[1], 1))
                W.split(pool, 0, 3, (g_done[1], 3))
                for _ in range(2):
                    pool.sem_inc(row_ready, 1)

                def weights(it, n):
                    e, tb = SCORE_STEPS[n]
                    width = (tb + 1) * P
                    pool.wait_ge(scanned, NSC * it + n + 1)
                    pool.wait_ge(t_done, rows_used(it, e, tb))
                    nc.gpsimd.tensor_tensor(rows[tb // 4][:, tb % 4, 0:width], beta[:, n % 2, 0:width],
                                            rest[:, n % 2, 1:width + 1], ALU.mult).then_inc(row_ready, 1)

                def body(it, last):
                    splits = {0: (4, 0), 8: (5, 1), 19: (6, 3), 25: (7, 6)}
                    for s in range(SLOTS):
                        if s in splits and not (last and s > 8):
                            step, uses = splits[s]
                            W.split(pool, units(it), step, (g_done[1], g_uses(it) + uses))
                        if s - 1 in SCORE_SLOT:
                            weights(it, SCORE_SLOT.index(s - 1))
                rounds(pool, PAIRS, body)

            @block.tensor
            def _(pe):
                pe.sem_inc(av_done, 2)
                pe.sem_inc(t_done, NWT)

                def fill(it_units, step, eighth, use):
                    half, part = eighth // 4, eighth % 4
                    if eighth == 0:
                        W.take(pe, it_units, step)
                    if part == 0:
                        pe.wait_ge(g_free[half], use + 1)
                    ins = project_part(nc, G[half][:], W.tile(step), hT, half, part, 4)
                    if part == 3:
                        ins.then_inc(g_done[half], 1)

                def mean_squares(prep, x, half, use):
                    pe.wait_ge(sq_ready, 4 * prep + 2 * x + half + 1)
                    pe.wait_ge(g_free[half], use + 1)
                    for t in range(TT // 2):
                        ins = nc.tensor.matmul(G[half][:, 2 * t:2 * t + 2], sq[:, half, t * P:(t + 1) * P],
                                               c["head_mean"][:], start=True, stop=True)
                    ins.then_inc(g_done[half], 1)

                def spread_k_rs(prep, half, use):
                    pe.wait_ge(k_rs_ready, prep + 1)
                    pe.wait_ge(g_free[half], use + 1)
                    for t in range(TT // 2):
                        ins = nc.tensor.matmul(G[half][:, t * P:(t + 1) * P], k_rs[:, half * (TT // 2) + t, :],
                                               c["ident"][:], start=True, stop=True)
                    ins.then_inc(g_done[half], 1)

                def transpose_v(part, copied):
                    pe.wait_ge(g_free[part], copied)
                    for j in range(4 * part, 4 * part + 4):
                        ins = nc.tensor.transpose(Z[1][:, j * P:(j + 1) * P], vt[:, j * P:(j + 1) * P], c["ident"][:])
                    if part == 1:
                        ins.then_inc(vt_done, 1)

                for step in range(3):
                    for eighth in range(8):
                        fill(0, step, eighth, (0, 2, 5)[step])
                    if step < 2:
                        for half in range(NH):
                            mean_squares(0, step, half, 2 * step + 1)
                    if step == 1:
                        for half in range(NH):
                            spread_k_rs(0, half, 4)
                for part in range(2):
                    transpose_v(part, 7)

                def scores(it, n):
                    e, tb = SCORE_STEPS[n]
                    if n == 0:
                        pe.wait_ge(stacked, 16 * STACKS * (it + 1))
                    pe.wait_ge(z_free, NSC * it + n + 1)
                    if n == 1:
                        pe.wait_ge(v_ready, it + 1)
                    z, width = Z[n % 2], (tb + 1) * P
                    q = qs[e][:, tb * P:(tb + 1) * P]
                    for a in range(0, width, HALF):
                        b = min(a + HALF, (width + 255) // 256 * 256)
                        nc.tensor.matmul(z[:, a:b], q, kh[e][:, a:b], start=True, stop=False)
                        nc.tensor.matmul(z[:, a:b], q, kl[e][:, a:b], start=False, stop=(b < width))
                    nc.tensor.matmul(z[:, width - P:width], c["ident_b"][:], c["not_before"][:],
                                     start=False, stop=True).then_inc(z_done, 1)

                def transposes(it, m):
                    e, g, j = WEIGHT_STEPS[m]
                    first = max(j, 4 * g)
                    if j == 0:
                        pe.wait_ge(row_ready, 2 + NSC * it + 8 * e + 4 * g + 4)
                    pe.wait_ge(lo_ready, t_uses(it) + m + 1)
                    for tb in range(first, 4 * g + 4):
                        ins = nc.tensor.transpose(T[:, (tb - 4 * g) * P:(tb - 4 * g + 1) * P],
                                                  rows[g][:, tb - 4 * g, j * P:(j + 1) * P], c["ident"][:])
                    ins.then_inc(t_done, 1)

                def weigh(it, m):
                    e, g, j = WEIGHT_STEPS[m]
                    a = max(j - 4 * g, 0) * P
                    if j == 0:
                        pe.wait_ge(o_free, 4 * it + 2 * e + g + 1)
                    pe.wait_ge(lo_ready, t_uses(it) + m + 2)
                    o, hi, lo = O[0:SB_DH, a:HALF], wt_hi[:, m % 2, a:HALF], wt_lo[:, m % 2, a:HALF]
                    both = lambda: nc.tensor.matmul(O[:, a:HALF], v[:, j, e].rearrange("p x d -> p (x d)"), hi,
                                                    start=(j == 0), stop=(j == 4 * g + 3))
                    if j == 4 * g + 3:
                        nc.tensor.matmul(o, v[:, j, e, 0], lo, start=False, stop=False)
                        both().then_inc(av_done, 1)
                    else:
                        both()
                        nc.tensor.matmul(o, v[:, j, e, 0], lo, start=False, stop=False).then_inc(av_done, 1)

                def body(it, last):
                    fills = LAST_GATES if last else 4
                    for s in range(SLOTS):
                        m = s - WEIGHT_SLOT
                        if 0 <= m < NWT:
                            transposes(it, m)
                        if s in SCORE_SLOT:
                            scores(it, SCORE_SLOT.index(s))
                        if not last and s in MS_SLOT:
                            i = MS_SLOT.index(s)
                            mean_squares(it + 1, i // 2, i % 2, g_uses(it) + 2 * (i // 2) + 1)
                        if not last and s in SPREAD_SLOT:
                            spread_k_rs(it + 1, SPREAD_SLOT.index(s), g_uses(it) + 4)
                        u, eighth = slot_of_unit(s)
                        if u < fills:
                            fill(units(it), 3 + u, eighth, g_uses(it) + (u if last else (0, 2, 5, 6)[u]))
                        if 0 <= m - 1 < NWT:
                            weigh(it, m - 1)
                        if not last and s in V_SLOT:
                            if s == V_SLOT[0]:
                                pe.wait_ge(z_free, NSC * (it + 1) + 2)
                            transpose_v(V_SLOT.index(s), g_uses(it) + 7)
                rounds(pe, PAIRS, body)

            @block.scalar
            def _(act):
                for sem_ in (z_free, z_free):
                    act.sem_inc(sem_, 1)
                act.sem_inc(gs_out, 16)

                def square(half, use):
                    act.wait_ge(g_done[half], use + 1)
                    nc.scalar.activation(sq[:, half, :], G[half][:], ACT.Square).then_inc(sq_ready, 1)

                def high_q(prep, half):
                    need(act, stacked, 16 * STACKS * prep)
                    nc.scalar.copy(q_st[:, 0, half * HALF:(half + 1) * HALF], G[half][:]).then_inc(q_high, 1)

                def high_k(prep, half, use):
                    act.wait_ge(g_free[half], use + 2)
                    need(act, stacked, 16 * STACKS * prep)
                    at = slice(half * HALF, (half + 1) * HALF)
                    nc.scalar.copy(k_st[:, 0, at], k_new[:, at]).then_inc(k_high, 1)

                def copy_vt(half, use):
                    act.wait_ge(g_done[half], use + 1)
                    nc.scalar.copy(vt[:, half * HALF:(half + 1) * HALF], G[half][:]).then_inc(g_free[half], 1)

                def high_v(prep, first=False):
                    act.wait_ge(vt_done, prep + 1)
                    if not first:
                        act.wait_ge(av_done, NWT * prep + 2)
                    nc.scalar.copy(v[:, :, :, 0, :], Z[1][:].rearrange("p (j e d) -> p j e d", j=TT, e=2)
                                   ).then_inc(v_high, 1)

                def gate(n_done, half, use):
                    act.wait_ge(g_done[half], use + 1)
                    act.wait_ge(gs_out, 16 * (NH * n_done + 1))
                    nc.scalar.activation(sq[:, half, :], G[half][:], ACT.Sigmoid).then_inc(g_free[half], 1)

                for half in range(NH):
                    square(half, 0)
                for half in range(NH):
                    square(half, 2)
                    high_q(0, half)
                for half in range(NH):
                    high_k(0, half, 4)
                for half in range(NH):
                    copy_vt(half, 5)
                high_v(0, first=True)

                def sigmoids(it, n):
                    e, tb = SCORE_STEPS[n]
                    if n == 0:
                        act.wait_ge(q_scale_ready, it + 1)
                    act.wait_ge(z_done, NSC * it + n + 1)
                    act.wait_ge(row_ready, NSC * it + n + 1)
                    width = (tb + 1) * P
                    scale = [q_scale[:, x, 2 * tb + e:2 * tb + e + 1] for x in range(2)]
                    nc.scalar.activation(rest[:, n % 2, 0:width], Z[n % 2][:, 0:width], ACT.Sigmoid, scale=scale[0])
                    nc.scalar.activation(beta[:, n % 2, 0:width], Z[n % 2][:, 0:width], ACT.Sigmoid,
                                         scale=scale[1]).then_inc(z_free, 1)

                def wt_high(it, m):
                    e, g, j = WEIGHT_STEPS[m]
                    a = max(j - 4 * g, 0) * P
                    act.wait_ge(t_done, t_uses(it) + m + 1 + NWT)
                    act.wait_ge(av_done, NWT * it + m + 1)
                    nc.scalar.copy(wt_hi[:, m % 2, a:HALF], T[:, a:HALF]).then_inc(hi_ready, 1)

                def copy_o(it, e, g):
                    m = WEIGHT_STEPS.index((e, g, 4 * g + 3))
                    act.wait_ge(av_done, 2 + NWT * it + m + 1)
                    nc.scalar.copy(o_low[:], O[SB_DH:P, :]).then_inc(half_copied, 1)

                def body(it, last):
                    for s in range(SLOTS):
                        m = s - WEIGHT_SLOT
                        if 0 <= m < NWT:
                            wt_high(it, m)
                        if s in SCORE_SLOT:
                            sigmoids(it, SCORE_SLOT.index(s))
                        if not last:
                            if s in (4, 8):
                                if s == 4:
                                    act.wait_ge(gs_out, 16 * (NH * it + 1))
                                square(s // 4 - 1, g_uses(it))
                            if s in (12, 16):
                                square(s // 4 - 3, g_uses(it) + 2)
                                high_q(it + 1, s // 4 - 3)
                            if s in (15, 19):
                                high_k(it + 1, (s - 15) // 4, g_uses(it) + 4)
                            if s in (20, 24):
                                copy_vt((s - 20) // 4, g_uses(it) + 5)
                            if s == 28:
                                gate(it, 0, g_uses(it) + 6)
                        elif s in (4, 8, 12, 16, 20, 24):
                            i = (s - 4) // 4
                            gate(PAIRS - 1 + i // 2, i % 2, g_uses(it) + i // 2)
                        if 0 <= m - 1 < NWT and WEIGHT_STEPS[m - 1][2] == 4 * WEIGHT_STEPS[m - 1][1] + 3:
                            copy_o(it, *WEIGHT_STEPS[m - 1][:2])
                    if not last:
                        high_v(it + 1)
                        gate(it, 1, g_uses(it) + 6)
                rounds(act, PAIRS, body)

            @block.vector
            def _(dve):
                chain = Chain(dve, dve_step)
                for sem_ in (g_free[0], g_free[1], lo_ready, o_free):
                    dve.sem_inc(sem_, 1)
                dve.sem_inc(ot_out, 16)
                nc.vector.memset(rest[:], 1.0)
                dve.wait_ge(g_loaded, 64)
                nc.vector.tensor_tensor(gains[:, 0:1], gains[:, 0:1], gains[:, 1:2], ALU.mult).then_inc(gains_made, 1)
                dve.wait_ge(gains_made, 1)

                def copy_k(prep, half, use):
                    dve.wait_ge(sq_ready, 4 * prep + half + 1)
                    nc.vector.tensor_copy(k_new[:, half * HALF:(half + 1) * HALF], G[half][:]
                                          ).then_inc(g_free[half], 1)

                def low_q(prep, half):
                    dve.wait_ge(q_high, NH * prep + half + 1)
                    at = slice(half * HALF, (half + 1) * HALF)
                    nc.vector.tensor_tensor(q_st[:, 1, at], G[half][:], q_st[:, 0, at], ALU.subtract
                                            ).then_inc(g_free[half], 1)

                def copy_ms(x, half, use):
                    dve.wait_ge(g_done[half], use + 1)
                    nc.vector.tensor_scalar(ms[:, x, TT * half:TT * (half + 1)], G[half][:, 0:TT], EPS, None,
                                            ALU.add).then_inc(g_free[half], 1)

                def k_root(prep, use, part):
                    if part == 0:
                        chain.enter(SB_CHAIN * prep)
                        for half in range(NH):
                            dve.wait_ge(g_free[half], use + 2)
                        rsqrt_guess(nc, chain, ms[:, 0, :], rms[:, 0, :])
                    rsqrt_newton(nc, chain, ms[:, 0, :], rms[:, 0, :], tmp[:])

                def repeat_k_rs():
                    nc.vector.tensor_copy(k_rs[:].rearrange("p t (e d) -> p (t e) d", e=2),
                                          rms[:, 0, :, None].to_broadcast([P, TT * 2, SB_DH])).then_inc(k_rs_ready, 1)

                def q_root(use):
                    for half in range(NH):
                        dve.wait_ge(g_free[half], use + 2)
                    rsqrt(nc, chain, ms[:, 1, :], rms[:, 1, :], tmp[:])
                    for x in range(2):
                        ins = nc.vector.tensor_scalar(q_scale[:, x, :], rms[:, 1, :], (-1, 1)[x] * SB_DH ** -0.5,
                                                      None, ALU.mult)
                    ins.then_inc(q_scale_ready, 1)
                    assert chain.n == SB_CHAIN

                def scale_k(half, use):
                    dve.wait_ge(g_done[half], use + 1)
                    at = slice(half * HALF, (half + 1) * HALF)
                    nc.vector.scalar_tensor_tensor(k_new[:, at], k_new[:, at], gains[:, 0:1], G[half][:],
                                                   ALU.mult, ALU.mult).then_inc(g_free[half], 1)

                def low_k(prep, half):
                    dve.wait_ge(k_high, NH * prep + half + 1)
                    at = slice(half * HALF, (half + 1) * HALF)
                    nc.vector.tensor_tensor(k_st[:, 1, at], k_new[:, at], k_st[:, 0, at], ALU.subtract
                                            ).then_inc(split_done, 1)

                def sum_o(it, e, g):
                    dve.wait_ge(half_copied, 4 * it + 2 * e + g + 1)
                    if e == 0 and g == 0:
                        dve.wait_ge(ot_out, 16 * (it + 1))
                    nc.vector.tensor_tensor(ot[e * SB_DH:(e + 1) * SB_DH, g * HALF:(g + 1) * HALF],
                                            O[0:SB_DH, :], o_low[:], ALU.add).then_inc(o_free, 1)

                def low_v(prep):
                    dve.wait_ge(v_high, prep + 1)
                    nc.vector.tensor_tensor(v[:, :, :, 1, :], Z[1][:].rearrange("p (j e d) -> p j e d", j=TT, e=2),
                                            v[:, :, :, 0, :], ALU.subtract).then_inc(v_ready, 1)

                for half in range(NH):
                    copy_k(0, half, 0)
                for half in range(NH):
                    copy_ms(0, half, 1)
                for part in range(3):
                    k_root(0, 1, part)
                repeat_k_rs()
                for half in range(NH):
                    low_q(0, half)
                for half in range(NH):
                    copy_ms(1, half, 3)
                for half in range(NH):
                    scale_k(half, 4)
                for half in range(NH):
                    low_k(0, half)
                q_root(3)
                low_v(0)

                def row(it, n):
                    e, tb = SCORE_STEPS[n]
                    width, b = (tb + 1) * P, n % 2
                    dve.wait_ge(z_free, 2 + NSC * it + n + 1)
                    back = rest[:, b, width - 1::-1] if width == S + 1 else rest[:, b, 0:width][:, ::-1]
                    nc.vector.tensor_tensor_scan(back, back, back, 1.0, ALU.mult, ALU.bypass).then_inc(scanned, 1)

                def wt_low(it, m):
                    e, g, j = WEIGHT_STEPS[m]
                    a = max(j - 4 * g, 0) * P
                    dve.wait_ge(hi_ready, t_uses(it) + m + 1)
                    nc.vector.tensor_tensor(wt_lo[:, m % 2, a:HALF], T[:, a:HALF], wt_hi[:, m % 2, a:HALF],
                                            ALU.subtract).then_inc(lo_ready, 1)

                def body(it, last):
                    for s in range(SLOTS):
                        m = s - WEIGHT_SLOT
                        if 0 <= m < NWT:
                            wt_low(it, m)
                        if s - 1 in SCORE_SLOT:
                            row(it, SCORE_SLOT.index(s - 1))
                        if not last:
                            if s in (4, 8):
                                copy_k(it + 1, s // 4 - 1, g_uses(it))
                            if s in (12, 16):
                                low_q(it + 1, s // 4 - 3)
                            if s in MS_SLOT:
                                i = MS_SLOT.index(s)
                                copy_ms(i // 2, i % 2, g_uses(it) + 2 * (i // 2) + 1)
                            if s in (10, 11, 12):
                                k_root(it + 1, g_uses(it) + 1, s - 10)
                            if s == 13:
                                repeat_k_rs()
                            if s in SPREAD_SLOT:
                                scale_k(SPREAD_SLOT.index(s), g_uses(it) + 4)
                            if s in (15, 19):
                                low_k(it + 1, (s - 15) // 4)
                            if s == 29:
                                q_root(g_uses(it) + 3)
                        if 0 <= m - 1 < NWT and WEIGHT_STEPS[m - 1][2] == 4 * WEIGHT_STEPS[m - 1][1] + 3:
                            sum_o(it, *WEIGHT_STEPS[m - 1][:2])
                    if not last:
                        low_v(it + 1)
                rounds(dve, PAIRS, body)


GLA_SLOTS = 48
CHUNKS = S // P
LEVELS = 8
GLA_UNITS = 6
GLA_TASKS = 9
GLA_T = CHUNKS + 8
GLA_CHAIN = 13
N_MADE = 3 + 3 * (LEVELS - 1) + 1


def linear_attention(nc, c, hT, w_in, w2, gate_b, out_gain, ogla_t, gates_t):
    with ExitStack() as ctx:
        sb = lambda n, shape, dt=F32: ctx.enter_context(nc.sbuf_tensor(f"gla_{n}", shape, dt))
        ps = lambda n, shape: ctx.enter_context(nc.psum_tensor(f"gla_{n}", shape, F32))
        sem = lambda n: ctx.enter_context(nc.semaphore(f"gla_{n}"))
        W = Weights(nc, ctx, "glaw", 2)
        lr_raw, lr_hi, lr_lo = sb("lr_raw", [P, KT, LR]), sb("lr_hi", [P, KT, LR], F32R), sb("lr_lo", [P, KT, LR], F32R)
        lr_t = sb("lr_t", [LR, S])
        w2_all, w2_h = sb("w2_all", [LR, GLA_HEADS * GLA_DK]), sb("w2_h", [LR, GLA_DK])
        gb_all, gb_h = sb("gb_all", [P, GLA_HEADS]), sb("gb_h", [P, 1])
        og = sb("og", [P, 2])
        mask = sb("mask", [P, LEVELS, P])
        keep = sb("keep", [P, S], BF16)
        q_new, k_new = sb("q_new", [P, S]), sb("k_new", [P, S])
        q_diag, k_diag = sb("q_diag", [P, S]), sb("k_diag", [P, S])
        X = sb("x", [P, LEVELS - 1, S])
        q_in, k_out = sb("q_in", [P, S]), sb("k_out", [P, S])
        C = sb("c", [P, S])
        E = sb("e", [P, 2, S])
        dec = sb("dec", [P, CHUNKS])
        vt = sb("vt", [P, 2, S])
        V = sb("v", [P, CHUNKS, GLA_DV])
        RT = sb("rt", [P, 2, S])
        masked = E[:, 0, :].rearrange("p (l i) -> p l i", l=LEVELS)
        sc = sb("sc", [P, 2, P])
        kt = sb("kt", [P, 2, P])
        state = sb("state", [P, GLA_DV])
        obuf = sb("obuf", [P, CHUNKS, GLA_DV])
        junk = E[:, 1, 0:GLA_DV]
        ssq, stat = sb("ssq", [P, CHUNKS]), sb("stat", [P, 3, CHUNKS])
        gst = sb("gst", [P, HALF])
        G = [ps(f"g{h}", [P, HALF]) for h in range(NH)]
        SC = ps("s", [P, LEVELS, P])
        O = [ps(f"o{b}", [P, HALF]) for b in range(2)]
        ST = ps("st", [P, HALF])
        T = ps("t", [P, HALF])

        small_loaded = sem("small_loaded")
        made = sem("made")
        lr_split = sem("lr_split")
        g_done = [sem(f"g_done{h}") for h in range(NH)]
        g_free = [sem(f"g_free{h}") for h in range(NH)]
        r_sig = sem("r_sig")
        w2_ready = sem("w2_ready")
        s_done, s_free = sem("s_done"), sem("s_free")
        abs_ready, log_ready = sem("abs_ready"), sem("log_ready")
        d_ready, e_ready = sem("d_ready"), sem("e_ready")
        f_ready = sem("f_ready")
        sc_ready = sem("sc_ready")
        t_done, t_free = sem("t_done"), sem("t_free")
        o_done, o_free = sem("o_done"), sem("o_free")
        ssq_ready = sem("ssq_ready")
        st_done, st_free = sem("st_done"), sem("st_free")
        on_ready = sem("on_ready")
        gst_out = sem("gst_out")
        gate_out = [sem(f"gate_out{h}") for h in range(NH)]
        dve_step = sem("dve_step")

        g_uses = lambda it: 7 + GLA_UNITS * it
        t_uses = lambda it: 4 + GLA_T * it
        s_uses = lambda it: 1 + (CHUNKS + 1) * it
        N_LAST_GATES = 6

        def blocks(t, half):
            return t.rearrange("p (b a h) -> p b a h", a=2, h=half)

        with nc.Block() as block:
            @block.sync
            def _(sp):
                sp.dma_start(lr_raw[:], w_in.rearrange("(k p) c -> p k c", p=P)[:, :, GLLR:GLLR + LR]
                             ).then_inc(small_loaded, 16)
                sp.dma_start(w2_all[:], w2).then_inc(small_loaded, 16)
                for dst, src in ((gb_all, gate_b), (og, out_gain)):
                    for n in range(dst.shape[1]):
                        sp.dma_start(dst[:, n:n + 1], src[:, n * P:(n + 1) * P].rearrange("a p -> p a")
                                     ).then_inc(small_loaded, 16)

                cols = [(GLQ, GLA_DK), (GLK, GLA_DK), (GLV, GLA_DV), (GLV + P, GLA_DV), (GLR, GLA_DV), (GLR + P, GLA_DV)]
                for n, (col, _) in enumerate(cols):
                    W.load(sp, 0, n, weight_cols(w_in, col))

                def body(it, last):
                    for n, (col, width) in enumerate(cols):
                        src = GATE + (10 + n) * P if last else it * width + (col + width)
                        W.load(sp, GLA_UNITS * it, GLA_UNITS + n, weight_cols(w_in, src))
                rounds(sp, GLA_HEADS, body)
                sp.wait_ge(gst_out, 16 * (4 * GLA_HEADS + 1))
                for half in range(NH):
                    sp.wait_ge(gate_out[half], 16 * N_LAST_GATES)

            @block.gpsimd
            def _(pool):
                W.prime_pool(pool)
                W.split(pool, 0, 0)
                W.split(pool, 0, 1)
                chain = Chain(pool, made)
                chain.link(nc.gpsimd.memset(mask[:], 0.0))
                chain.link(nc.gpsimd.memset(keep[:], 1.0))
                chain.link(nc.gpsimd.memset(keep[:].rearrange("p (c t) -> p c t", t=P)[:, :, 0:1], 0.0))
                for lv in range(LEVELS - 1):
                    half = 1 << lv
                    second = blocks(mask[:, lv, :], half)[:, :, 1, :]
                    chain.link(nc.gpsimd.memset(second, 1.0))
                    pattern = lambda sign: [[sign * 2 * half, P // (2 * half)], [0, half]]
                    chain.link(nc.gpsimd.affine_select(out=second, in_=second, compare_op=ALU.is_ge, fill=0.0,
                                                       base=0, pattern=pattern(-1), channel_multiplier=1))
                    chain.link(nc.gpsimd.affine_select(out=second, in_=second, compare_op=ALU.is_ge, fill=0.0,
                                                       base=half - 1, pattern=pattern(1), channel_multiplier=-1))
                diag = mask[:, LEVELS - 1, :]
                chain.link(nc.gpsimd.affine_select(out=diag, in_=diag, compare_op=ALU.not_equal, fill=1.0,
                                                   base=0, pattern=[[-1, P]], channel_multiplier=1))
                assert chain.n == N_MADE
                for n in range(2, GLA_UNITS):
                    W.split(pool, 0, n, (g_done[1], n))

                def body(it, last):
                    for n in range(GLA_UNITS):
                        W.split(pool, GLA_UNITS * it, GLA_UNITS + n, (g_done[1], GLA_UNITS * it + (GLA_UNITS + n)))
                rounds(pool, GLA_HEADS, body)

            @block.tensor
            def _(pe):
                def fill(lot, step, eighth, use):
                    half, part = eighth // 4, eighth % 4
                    if eighth == 0:
                        W.take(pe, lot, step)
                    if part == 0:
                        pe.wait_ge(g_free[half], use + 1)
                    ins = project_part(nc, G[half][:], W.tile(step), hT, half, part, 4)
                    if part == 3:
                        ins.then_inc(g_done[half], 1)

                def transpose_v(n, use):
                    d, cg = n // 2, n % 2
                    pe.wait_ge(t_free, use)
                    for q in range(4):
                        j = 4 * cg + q
                        ins = nc.tensor.transpose(T[:, q * P:(q + 1) * P], vt[:, d, j * P:(j + 1) * P], c["ident"][:])
                    ins.then_inc(t_done, 1)

                def logits(prep, use):
                    pe.wait_ge(w2_ready, prep + 1)
                    pe.wait_ge(s_free, use + 1)
                    flat = SC[:].rearrange("p l i -> p (l i)")
                    for half in range(NH):
                        at = slice(half * HALF, (half + 1) * HALF)
                        ins = nc.tensor.matmul(flat[:, at], w2_h[:], lr_t[:, at], start=True, stop=True)
                    ins.then_inc(s_done, 1)

                pe.wait_ge(lr_split, 2)
                for half in range(NH):
                    pe.wait_ge(g_free[half], 1)
                    steps = [(a, b, k) for a, b in ((lr_hi, hT[0]), (lr_hi, hT[1]), (lr_lo, hT[0])) for k in range(KT)]
                    for n, (a, b, k) in enumerate(steps):
                        ins = nc.tensor.matmul(G[half][0:LR, :], a[:, k, :], b[:, k, half * HALF:(half + 1) * HALF],
                                               start=(n == 0), stop=(n == len(steps) - 1))
                    ins.then_inc(g_done[half], 1)
                for n in range(GLA_UNITS):
                    for eighth in range(8):
                        fill(0, n, eighth, 1 + n)
                    if n == 1:
                        for half in range(NH):
                            pe.wait_ge(g_free[half], 2)
                        logits(0, 0)
                    if n == 4:
                        for half in range(NH):
                            pe.wait_ge(g_free[half], 6)
                        for m in range(4):
                            if m:
                                transpose_v(m, m)
                            else:
                                for q in range(4):
                                    ins = nc.tensor.transpose(T[:, q * P:(q + 1) * P], vt[:, 0, q * P:(q + 1) * P],
                                                              c["ident"][:])
                                ins.then_inc(t_done, 1)

                def scores(it, ch):
                    if ch == 0:
                        pe.wait_ge(f_ready, GLA_TASKS * (it + 1))
                    at = slice(ch * P, (ch + 1) * P)
                    pe.wait_ge(t_free, t_uses(it) + ch)
                    nc.tensor.transpose(T[:, 0:P], k_out[:, at], c["ident"][:]).then_inc(t_done, 1)
                    pe.wait_ge(s_free, s_uses(it) + ch + 1)
                    for lv in range(LEVELS - 1):
                        nc.tensor.matmul(SC[:, lv, :], X[:, lv, at], X[:, lv, at], start=True, stop=True)
                    nc.tensor.matmul(SC[:, LEVELS - 1, :], k_diag[:, at], q_diag[:, at],
                                     start=True, stop=True).then_inc(s_done, 1)

                def outputs(it, ch):
                    at, o = slice(ch * P, (ch + 1) * P), O[ch % 2][:, 0:GLA_DV]
                    pe.wait_ge(o_free, CHUNKS * it + ch + 1)
                    if ch:
                        pe.wait_ge(st_free, (CHUNKS - 1) * it + ch + 1)
                        nc.tensor.matmul(o, q_in[:, at], state[:], start=True, stop=False)
                    pe.wait_ge(sc_ready, CHUNKS * it + ch + 1)
                    nc.tensor.matmul(o, sc[:, ch % 2, :], V[:, ch, :], start=(ch == 0), stop=True).then_inc(o_done, 1)
                    if ch < CHUNKS - 1:
                        pe.wait_ge(t_free, t_uses(it) + ch + 1)
                        pe.wait_ge(st_free, (CHUNKS - 1) * it + ch + 1)
                        nc.tensor.matmul(ST[:, 0:GLA_DV], kt[:, ch % 2, :], V[:, ch, :],
                                         start=True, stop=True).then_inc(st_done, 1)

                def transpose_o(it, n):
                    d, cg = n // 2, n % 2
                    if n == 0:
                        pe.wait_ge(on_ready, it + 1)
                    pe.wait_ge(t_free, t_uses(it) + CHUNKS + n)
                    for q in range(4):
                        ins = nc.tensor.transpose(T[:, q * P:(q + 1) * P], obuf[:, 4 * cg + q, d * P:(d + 1) * P],
                                                  c["ident"][:])
                    ins.then_inc(t_done, 1)

                def body(it, last):
                    for s in range(GLA_SLOTS):
                        if s < 3 * CHUNKS and s % 3 == 0:
                            scores(it, s // 3)
                        if s < 3 * CHUNKS and s % 3 == 2:
                            outputs(it, s // 3)
                        if s in (27, 28, 29, 30):
                            transpose_o(it, s - 27)
                        if not last:
                            if s == 25:
                                logits(it + 1, s_uses(it) + CHUNKS)
                            if s in (33, 34, 35, 36):
                                if s == 33:
                                    for half in range(NH):
                                        pe.wait_ge(g_free[half], g_uses(it) + 5)
                                transpose_v(s - 33, t_uses(it) + CHUNKS + 4 + s - 33)
                        fill(GLA_UNITS * it, GLA_UNITS + s // 8, s % 8, g_uses(it) + s // 8)
                rounds(pe, GLA_HEADS, body)

            @block.scalar
            def _(act):
                for sem_ in (o_free, o_free, ssq_ready):
                    act.sem_inc(sem_, 1)

                def copy_vt(d, half, use):
                    act.wait_ge(g_done[half], use + 1)
                    nc.scalar.copy(vt[:, d, half * HALF:(half + 1) * HALF], G[half][:]).then_inc(g_free[half], 1)

                def sigmoid_r(d, half, use):
                    act.wait_ge(g_done[half], use + 1)
                    nc.scalar.activation(RT[:, d, half * HALF:(half + 1) * HALF], G[half][:],
                                         ACT.Sigmoid).then_inc(r_sig, 1)

                def copy_v(n, use):
                    d, cg = n // 2, n % 2
                    act.wait_ge(t_done, use + 1)
                    nc.scalar.copy(V[:, 4 * cg:4 * cg + 4, d * P:(d + 1) * P],
                                   T[:].rearrange("p (j n) -> p j n", j=4)).then_inc(t_free, 1)

                def log_sigmoid(prep, use):
                    act.wait_ge(s_done, use + 1)
                    e, flat = E[:, 0, :], SC[:].rearrange("p l i -> p (l i)")
                    nc.scalar.activation(e, flat, ACT.Abs, bias=gb_h[:]).then_inc(abs_ready, 1)
                    act.wait_ge(abs_ready, 2 * prep + 1)
                    nc.scalar.activation(e, e, ACT.Exp, scale=-1.0).then_inc(abs_ready, 1)
                    act.wait_ge(abs_ready, 2 * prep + 2)
                    nc.scalar.activation(e, e, ACT.Ln, bias=1.0).then_inc(log_ready, 1)

                def exponential(prep, task):
                    act.wait_ge(d_ready, GLA_TASKS * prep + task + 1)
                    e = E[:, task % 2, :]
                    if task == 0:
                        nc.scalar.activation(dec[:], C[:].rearrange("p (c t) -> p c t", t=P)[:, :, P - 1],
                                             ACT.Exp, scale=1.0 / TAU)
                    nc.scalar.activation(e, C[:] if task == 0 else e, ACT.Exp,
                                         scale=1.0 / TAU).then_inc(e_ready, 1)

                for half in range(NH):
                    act.wait_ge(g_done[half], 1)
                    nc.scalar.copy(lr_t[:, half * HALF:(half + 1) * HALF], G[half][0:LR, :]).then_inc(g_free[half], 1)
                log_sigmoid(0, 0)
                for task in range(GLA_TASKS):
                    exponential(0, task)
                for d in range(2):
                    for half in range(NH):
                        copy_vt(d, half, 3 + d)
                for n in range(4):
                    if n == 2:
                        for half in range(NH):
                            sigmoid_r(0, half, 5)
                    copy_v(n, n)
                for half in range(NH):
                    sigmoid_r(1, half, 6)

                def copy_kt(it, ch):
                    act.wait_ge(t_done, t_uses(it) + ch + 1)
                    nc.scalar.copy(kt[:, ch % 2, :], T[:, 0:P]).then_inc(t_free, 1)

                def copy_o(it, ch):
                    act.wait_ge(o_done, CHUNKS * it + ch + 1)
                    nc.scalar.copy(obuf[:, ch, :], O[ch % 2][:, 0:GLA_DV]).then_inc(o_free, 1)
                    act.wait_ge(o_free, CHUNKS * it + ch + 3)
                    act.wait_ge(ssq_ready, CHUNKS * it + ch + 1)
                    nc.scalar.activation(junk, obuf[:, ch, :], ACT.Square,
                                         accum_out=ssq[:, ch:ch + 1]).then_inc(ssq_ready, 1)

                def send_gate(n, half, use):
                    at = slice(half * HALF, (half + 1) * HALF)
                    act.wait_ge(g_done[half], use + 1)
                    need(act, gate_out[half], 16 * n)
                    nc.scalar.activation(q_new[:, at], G[half][:], ACT.Sigmoid).then_inc(g_free[half], 1)
                    act.wait_ge(g_free[half], use + 2)
                    act.dma_start(gates_t[(10 + n) * P:(11 + n) * P, at], q_new[:, at]).then_inc(gate_out[half], 16)

                def send_o(it, n):
                    d, cg = n // 2, n % 2
                    act.wait_ge(t_free, t_uses(it) + CHUNKS + n + 1)
                    act.dma_start(ogla_t[ds(it * GLA_DV + d * P, P), cg * HALF:(cg + 1) * HALF],
                                  gst[:]).then_inc(gst_out, 16)

                def body(it, last):
                    for s in range(GLA_SLOTS):
                        if s < 3 * CHUNKS and s % 3 == 0:
                            copy_kt(it, s // 3)
                        if 3 <= s <= 3 * CHUNKS and s % 3 == 0:
                            copy_o(it, s // 3 - 1)
                        if s in (28, 29, 30, 31):
                            send_o(it, s - 28)
                        if not last:
                            if s in (20, 24, 28, 32):
                                i = (s - 20) // 4
                                copy_vt(i // 2, i % 2, g_uses(it) + 2 + i // 2)
                            if s == 26:
                                log_sigmoid(it + 1, s_uses(it) + CHUNKS)
                            if s in (33, 34, 35, 36):
                                copy_v(s - 33, t_uses(it) + CHUNKS + 4 + s - 33)
                            if s in (31, 32, 34, 37, 38, 39, 41, 42, 43):
                                exponential(it + 1, (31, 32, 34, 37, 38, 39, 41, 42, 43).index(s))
                            if s in (36, 40, 44):
                                i = (s - 36) // 4
                                sigmoid_r(i // 2, i % 2, g_uses(it) + 4 + i // 2)
                        elif s >= 4 and s % 4 == 0:
                            i = s // 4 - 1
                            send_gate(i // 2, i % 2, g_uses(it) + i // 2)
                    if last:
                        send_gate(N_LAST_GATES - 1, 1, g_uses(it) + N_LAST_GATES - 1)
                    else:
                        sigmoid_r(1, 1, g_uses(it) + 5)
                rounds(act, GLA_HEADS, body)

            @block.vector
            def _(dve):
                chain = Chain(dve, dve_step)
                for sem_ in (g_free[0], g_free[1], s_free, st_free):
                    dve.sem_inc(sem_, 1)
                dve.sem_inc(gst_out, 16)
                dve.wait_ge(small_loaded, 16 * (2 + GLA_HEADS + 2))
                nc.vector.tensor_copy(lr_hi[:], lr_raw[:]).then_inc(lr_split, 1)
                dve.wait_ge(lr_split, 1)
                nc.vector.tensor_tensor(lr_lo[:], lr_raw[:], lr_hi[:], ALU.subtract).then_inc(lr_split, 1)
                dve.wait_ge(made, N_MADE)

                def copy_q(half, use):
                    dve.wait_ge(g_done[half], use + 1)
                    nc.vector.tensor_scalar(q_new[:, half * HALF:(half + 1) * HALF], G[half][:], GLA_DK ** -0.5,
                                            None, ALU.mult).then_inc(g_free[half], 1)

                def copy_k(half, use):
                    dve.wait_ge(g_done[half], use + 1)
                    nc.vector.tensor_copy(k_new[:, half * HALF:(half + 1) * HALF], G[half][:]
                                          ).then_inc(g_free[half], 1)

                def head_gate(prep):
                    nc.vector.tensor_copy(w2_h[:], w2_all[:, ds(prep * GLA_DK, GLA_DK)])
                    nc.vector.tensor_copy(gb_h[:], gb_all[:, ds(prep, 1)]).then_inc(w2_ready, 1)

                def cumulate(prep, use):
                    dve.wait_ge(s_done, use + 1)
                    dve.wait_ge(abs_ready, 2 * prep + 1)
                    dve.wait_ge(w2_ready, prep + 1)
                    flat = SC[:].rearrange("p l i -> p (l i)")
                    e0, e1 = E[:, 0, :], E[:, 1, :]
                    nc.vector.tensor_scalar(e1, flat, gb_h[:], 0.0, ALU.add, ALU.min).then_inc(s_free, 1)
                    dve.wait_ge(log_ready, prep + 1)
                    dve.wait_ge(s_free, use + 2)
                    chain.link(nc.vector.tensor_tensor(e1, e1, e0, ALU.subtract))
                    nc.vector.tensor_tensor_scan(C[:], keep[:], e1, 0.0, ALU.mult, ALU.add).then_inc(d_ready, 1)
                    dve.wait_ge(d_ready, GLA_TASKS * prep + 1)

                def exponents(prep, task):
                    e = E[:, task % 2, :]
                    if task >= 2:
                        dve.wait_ge(f_ready, GLA_TASKS * prep + task - 1)
                    if task == 1:
                        view = lambda t: t.rearrange("p (c t) -> p c t", t=P)
                        nc.vector.tensor_tensor(view(e), view(C[:])[:, :, P - 1:P].to_broadcast([P, CHUNKS, P]),
                                                view(C[:]), ALU.subtract).then_inc(d_ready, 1)
                        return
                    half = 1 << (task - 2)
                    cb, eb = blocks(C[:], half), blocks(e, half)
                    mid = cb[:, :, 0, half - 1:half].to_broadcast([P, S // (2 * half), half])
                    nc.vector.tensor_tensor(eb[:, :, 0, :], mid, cb[:, :, 0, :], ALU.subtract)
                    nc.vector.tensor_tensor(eb[:, :, 1, :], cb[:, :, 1, :], mid, ALU.subtract).then_inc(d_ready, 1)

                def factors(prep, task):
                    dve.wait_ge(e_ready, GLA_TASKS * prep + task + 1)
                    e = E[:, task % 2, :]
                    if task == 0:
                        ins = nc.vector.tensor_tensor(q_in[:], q_new[:], e, ALU.mult)
                    elif task == 1:
                        ins = nc.vector.tensor_tensor(k_out[:], k_new[:], e, ALU.mult)
                    else:
                        half = 1 << (task - 2)
                        eb, xb = blocks(e, half), blocks(X[:, task - 2, :], half)
                        nc.vector.tensor_tensor(xb[:, :, 0, :], eb[:, :, 0, :], blocks(k_new[:], half)[:, :, 0, :], ALU.mult)
                        ins = nc.vector.tensor_tensor(xb[:, :, 1, :], eb[:, :, 1, :], blocks(q_new[:], half)[:, :, 1, :],
                                                      ALU.mult)
                    ins.then_inc(f_ready, 1)

                def diagonal():
                    nc.vector.tensor_copy(q_diag[:], q_new[:])
                    nc.vector.tensor_copy(k_diag[:], k_new[:])

                def gate_r(d, half, use, count):
                    dve.wait_ge(r_sig, count + 1)
                    r = RT[:, d, half * HALF:(half + 1) * HALF]
                    nc.vector.scalar_tensor_tensor(r, G[half][:], og[:, d:d + 1], r, ALU.mult,
                                                   ALU.mult).then_inc(g_free[half], 1)

                head_gate(0)
                for half in range(NH):
                    copy_q(half, 1)
                for half in range(NH):
                    copy_k(half, 2)
                chain.enter(0)
                cumulate(0, 0)
                diagonal()
                for task in range(GLA_TASKS):
                    if task + 1 < GLA_TASKS:
                        exponents(0, task + 1)
                    factors(0, task)
                for d in range(2):
                    for half in range(NH):
                        gate_r(d, half, 5 + d, 2 * d + half)
                first = chain.n

                def mask_scores(it, ch):
                    dve.wait_ge(s_done, s_uses(it) + ch + 1)
                    nc.vector.tensor_tensor(masked, SC[:], mask[:], ALU.mult).then_inc(s_free, 1)
                    dve.wait_ge(s_free, s_uses(it) + ch + 2)
                    nc.vector.tensor_reduce(sc[:, ch % 2, :], masked.rearrange("p l i -> p i l"), AX_X,
                                            ALU.add).then_inc(sc_ready, 1)

                def update(it, ch):
                    dve.wait_ge(st_done, (CHUNKS - 1) * it + ch + 1)
                    if ch == 0:
                        ins = nc.vector.tensor_copy(state[:], ST[:, 0:GLA_DV])
                    else:
                        dve.wait_ge(st_free, (CHUNKS - 1) * it + ch + 1)
                        ins = nc.vector.scalar_tensor_tensor(state[:], state[:], dec[:, ch:ch + 1], ST[:, 0:GLA_DV],
                                                             ALU.mult, ALU.add)
                    ins.then_inc(st_free, 1)

                def normalise(it):
                    dve.wait_ge(ssq_ready, CHUNKS * (it + 1) + 1)
                    ms, y, u = stat[:, 0, :], stat[:, 1, :], stat[:, 2, :]
                    chain.link(nc.vector.tensor_scalar(ms, ssq[:], 1.0 / GLA_DV, EPS, ALU.mult, ALU.add))
                    rsqrt(nc, chain, ms, y, u)
                    for ch in range(CHUNKS):
                        ins = nc.vector.tensor_scalar(obuf[:, ch, :], obuf[:, ch, :], y[:, ch:ch + 1], None, ALU.mult)
                    ins.then_inc(on_ready, 1)

                def gate_o(it, n):
                    d, cg = n // 2, n % 2
                    dve.wait_ge(t_done, t_uses(it) + CHUNKS + n + 1)
                    dve.wait_ge(gst_out, 16 * (4 * it + n + 1))
                    nc.vector.tensor_tensor(gst[:], T[:], RT[:, d, cg * HALF:(cg + 1) * HALF], ALU.mult
                                            ).then_inc(t_free, 1)

                def body(it, last):
                    chain.enter(GLA_CHAIN * it + first)
                    for s in range(GLA_SLOTS):
                        if s < 3 * (CHUNKS - 1) + 1 and s % 3 == 0 and s:
                            update(it, s // 3 - 1)
                        if s < 3 * CHUNKS and s % 3 == 0:
                            mask_scores(it, s // 3)
                        if s == 25:
                            normalise(it)
                        if s in (27, 28, 29, 30):
                            gate_o(it, s - 27)
                        if not last:
                            if s in (4, 8):
                                copy_q(s // 4 - 1, g_uses(it))
                            if s in (12, 16):
                                copy_k(s // 4 - 3, g_uses(it) + 1)
                            if s == 24:
                                head_gate(it + 1)
                            if s == 31:
                                cumulate(it + 1, s_uses(it) + CHUNKS)
                                exponents(it + 1, 1)
                                diagonal()
                            if s == 32:
                                factors(it + 1, 0)
                                exponents(it + 1, 2)
                            if s in (34, 37, 38, 39, 41, 42, 43):
                                task = (34, 37, 38, 39, 41, 42, 43).index(s) + 1
                                factors(it + 1, task)
                                if task + 2 < GLA_TASKS:
                                    exponents(it + 1, task + 2)
                            if s in (36, 40, 44):
                                i = (s - 36) // 4
                                gate_r(i // 2, i % 2, g_uses(it) + 4 + i // 2, 4 * it + 4 + i)
                    if not last:
                        factors(it + 1, GLA_TASKS - 1)
                        gate_r(1, 1, g_uses(it) + 5, 4 * it + 7)
                        assert chain.n == GLA_CHAIN, chain.n
                rounds(dve, GLA_HEADS, body)


def merge_and_project(nc, o_t, gates_t, weights, w_out, x, y):
    OUTS = TT * NH
    ROUND = 2 * NH + OUTS
    with ExitStack() as ctx:
        sb = lambda n, shape, dt=F32: ctx.enter_context(nc.sbuf_tensor(f"mp_{n}", shape, dt))
        sem = lambda n: ctx.enter_context(nc.semaphore(f"mp_{n}"))
        W = Weights(nc, ctx, "mpw", 2)
        parts = [[sb(f"o{b}_{part}", [P, KT, S], F32R) for part in ("hi", "lo")] for b in range(2)]
        sig = sb("sig", [P, 2, S])
        merged = sb("merged", [P, S])
        m_hi, m_lo = sb("m_hi", [P, S], F32R), sb("m_lo", [P, S], F32R)
        ps = lambda n: ctx.enter_context(nc.psum_tensor(f"mp_{n}", [P, HALF], F32))
        acc = [[ps(f"acc{b}{h}") for h in range(NH)] for b in range(2)]
        outs = [ps(f"out{i}") for i in range(4)]
        o_loaded = [sem(f"o_loaded{i}") for i in range(TT)]
        hi_done, lo_done = sem("hi_done"), sem("lo_done")
        x_loaded = sem("x_loaded")
        sig_loaded = [sem(f"sig_loaded{b}") for b in range(2)]
        pe_done = sem("pe_done")
        acc_free = sem("acc_free")
        m_ready = sem("m_ready")
        m_high, m_split = sem("m_high"), sem("m_split")
        out_free = sem("out_free")
        base = lambda j: 2 * NH + ROUND * j
        row_tiles = [(b, k) for b in range(2) for k in range(KT)]

        def steps(eng, prologue, step):
            prologue()
            with eng.Fori(0, (KT - 1) // 2, 1) as i:
                for u in range(2):
                    step(i, u, False)
            step((KT - 1) // 2, 0, False)
            step((KT - 1) // 2, 1, True)

        with nc.Block() as block:
            @block.sync
            def _(sp):
                def load_sig(b, row):
                    sp.dma_start(sig[:, b, :], gates_t[ds(row + b * D, P), :]).then_inc(sig_loaded[b], 16)

                def prologue():
                    for b in range(2):
                        W.load(sp, 0, b, weight_cols(weights[b], 0))
                    for n, (b, k) in enumerate(row_tiles):
                        if n >= TT:
                            sp.wait_ge(lo_done, n - TT + 1)
                        sp.dma_start(y[:, n % TT, :], o_t[b][k * P:(k + 1) * P, :]).then_inc(o_loaded[n % TT], 16)
                    for b in range(2):
                        load_sig(b, 0)
                    for i in range(TT):
                        sp.wait_ge(lo_done, TT + i + 1)
                        sp.dma_start(y[:, i, :], x[i * P:(i + 1) * P, :]).then_inc(x_loaded, 16)

                def step(i, u, last):
                    j, lot, n = 2 * i + u, 6 * i, 2 + 3 * u
                    if last:
                        W.load(sp, lot, n, w_out[j * P:(j + 1) * P, :].rearrange("p (k c) -> p k c", k=KT))
                        return
                    row = i * (2 * P) + u * P
                    W.load(sp, lot, n, weight_cols(weights[0], row + P))
                    sp.wait_ge(acc_free, 4 + 4 * j + NH)
                    load_sig(0, row + P)
                    W.load(sp, lot, n + 1, w_out[ds(row, P), :].rearrange("p (k c) -> p k c", k=KT))
                    sp.wait_ge(m_ready, NH * (j + 1))
                    load_sig(1, row + P)
                    W.load(sp, lot, n + 2, weight_cols(weights[1], row + P))
                steps(sp, prologue, step)

            @block.gpsimd
            def _(pool):
                W.prime_pool(pool)

                def prologue():
                    for n in range(2):
                        W.split(pool, 0, n)

                def step(i, u, last):
                    j = 2 * i + u
                    for n, done in enumerate((base(j) - 2, base(j), base(j) + NH)[:1 if last else 3]):
                        W.split(pool, 6 * i, 2 + 3 * u + n, (pe_done, done))
                steps(pool, prologue, step)

            @block.scalar
            def _(act):
                def high_m(j):
                    for half in range(NH):
                        at = slice(half * HALF, (half + 1) * HALF)
                        act.wait_ge(m_ready, NH * j + half + 1)
                        nc.scalar.copy(m_hi[:, at], merged[:, at]).then_inc(m_high, 1)

                def prologue():
                    for n, (b, k) in enumerate(row_tiles):
                        act.wait_ge(o_loaded[n % TT], 16 * (n // TT + 1))
                        nc.scalar.copy(parts[b][0][:, k, :], y[:, n % TT, :]).then_inc(hi_done, 1)
                    high_m(0)

                def step(i, u, last):
                    if not last:
                        high_m(2 * i + (u + 1))
                steps(act, prologue, step)

            @block.vector
            def _(dve):
                for sem_ in (acc_free, out_free):
                    dve.sem_inc(sem_, 4)

                def sb_term(at, j, first=False):
                    dve.wait_ge(sig_loaded[0], 16 * (j + 1))
                    if not first:
                        dve.wait_ge(m_split, NH * j)
                    for half in range(NH):
                        cols = slice(half * HALF, (half + 1) * HALF)
                        dve.wait_ge(pe_done, at + half + 1)
                        nc.vector.tensor_tensor(merged[:, cols], acc[0][half][:], sig[:, 0, cols], ALU.mult
                                                ).then_inc(acc_free, 1)

                def merge(at, j):
                    dve.wait_ge(sig_loaded[1], 16 * (j + 1))
                    for half in range(NH):
                        cols = slice(half * HALF, (half + 1) * HALF)
                        dve.wait_ge(pe_done, at + half + 1)
                        nc.vector.tensor_tensor(sig[:, 1, cols], acc[1][half][:], sig[:, 1, cols], ALU.mult
                                                ).then_inc(acc_free, 1)
                        dve.wait_ge(acc_free, 4 + 4 * j + NH + half + 1)
                        nc.vector.tensor_tensor(merged[:, cols], merged[:, cols], sig[:, 1, cols], ALU.add
                                                ).then_inc(m_ready, 1)
                    for half in range(NH):
                        cols = slice(half * HALF, (half + 1) * HALF)
                        dve.wait_ge(m_high, NH * j + half + 1)
                        nc.vector.tensor_tensor(m_lo[:, cols], merged[:, cols], m_hi[:, cols], ALU.subtract
                                                ).then_inc(m_split, 1)

                def prologue():
                    for n, (b, k) in enumerate(row_tiles):
                        dve.wait_ge(hi_done, n + 1)
                        nc.vector.tensor_tensor(parts[b][1][:, k, :], y[:, n % TT, :], parts[b][0][:, k, :],
                                                ALU.subtract).then_inc(lo_done, 1)
                    sb_term(0, 0, first=True)
                    merge(NH, 0)
                    dve.wait_ge(x_loaded, 16 * TT)

                def step(i, u, last):
                    j = 2 * i + u
                    first = base(j) + (0 if last else NH)
                    if not last:
                        sb_term(base(j), j + 1)
                    for o in range(OUTS):
                        at = y[:, o // NH, (o % NH) * HALF:(o % NH + 1) * HALF]
                        dve.wait_ge(pe_done, first + o + 1)
                        nc.vector.tensor_tensor(at, outs[o % 4][:], at, ALU.add).then_inc(out_free, 1)
                    if not last:
                        merge(base(j) + NH + OUTS, j + 1)
                steps(dve, prologue, step)

            @block.tensor
            def _(pe):
                def unit(b, lot, n, j):
                    W.take(pe, lot, n)
                    for half in range(NH):
                        pe.wait_ge(acc_free, 4 * j + NH * b + half + 1)
                        project_part(nc, acc[b][half][:], W.tile(n), parts[b], half, 0, 1).then_inc(pe_done, 1)

                def first_unit(b):
                    W.take(pe, 0, b)
                    pe.wait_ge(acc_free, NH * b + NH)
                    w = W.tile(b)
                    for k in range(KT):
                        pe.wait_ge(lo_done, KT * b + k + 1)
                        for half in range(NH):
                            for n, (wp, xp) in enumerate(((0, 0), (0, 1), (1, 0))):
                                ins = nc.tensor.matmul(acc[b][half][:], w[wp][:, k, :],
                                                       parts[b][xp][:, k, half * HALF:(half + 1) * HALF],
                                                       start=(k == 0 and n == 0), stop=(k == KT - 1 and n == 2))
                            if k == KT - 1:
                                ins.then_inc(pe_done, 1)

                def prologue():
                    for b in range(2):
                        first_unit(b)

                def step(i, u, last):
                    j, lot, n = 2 * i + u, 6 * i, 2 + 3 * u
                    if not last:
                        unit(0, lot, n, j + 1)
                        n += 1
                    W.take(pe, lot, n)
                    pe.wait_ge(m_split, NH * (j + 1))
                    hi, lo = W.hi[:, n % 2, :], W.lo[:, n % 2, :]
                    for o in range(OUTS):
                        rows, cols = slice(o // NH * P, (o // NH + 1) * P), slice((o % NH) * HALF, (o % NH + 1) * HALF)
                        pe.wait_ge(out_free, OUTS * j + o + 1)
                        for q, (m, w) in enumerate(((m_hi, hi), (m_hi, lo), (m_lo, hi))):
                            ins = nc.tensor.matmul(outs[o % 4][:], m[:, rows], w[:, cols], start=(q == 0), stop=(q == 2))
                        ins.then_inc(pe_done, 1)
                    if not last:
                        unit(1, lot, n + 1, j + 1)
                steps(pe, prologue, step)


def feed_forward(nc, hT, w_gate, w_up, w_down, y, out):
    CHUNK = 2
    N = FF // P // CHUNK
    OUTS = TT * NH
    ROUND = 4 * CHUNK + OUTS
    with ExitStack() as ctx:
        sb = lambda n, shape, dt=F32: ctx.enter_context(nc.sbuf_tensor(f"ff_{n}", shape, dt))
        sem = lambda n: ctx.enter_context(nc.semaphore(f"ff_{n}"))
        W = Weights(nc, ctx, "ffw", 3)
        hid_hi = sb("hid_hi", [P, 2, CHUNK, S], F32R)
        hid_lo = sb("hid_lo", [P, 2, CHUNK, S], F32R)
        act_buf = sb("act", [P, NH, HALF])
        ps = lambda n: ctx.enter_context(nc.psum_tensor(f"ff_{n}", [P, HALF], F32))
        gate, up = [ps(f"gate{h}") for h in range(NH)], [ps(f"up{h}") for h in range(NH)]
        down = [ps(f"down{i}") for i in range(4)]
        pe_done = sem("pe_done")
        sig_done = sem("sig_done")
        silu_done = sem("silu_done")
        gu_free = sem("gu_free")
        hi_done, lo_done = sem("hi_done"), sem("lo_done")
        d_free = sem("d_free")
        out_done = sem("out_done")
        base = lambda c: 8 + ROUND * c
        tiles = lambda k: 12 * k

        def steps(eng, prologue, step):
            prologue()
            with eng.Fori(0, (N - 1) // 2, 1) as k:
                for j in range(2):
                    step(k, j, False)
            step((N - 1) // 2, 0, True)

        with nc.Block() as block:
            @block.sync
            def _(sp):
                def units(k, first, col):
                    for n, w in enumerate((w_gate, w_up, w_gate, w_up)):
                        W.load(sp, tiles(k), first + n, weight_cols(w, col + (n // 2) * P))

                def step(k, j, last):
                    if not last:
                        units(k, 4 + 6 * j, k * (4 * P) + (j + 1) * 2 * P)
                    for f in range(CHUNK):
                        row = k * (4 * P) + (2 * j + f) * P
                        W.load(sp, tiles(k), 4 + 6 * j + f + (0 if last else 4),
                               w_down[ds(row, P), :].rearrange("p (k c) -> p k c", k=KT))
                steps(sp, lambda: units(0, 0, 0), step)
                for t in range(TT):
                    sp.wait_ge(d_free, 4 + OUTS * (N - 1) + NH * (t + 1))
                    sp.dma_start(out[t * P:(t + 1) * P, :], y[:, t, :]).then_inc(out_done, 16)
                sp.wait_ge(out_done, 16 * TT)

            @block.gpsimd
            def _(pool):
                W.prime_pool(pool)

                def prologue():
                    for n in range(3):
                        W.split(pool, 0, n)
                    W.split(pool, 0, 3, (pe_done, 2))

                def step(k, j, last):
                    c = 2 * k + j
                    done = [base(c) - 4, base(c), base(c), base(c) + 2, base(c) + 4, base(c) + 6]
                    for n in range(2 if last else 6):
                        W.split(pool, tiles(k), 4 + 6 * j + n, (pe_done, done[n]))
                steps(pool, prologue, step)

            @block.tensor
            def _(pe):
                def units(k, first, chunk):
                    for n in range(4):
                        W.take(pe, tiles(k), first + n)
                        for half in range(NH):
                            f = n // 2
                            if n % 2 == 0:
                                pe.wait_ge(gu_free, 2 * (2 * chunk + f) + half + 1)
                            acc = (gate, up)[n % 2][half]
                            project_part(nc, acc[:], W.tile(first + n), hT, half, 0, 1).then_inc(pe_done, 1)

                def step(k, j, last):
                    c = 2 * k + j
                    if not last:
                        units(k, 4 + 6 * j, c + 1)
                    first = 4 + 6 * j + (0 if last else 4)
                    for f in range(CHUNK):
                        W.take(pe, tiles(k), first + f)
                    pe.wait_ge(lo_done, 2 * CHUNK * (c + 1))
                    w = [(W.hi[:, (first + f) % 3, :], W.lo[:, (first + f) % 3, :]) for f in range(CHUNK)]
                    for o in range(OUTS):
                        t, nh = o // NH, o % NH
                        pe.wait_ge(d_free, OUTS * c + o + 1)
                        rows, cols = slice(t * P, (t + 1) * P), slice(nh * HALF, (nh + 1) * HALF)
                        for n in range(3 * CHUNK):
                            f, kind = n // 3, n % 3
                            h = (hid_hi, hid_hi, hid_lo)[kind][:, j, f, rows]
                            ins = nc.tensor.matmul(down[o % 4][:], h, w[f][(0, 1, 0)[kind]][:, cols],
                                                   start=(n == 0), stop=(n == 3 * CHUNK - 1))
                        ins.then_inc(pe_done, 1)
                steps(pe, lambda: units(0, 0, 0), step)

            @block.scalar
            def _(act):
                def units(at, chunk, buf):
                    for f in range(CHUNK):
                        for half in range(NH):
                            num = 2 * CHUNK * chunk + 2 * f + half
                            act.wait_ge(pe_done, at + 4 * f + half + 1)
                            need(act, lo_done, num - 1)
                            nc.scalar.activation(act_buf[:, half, :], gate[half][:], ACT.Sigmoid).then_inc(sig_done, 1)
                            act.wait_ge(gu_free, num + 3)
                            nc.scalar.copy(hid_hi[:, buf, f, half * HALF:(half + 1) * HALF], act_buf[:, half, :]
                                           ).then_inc(hi_done, 1)

                def step(k, j, last):
                    if not last:
                        units(base(2 * k + j), 2 * k + (j + 1), (j + 1) % 2)
                steps(act, lambda: units(0, 0, 0), step)

            @block.vector
            def _(dve):
                dve.sem_inc(gu_free, 2)
                dve.sem_inc(d_free, 4)

                def units(at, chunk, buf):
                    for f in range(CHUNK):
                        for half in range(NH):
                            num, a = 2 * CHUNK * chunk + 2 * f + half, act_buf[:, half, :]
                            dve.wait_ge(sig_done, num + 1)
                            nc.vector.tensor_tensor(a, gate[half][:], a, ALU.mult).then_inc(silu_done, 1)
                            dve.wait_ge(silu_done, num + 1)
                            dve.wait_ge(pe_done, at + 4 * f + 2 + half + 1)
                            nc.vector.tensor_tensor(a, up[half][:], a, ALU.mult).then_inc(gu_free, 1)
                            dve.wait_ge(hi_done, num + 1)
                            cols = slice(half * HALF, (half + 1) * HALF)
                            nc.vector.tensor_tensor(hid_lo[:, buf, f, cols], a, hid_hi[:, buf, f, cols],
                                                    ALU.subtract).then_inc(lo_done, 1)

                def step(k, j, last):
                    c = 2 * k + j
                    if not last:
                        units(base(c), 2 * k + (j + 1), (j + 1) % 2)
                    first = base(c) + (0 if last else 4 * CHUNK)
                    for o in range(OUTS):
                        t, nh = o // NH, o % NH
                        at = y[:, t, nh * HALF:(nh + 1) * HALF]
                        dve.wait_ge(pe_done, first + o + 1)
                        nc.vector.tensor_tensor(at, down[o % 4][:], at, ALU.add).then_inc(d_free, 1)
                steps(dve, lambda: units(0, 0, 0), step)


def layer(nc, x, norm1_g, w_in, sb_q_norm_g, sb_k_norm_g, gla_gate_w2, gla_gate_b, gla_out_norm_g,
          w_branch_sb, w_branch_gla, w_out, norm2_g, w_ffn_gate, w_ffn_up, w_ffn_down, out):
    scratch = lambda n, rows: nc.dram_tensor(n, [rows, S], F32, kind="Internal").ap()
    osb_t, ogla_t = scratch("osb_t", D), scratch("ogla_t", D)
    gates_t = scratch("gates_t", 2 * D)
    with ExitStack() as ctx:
        c = constants(nc, ctx)
        with ExitStack() as heads:
            hT = [heads.enter_context(nc.sbuf_tensor(f"h1_{n}", [P, KT, S], F32R)) for n in ("hi", "lo")]
            with ExitStack() as first:
                x_sb = first.enter_context(nc.sbuf_tensor("x_sb", [P, TT, D], F32))
                norm_transposed(nc, c, "norm1", x[0], x_sb, norm1_g, hT)
            linear_attention(nc, c, hT, w_in[0], gla_gate_w2[0], gla_gate_b, gla_out_norm_g, ogla_t, gates_t)
            stick_breaking(nc, c, hT, w_in[0], (sb_q_norm_g, sb_k_norm_g), osb_t, gates_t)
        y = ctx.enter_context(nc.sbuf_tensor("y", [P, TT, D], F32))
        merge_and_project(nc, (osb_t, ogla_t), gates_t, (w_branch_sb[0], w_branch_gla[0]), w_out[0], x[0], y)
        hT = [ctx.enter_context(nc.sbuf_tensor(f"h2_{n}", [P, KT, S], F32R)) for n in ("hi", "lo")]
        norm_transposed(nc, c, "norm2", None, y, norm2_g, hT)
        feed_forward(nc, hT, w_ffn_gate[0], w_ffn_up[0], w_ffn_down[0], y, out[0])


_INS = ["x", "norm1_g", "w_in", "sb_q_norm_g", "sb_k_norm_g", "gla_gate_w2", "gla_gate_b", "gla_out_norm_g",
        "w_branch_sb", "w_branch_gla", "w_out", "norm2_g", "w_ffn_gate", "w_ffn_up", "w_ffn_down"]


def kernel(**inputs):
    import concourse.bacc as bacc
    from concourse.bass_utils import run_bass_kernel_spmd

    nc = bacc.Bacc("TRN2", target_bir_lowering=False, num_devices=1)
    arrays = {n: np.ascontiguousarray(inputs[n]) for n in _INS}
    args = [nc.dram_tensor(n, a.shape, mybir.dt.from_np(a.dtype), kind="ExternalInput").ap()
            for n, a in arrays.items()]
    out = nc.dram_tensor("out", [1, S, D], F32, kind="ExternalOutput").ap()
    layer(nc, *args, out)
    result = run_bass_kernel_spmd(nc, [arrays], core_ids=[0])
    return result.results[0]["out"]
```

```python
from contextlib import ExitStack

import numpy as np
import concourse.bass as bass
from concourse import mybir

F32 = mybir.dt.float32
F32R = mybir.dt.float32r
I32 = mybir.dt.int32
BF16 = mybir.dt.bfloat16
ALU = mybir.AluOpType
ACT = mybir.ActivationFunctionType
AX_X = mybir.AxisListType.X
ds = bass.ds

P = 128
S = 1024
D = 1024
KT = D // P
TT = S // P
HALF = 512
NH = S // HALF
EPS = 1e-6

SB_HEADS, SB_DH = 16, 64
PAIRS = SB_HEADS * SB_DH // P
GLA_HEADS, GLA_DK, GLA_DV = 4, 128, 256
LR = 16
TAU = 16.0
FF = 2816

SBQ, SBK, SBV = 0, 1024, 2048
GLQ, GLK, GLV, GLR, GLLR = 3072, 3584, 4096, 5120, 6144
GATE = 6160


def need(eng, sem, value):
    if isinstance(value, int) and value <= 0:
        return
    eng.wait_ge(sem, value)


class Chain:

    def __init__(self, eng, sem):
        self.eng, self.sem, self.base, self.n = eng, sem, 0, 0

    def enter(self, base):
        self.base, self.n = base, 0

    def link(self, ins):
        self.n += 1
        ins.then_inc(self.sem, 1)
        self.eng.wait_ge(self.sem, self.base + self.n)


def rounds(eng, count, body):
    with eng.Fori(0, count - 1, 1) as i:
        body(i, False)
    body(count - 1, True)


class Weights:

    def __init__(self, nc, ctx, name, ring):
        self.nc, self.ring, self.base = nc, ring, 0
        sb = lambda n, dt: ctx.enter_context(nc.sbuf_tensor(f"{name}_{n}", [P, ring, D], dt))
        sem = lambda n: ctx.enter_context(nc.semaphore(f"{name}_{n}"))
        self.ones = ctx.enter_context(nc.sbuf_tensor(f"{name}_ones", [P, 64], F32))
        self.raw, self.hi, self.lo = sb("raw", F32), sb("hi", F32R), sb("lo", F32R)
        self.loaded = [sem(f"loaded{i}") for i in range(ring)]
        self.rounded = sem("rounded")
        self.ready = sem("ready")

    def prime_pool(self, pool):
        self.nc.gpsimd.memset(self.ones[:], 1.0).then_inc(self.rounded, 1)
        pool.wait_ge(self.rounded, 1)
        pool.sem_inc(self.ready, self.ring)

    def next_phase(self, tiles):
        assert tiles % self.ring == 0
        self.base += tiles

    def take(self, pe, lot, step):
        pe.wait_ge(self.ready, self.ring + self.base + lot + step + 1)

    def load(self, sp, lot, step, src):
        s = step % self.ring
        need(sp, self.ready, self.base + lot + step + 1)
        dst = self.raw[:, s, :].rearrange("p (k c) -> p k c", k=src.shape[1])
        sp.dma_start(dst, src).then_inc(self.loaded[s], 16)

    def split(self, pool, lot, step, done=None):
        s = step % self.ring
        raw, hi, lo = self.raw[:, s, :], self.hi[:, s, :], self.lo[:, s, :]
        pool.wait_ge(self.loaded[s], ((self.base + lot) // self.ring + step // self.ring + 1) * 16)
        if done is not None:
            pool.wait_ge(*done)
        self.nc.gpsimd.tensor_tensor(hi[:, 0:64], raw[:, 0:64], self.ones[:], ALU.mult)
        self.nc.gpsimd.tensor_scalar(hi[:, 64:D], raw[:, 64:D], 1.0, 0.0, ALU.mult, ALU.add).then_inc(self.rounded, 1)
        pool.wait_ge(self.rounded, self.base + lot + step + 2)
        self.nc.gpsimd.tensor_tensor(lo, raw, hi, ALU.subtract).then_inc(self.ready, 1)

    def tile(self, step):
        s = step % self.ring
        view = lambda t: t[:, s, :].rearrange("p (k c) -> p k c", k=KT)
        return view(self.hi), view(self.lo)


def weight_cols(w, col):
    return w.rearrange("(k p) c -> p k c", p=P)[:, :, ds(col, P)]


def project_part(nc, acc, wt, xt, half, part, parts):
    (w_hi, w_lo), (x_hi, x_lo) = wt, xt
    steps = [(a, b, k) for a, b in ((w_hi, x_hi), (w_hi, x_lo), (w_lo, x_hi)) for k in range(KT)]
    per = len(steps) // parts
    ins = None
    for n in range(part * per, (part + 1) * per):
        a, b, k = steps[n]
        ins = nc.tensor.matmul(acc, a[:, k, :], b[:, k, half * HALF:(half + 1) * HALF],
                               start=(n == 0), stop=(n == len(steps) - 1))
    return ins


def constants(nc, ctx):
    sb = lambda n, shape, dt: ctx.enter_context(nc.sbuf_tensor(n, shape, dt))
    c = {
        "ident": sb("ident", [P, P], F32), "ident_b": sb("ident_b", [P, P], BF16),
        "not_before": sb("not_before", [P, P], BF16), "head_mean": sb("head_mean", [P, P // SB_DH], F32),
    }
    made = ctx.enter_context(nc.semaphore("const_made"))
    with nc.Block() as block:
        @block.gpsimd
        def _(pool):
            chain = Chain(pool, made)
            for name in ("ident", "ident_b", "not_before", "head_mean"):
                chain.link(nc.gpsimd.memset(c[name][:], 0.0))
            for r in range(0, P, SB_DH):
                chain.link(nc.gpsimd.memset(c["head_mean"][r:r + SB_DH, r // SB_DH:r // SB_DH + 1], 1.0 / SB_DH))
            for name in ("ident", "ident_b"):
                chain.link(nc.gpsimd.affine_select(out=c[name][:], in_=c[name][:], compare_op=ALU.not_equal,
                                                   fill=1.0, base=0, pattern=[[-1, P]], channel_multiplier=1))
            chain.link(nc.gpsimd.affine_select(out=c["not_before"][:], in_=c["not_before"][:],
                                               compare_op=ALU.is_gt, fill=-1e30, base=0, pattern=[[-1, P]],
                                               channel_multiplier=1))
    return c


def rsqrt_guess(nc, chain, ms, y):
    chain.link(nc.vector.tensor_scalar(y.bitcast(I32), ms.bitcast(I32), -0.5, 1597463007.0, ALU.mult, ALU.add))
    chain.link(nc.vector.tensor_scalar(ms, ms, -0.5, None, ALU.mult))


def rsqrt_newton(nc, chain, ms, y, u):
    chain.link(nc.vector.tensor_tensor(u, y, y, ALU.mult))
    chain.link(nc.vector.tensor_tensor(u, u, ms, ALU.mult))
    chain.link(nc.vector.scalar_tensor_tensor(y, u, 1.5, y, ALU.add, ALU.mult))


def rsqrt(nc, chain, ms, y, u):
    rsqrt_guess(nc, chain, ms, y)
    for _ in range(3):
        rsqrt_newton(nc, chain, ms, y, u)


def norm_transposed(nc, c, name, src, x, g_all, ssq, gain, hT, W, following):
    h_hi, h_lo = hT
    if src is None:
        groups, gpsimd_tiles = [range(TT)], (3, 6)
        gains_first, gains_before, group_after = (0, 1), {0: (2,), 1: (4,), 2: (5,), 3: (7,)}, {}
    else:
        groups, gpsimd_tiles = [range(4), range(4, TT)], (3, 6, 7)
        gains_first, gains_before, group_after = (0, 1, 2), {0: (4, 5)}, {0: 1}
    dve_tiles = [i for i in range(TT) if i not in gpsimd_tiles]
    with ExitStack() as ctx:
        sb = lambda n, shape, dt=F32: ctx.enter_context(nc.sbuf_tensor(f"{name}_{n}", shape, dt))
        sem = lambda n: ctx.enter_context(nc.semaphore(f"{name}_{n}"))
        xg = sb("xg", [P, TT, D])
        junk = sb("junk", [P, 2, D])
        work = sb("work", [P, 3, TT])
        diag = sb("diag", [P, TT, P])
        bank = [ctx.enter_context(nc.psum_tensor(f"{name}_t{i}", [P, 4, P], F32)) for i in range(4)]
        x_loaded = [sem(f"x_loaded{i}") for i in range(TT)]
        g_loaded = sem("g_loaded")
        ssq_ready = sem("ssq_ready")
        xg_dve, xg_pool = sem("xg_dve"), sem("xg_pool")
        dve_step = sem("dve_step")
        diag_ready = sem("diag_ready")
        t_done = sem("t_done")
        hi_done = sem("hi_done")
        lo_done = sem("lo_done")

        def block_of(t, i, half):
            return t[:, 4 * half:4 * half + 4, i * P:(i + 1) * P]

        with nc.Block() as block:
            @block.sync
            def _(sp):
                for i in range(TT if src is not None else 1):
                    if src is not None:
                        sp.dma_start(x[:, i, :], src[i * P:(i + 1) * P, :]).then_inc(x_loaded[i], 16)
                    if i == 0:
                        sp.dma_start(g_all[:], gain[0].partition_broadcast(P)).then_inc(g_loaded, 16)
                for n, w in enumerate(following):
                    W.load(sp, 0, n, w)

            @block.scalar
            def _(act):
                def square(i):
                    act.wait_ge(x_loaded[i], 16)
                    if i > 1:
                        act.wait_ge(ssq_ready, i - 1)
                    nc.scalar.activation(junk[:, i % 2, :], x[:, i, :], ACT.Square,
                                         accum_out=ssq[:, i:i + 1]).then_inc(ssq_ready, 1)

                def high(i):
                    for half in range(2):
                        act.wait_ge(t_done, 2 * i + half + 1)
                        nc.scalar.copy(block_of(h_hi, i, half), bank[(2 * i + half) % 4][:]).then_inc(hi_done, 1)

                for i in range(TT if src is not None else 0):
                    square(i)
                for i in range(TT):
                    high(i)

            @block.gpsimd
            def _(pool):
                W.prime_pool(pool)
                pool.wait_ge(g_loaded, 16)
                for i in gpsimd_tiles:
                    if src is not None:
                        pool.wait_ge(x_loaded[i], 16)
                    nc.gpsimd.tensor_tensor(xg[:, i, :], x[:, i, :], g_all[:], ALU.mult).then_inc(xg_pool, 1)
                for n in range(len(following)):
                    W.split(pool, 0, n)

            @block.vector
            def _(dve):
                chain = Chain(dve, dve_step)
                dve.sem_inc(lo_done, 4)

                def apply_gain(i):
                    if src is not None:
                        dve.wait_ge(x_loaded[i], 16)
                    nc.vector.tensor_tensor(xg[:, i, :], x[:, i, :], g_all[:], ALU.mult).then_inc(xg_dve, 1)

                def group(g):
                    tiles = groups[g]
                    at = slice(tiles[0], tiles[-1] + 1)
                    if src is not None:
                        dve.wait_ge(ssq_ready, tiles[-1] + 1)
                    chain.link(nc.vector.tensor_scalar(work[:, 0, at], ssq[:, at], 1.0 / D, EPS, ALU.mult, ALU.add))
                    rsqrt(nc, chain, work[:, 0, at], work[:, 1, at], work[:, 2, at])
                    for i in tiles:
                        nc.vector.tensor_scalar(diag[:, i, :], c["ident"][:], work[:, 1, i:i + 1], None, ALU.mult
                                                ).then_inc(diag_ready, 1)

                def low(i):
                    for half in range(2):
                        dve.wait_ge(hi_done, 2 * i + half + 1)
                        nc.vector.tensor_tensor(block_of(h_lo, i, half), bank[(2 * i + half) % 4][:],
                                                block_of(h_hi, i, half), ALU.subtract).then_inc(lo_done, 1)

                if src is None:
                    group(0)
                dve.wait_ge(g_loaded, 16)
                for i in gains_first:
                    apply_gain(i)
                if src is not None:
                    group(0)
                for t in range(TT):
                    for i in gains_before.get(t, ()):
                        apply_gain(i)
                    low(t)
                    if t in group_after:
                        group(group_after[t])

            @block.tensor
            def _(pe):
                for i in range(TT):
                    mine = dve_tiles if i in dve_tiles else gpsimd_tiles
                    pe.wait_ge(xg_dve if i in dve_tiles else xg_pool, mine.index(i) + 1)
                    pe.wait_ge(diag_ready, i + 1)
                    for half in range(2):
                        u = (2 * i + half) % 4
                        pe.wait_ge(lo_done, 2 * i + half + 1)
                        for q in range(4):
                            k = 4 * half + q
                            ins = nc.tensor.matmul(bank[u][:, q, :], xg[:, i, k * P:(k + 1) * P], diag[:, i, :],
                                                   start=True, stop=True)
                        ins.then_inc(t_done, 1)


SLOTS = 32
SCORE_SLOT = [0, 1, 2, 3, 4, 5, 6, 7, 9, 11, 12, 13, 14, 15, 16, 17]
SCORE_STEPS = [(hh, tb) for hh in range(2) for tb in range(TT)]
WEIGHT_STEPS = [(hh, g, j) for hh in range(2) for g in range(NH) for j in range(4 * g + 4)]
WEIGHT_SLOT = 7
NSC, NWT = len(SCORE_STEPS), len(WEIGHT_STEPS)
STACKS = 12
SB_CHAIN = 22
LAST_GATES = 3
SB_TILES = 3 + 4 * (PAIRS - 1) + LAST_GATES
LAST_LATER = 2
MS_SLOT = [6, 10, 13, 17]
V_SLOT = [25, 27]
SPREAD_SLOT = [14, 18]


def stick_breaking(nc, c, hT, w_in, qk_gains, osb_t, gates_t, W, following, ot, ot_out):
    with ExitStack() as ctx:
        sb = lambda n, shape, dt: ctx.enter_context(nc.sbuf_tensor(f"sb_{n}", shape, dt))
        ps = lambda n, shape: ctx.enter_context(nc.psum_tensor(f"sb_{n}", shape, F32))
        sem = lambda n: ctx.enter_context(nc.semaphore(f"sb_{n}"))
        qs = [sb(f"qs{e}", [P, S], F32R) for e in range(2)]
        kh = [sb(f"kh{e}", [P, S], F32R) for e in range(2)]
        kl = [sb(f"kl{e}", [P, S], F32R) for e in range(2)]
        k_new = sb("k_new", [P, S], F32)
        q_st = sb("q_st", [P, 2, S], F32R)
        k_st = sb("k_st", [P, 2, S], F32R)
        sq = sb("sq", [P, NH, HALF], F32)
        gains = sb("gains", [P, 2], F32)
        ms = sb("ms", [P, 2, TT * 2], F32)
        rms = sb("rms", [P, 2, TT * 2], F32)
        tmp = sb("tmp", [P, TT * 2], F32)
        k_rs = sb("k_rs", [P, TT, P], F32)
        q_scale = sb("q_scale", [P, 2, TT * 2], F32)
        vt = sb("vt", [P, S], F32)
        v = sb("v", [P, TT, 2, 2, SB_DH], F32R)
        rest = sb("rest", [P, 2, S + 1], F32)
        beta = sb("beta", [P, 2, S], F32)
        rows = [sb(f"rows{g}", [P, 4, HALF * (g + 1)], F32) for g in range(NH)]
        wt_hi = sb("wt_hi", [P, 2, HALF], F32R)
        wt_lo = sb("wt_lo", [P, 2, HALF], F32R)
        o_low = sb("o_low", [SB_DH, HALF], F32)
        G = [ps(f"g{h}", [P, HALF]) for h in range(NH)]
        Z = [ps(f"z{b}", [P, S]) for b in range(2)]
        T = ps("t", [P, HALF])
        O = ps("o", [P, HALF])

        g_loaded, gains_made = sem("g_loaded"), sem("gains_made")
        g_done = [sem(f"g_done{h}") for h in range(NH)]
        g_free = [sem(f"g_free{h}") for h in range(NH)]
        sq_ready = sem("sq_ready")
        k_rs_ready = sem("k_rs_ready")
        q_scale_ready = sem("q_scale_ready")
        q_high, k_high = sem("q_high"), sem("k_high")
        split_done = sem("split_done")
        half_copied = sem("half_copied")
        stacked = sem("stacked")
        z_done = sem("z_done")
        z_free = sem("z_free")
        row_ready = sem("row_ready")
        scanned = sem("scanned")
        t_done = sem("t_done")
        hi_ready = sem("hi_ready")
        lo_ready = sem("lo_ready")
        vt_done = sem("vt_done")
        v_high = sem("v_high")
        v_ready = sem("v_ready")
        av_done = sem("av_done")
        o_free = sem("o_free")
        gs_out = sem("gs_out")
        dve_step = sem("dve_step")

        units = lambda it: 4 * it
        g_uses = lambda it: 6 + 7 * it
        t_uses = lambda it: NWT * it
        def rows_used(it, e, tb):
            before = WEIGHT_STEPS.index((0, tb // 4, tb)) + 1
            return t_uses(it) + before + (NWT if e == 1 else NWT // 2)

        def v_block(part):
            return Z[1][:, part * HALF:(part + 1) * HALF].rearrange("p (j e d) -> p j e d", j=TT // 2, e=2)

        def slot_of_unit(s):
            return s // 8, s % 8

        with nc.Block() as block:
            @block.sync
            def _(sp):
                for half in range(2):
                    for x in range(2):
                        sp.dma_start(gains[half * SB_DH:(half + 1) * SB_DH, x:x + 1],
                                     qk_gains[x].rearrange("a d -> d a")).then_inc(g_loaded, 16)

                def stacks(it):
                    sp.wait_ge(split_done, NH * (it + 2))
                    need(sp, z_done, NSC * (it + 1))
                    for e in range(2):
                        rows_e = slice(e * SB_DH, (e + 1) * SB_DH)
                        for top in range(2):
                            to = slice(top * SB_DH, (top + 1) * SB_DH)
                            for dst, src, x in ((qs[e], q_st, top), (kh[e], k_st, 0), (kl[e], k_st, 1)):
                                sp.dma_start(dst[to, :].bitcast(F32), src[rows_e, x, :].bitcast(F32)).then_inc(stacked, 16)

                W.load(sp, 0, 2, weight_cols(w_in, SBV))
                W.load(sp, 0, 3, weight_cols(w_in, SBK + P))
                stacks(-1)
                W.load(sp, 0, 4, weight_cols(w_in, SBQ + P))

                def send_gate(half, use, row):
                    sp.wait_ge(g_free[half], use + 2)
                    sp.dma_start(gates_t[ds(row, P), half * HALF:(half + 1) * HALF], sq[:, half, :]
                                 ).then_inc(gs_out, 16)

                def send_o(it):
                    sp.wait_ge(o_free, 4 * it + 5)
                    sp.dma_start(osb_t[ds(it * P, P), :], ot[:]).then_inc(ot_out, 16)

                def body(it, k_next, q_next):
                    W.load(sp, units(it), 5, weight_cols(w_in, it * P + (SBV + P)))
                    W.load(sp, units(it), 6, weight_cols(w_in, it * P + GATE))
                    W.load(sp, units(it), 7, weight_cols(w_in, k_next))
                    stacks(it)
                    W.load(sp, units(it), 8, weight_cols(w_in, q_next))
                    send_gate(0, g_uses(it) + 6, it * P)
                    send_gate(1, g_uses(it) + 6, it * P)
                    send_o(it)

                last_gates = [GATE + (PAIRS - 1 + n) * P for n in range(LAST_GATES)]
                with sp.Fori(0, PAIRS - 2, 1) as it:
                    body(it, it * P + (SBK + 2 * P), it * P + (SBQ + 2 * P))
                body(PAIRS - 2, last_gates[0], last_gates[1])
                W.load(sp, units(PAIRS - 1), 5, weight_cols(w_in, last_gates[2]))
                for n in range(2):
                    W.load(sp, units(PAIRS - 1), 6 + n, following[n])
                for n in range(LAST_GATES):
                    for half in range(NH):
                        send_gate(half, g_uses(PAIRS - 1) + n, (PAIRS - 1 + n) * P)
                send_o(PAIRS - 1)
                sp.wait_ge(gs_out, 16 * (NH * (PAIRS - 1 + LAST_GATES) + 1))

            @block.gpsimd
            def _(pool):
                W.split(pool, 0, 1)
                W.split(pool, 0, 2, (g_done[1], 1))
                W.split(pool, 0, 3, (g_done[1], 3))
                for _ in range(2):
                    pool.sem_inc(row_ready, 1)

                def weights(it, n):
                    e, tb = SCORE_STEPS[n]
                    width = (tb + 1) * P
                    pool.wait_ge(scanned, NSC * it + n + 1)
                    pool.wait_ge(t_done, rows_used(it, e, tb))
                    nc.gpsimd.tensor_tensor(rows[tb // 4][:, tb % 4, 0:width], beta[:, n % 2, 0:width],
                                            rest[:, n % 2, 1:width + 1], ALU.mult).then_inc(row_ready, 1)

                def body(it, last):
                    if last:
                        splits = {0: (4, 0), 9 + LAST_LATER: (5, 1), 17 + LAST_LATER: (6, 2), 25 + LAST_LATER: (7, 3)}
                    else:
                        splits = {0: (4, 0), 10: (5, 1), 19: (6, 3), 25: (7, 6)}
                    for s in range(SLOTS):
                        if s in splits:
                            step, uses = splits[s]
                            W.split(pool, units(it), step, (g_done[1], g_uses(it) + uses))
                        if s - 1 in SCORE_SLOT:
                            weights(it, SCORE_SLOT.index(s - 1))
                rounds(pool, PAIRS, body)

            @block.tensor
            def _(pe):
                pe.sem_inc(av_done, 2)
                pe.sem_inc(t_done, NWT)

                def fill(it_units, step, eighth, use):
                    half, part = eighth // 4, eighth % 4
                    if eighth == 0:
                        W.take(pe, it_units, step)
                    if part == 0:
                        pe.wait_ge(g_free[half], use + 1)
                    ins = project_part(nc, G[half][:], W.tile(step), hT, half, part, 4)
                    if part == 3:
                        ins.then_inc(g_done[half], 1)

                def mean_squares(prep, x, half, use):
                    pe.wait_ge(sq_ready, 4 * prep + 2 * x + half + 1)
                    pe.wait_ge(g_free[half], use + 1)
                    for t in range(TT // 2):
                        ins = nc.tensor.matmul(G[half][:, 2 * t:2 * t + 2], sq[:, half, t * P:(t + 1) * P],
                                               c["head_mean"][:], start=True, stop=True)
                    ins.then_inc(g_done[half], 1)

                def spread_k_rs(prep, half, use):
                    pe.wait_ge(k_rs_ready, prep + 1)
                    pe.wait_ge(g_free[half], use + 1)
                    for t in range(TT // 2):
                        ins = nc.tensor.matmul(G[half][:, t * P:(t + 1) * P], k_rs[:, half * (TT // 2) + t, :],
                                               c["ident"][:], start=True, stop=True)
                    ins.then_inc(g_done[half], 1)

                def transpose_v(part, copied):
                    pe.wait_ge(g_free[part], copied)
                    for j in range(4 * part, 4 * part + 4):
                        ins = nc.tensor.transpose(Z[1][:, j * P:(j + 1) * P], vt[:, j * P:(j + 1) * P], c["ident"][:])
                    ins.then_inc(vt_done, 1)

                for step in range(3):
                    for eighth in range(8):
                        fill(0, step, eighth, (0, 2, 5)[step])
                    if step < 2:
                        for half in range(NH):
                            mean_squares(0, step, half, 2 * step + 1)
                    if step == 1:
                        for half in range(NH):
                            spread_k_rs(0, half, 4)
                for part in range(2):
                    transpose_v(part, 7)

                def scores(it, n):
                    e, tb = SCORE_STEPS[n]
                    if n == 0:
                        pe.wait_ge(stacked, 16 * STACKS * (it + 1))
                    pe.wait_ge(z_free, NSC * it + n + 1)
                    if n == 1:
                        pe.wait_ge(v_ready, 2 * (it + 1))
                    z, width = Z[n % 2], (tb + 1) * P
                    q = qs[e][:, tb * P:(tb + 1) * P]
                    for a in range(0, width, HALF):
                        b = min(a + HALF, (width + 255) // 256 * 256)
                        nc.tensor.matmul(z[:, a:b], q, kh[e][:, a:b], start=True, stop=False)
                        nc.tensor.matmul(z[:, a:b], q, kl[e][:, a:b], start=False, stop=(b < width))
                    nc.tensor.matmul(z[:, width - P:width], c["ident_b"][:], c["not_before"][:],
                                     start=False, stop=True).then_inc(z_done, 1)

                def transposes(it, m):
                    e, g, j = WEIGHT_STEPS[m]
                    first = max(j, 4 * g)
                    if j == 0:
                        pe.wait_ge(row_ready, 2 + NSC * it + 8 * e + 4 * g + 4)
                    pe.wait_ge(lo_ready, t_uses(it) + m + 1)
                    for tb in range(first, 4 * g + 4):
                        ins = nc.tensor.transpose(T[:, (tb - 4 * g) * P:(tb - 4 * g + 1) * P],
                                                  rows[g][:, tb - 4 * g, j * P:(j + 1) * P], c["ident"][:])
                    ins.then_inc(t_done, 1)

                def weigh(it, m):
                    e, g, j = WEIGHT_STEPS[m]
                    a = max(j - 4 * g, 0) * P
                    if j == 0:
                        pe.wait_ge(o_free, 4 * it + 2 * e + g + 1)
                    pe.wait_ge(lo_ready, t_uses(it) + m + 2)
                    o, hi, lo = O[0:SB_DH, a:HALF], wt_hi[:, m % 2, a:HALF], wt_lo[:, m % 2, a:HALF]
                    both = lambda: nc.tensor.matmul(O[:, a:HALF], v[:, j, e].rearrange("p x d -> p (x d)"), hi,
                                                    start=(j == 0), stop=(j == 4 * g + 3))
                    if j == 4 * g + 3:
                        nc.tensor.matmul(o, v[:, j, e, 0], lo, start=False, stop=False)
                        both().then_inc(av_done, 1)
                    else:
                        both()
                        nc.tensor.matmul(o, v[:, j, e, 0], lo, start=False, stop=False).then_inc(av_done, 1)

                def body(it, last):
                    fills = LAST_GATES if last else 4
                    for s in range(SLOTS):
                        m = s - WEIGHT_SLOT
                        if 0 <= m < NWT:
                            transposes(it, m)
                        if s in SCORE_SLOT:
                            scores(it, SCORE_SLOT.index(s))
                        if not last and s in MS_SLOT:
                            i = MS_SLOT.index(s)
                            mean_squares(it + 1, i // 2, i % 2, g_uses(it) + 2 * (i // 2) + 1)
                        if not last and s in SPREAD_SLOT:
                            spread_k_rs(it + 1, SPREAD_SLOT.index(s), g_uses(it) + 4)
                        u, eighth = slot_of_unit(s - (LAST_LATER if last else 0))
                        if 0 <= u < fills:
                            fill(units(it), 3 + u, eighth, g_uses(it) + (u if last else (0, 2, 5, 6)[u]))
                        if 0 <= m - 1 < NWT:
                            weigh(it, m - 1)
                        if not last and s in V_SLOT:
                            if s == V_SLOT[0]:
                                pe.wait_ge(z_free, NSC * (it + 1) + 2)
                            transpose_v(V_SLOT.index(s), g_uses(it) + 7)
                rounds(pe, PAIRS, body)

            @block.scalar
            def _(act):
                for sem_ in (z_free, z_free):
                    act.sem_inc(sem_, 1)
                act.sem_inc(gs_out, 16)

                def square(half, use):
                    act.wait_ge(g_done[half], use + 1)
                    nc.scalar.activation(sq[:, half, :], G[half][:], ACT.Square).then_inc(sq_ready, 1)

                def high_q(prep, half):
                    need(act, stacked, 16 * STACKS * prep)
                    nc.scalar.copy(q_st[:, 0, half * HALF:(half + 1) * HALF], G[half][:]).then_inc(q_high, 1)

                def high_k(prep, half, use):
                    act.wait_ge(g_free[half], use + 2)
                    need(act, stacked, 16 * STACKS * prep)
                    at = slice(half * HALF, (half + 1) * HALF)
                    nc.scalar.copy(k_st[:, 0, at], k_new[:, at]).then_inc(k_high, 1)

                def copy_vt(half, use):
                    act.wait_ge(g_done[half], use + 1)
                    nc.scalar.copy(vt[:, half * HALF:(half + 1) * HALF], G[half][:]).then_inc(g_free[half], 1)

                def high_v(prep, part, used=None):
                    act.wait_ge(vt_done, 2 * prep + part + 1)
                    if used is not None:
                        act.wait_ge(av_done, used)
                    nc.scalar.copy(v[:, 4 * part:4 * part + 4, :, 0, :], v_block(part)).then_inc(v_high, 1)

                def gate(n_done, half, use):
                    act.wait_ge(g_done[half], use + 1)
                    act.wait_ge(gs_out, 16 * (NH * n_done + 1))
                    nc.scalar.activation(sq[:, half, :], G[half][:], ACT.Sigmoid).then_inc(g_free[half], 1)

                for half in range(NH):
                    square(half, 0)
                for half in range(NH):
                    square(half, 2)
                    high_q(0, half)
                for half in range(NH):
                    high_k(0, half, 4)
                for half in range(NH):
                    copy_vt(half, 5)
                for part in range(2):
                    high_v(0, part)

                def sigmoids(it, n):
                    e, tb = SCORE_STEPS[n]
                    if n == 0:
                        act.wait_ge(q_scale_ready, it + 1)
                    act.wait_ge(z_done, NSC * it + n + 1)
                    act.wait_ge(row_ready, NSC * it + n + 1)
                    width = (tb + 1) * P
                    scale = [q_scale[:, x, 2 * tb + e:2 * tb + e + 1] for x in range(2)]
                    nc.scalar.activation(rest[:, n % 2, 0:width], Z[n % 2][:, 0:width], ACT.Sigmoid, scale=scale[0])
                    nc.scalar.activation(beta[:, n % 2, 0:width], Z[n % 2][:, 0:width], ACT.Sigmoid,
                                         scale=scale[1]).then_inc(z_free, 1)

                def wt_high(it, m):
                    e, g, j = WEIGHT_STEPS[m]
                    a = max(j - 4 * g, 0) * P
                    act.wait_ge(t_done, t_uses(it) + m + 1 + NWT)
                    act.wait_ge(av_done, NWT * it + m + 1)
                    nc.scalar.copy(wt_hi[:, m % 2, a:HALF], T[:, a:HALF]).then_inc(hi_ready, 1)

                def copy_o(it, e, g):
                    m = WEIGHT_STEPS.index((e, g, 4 * g + 3))
                    act.wait_ge(av_done, 2 + NWT * it + m + 1)
                    nc.scalar.copy(o_low[:], O[SB_DH:P, :]).then_inc(half_copied, 1)

                def body(it, last):
                    for s in range(SLOTS):
                        m = s - WEIGHT_SLOT
                        if 0 <= m < NWT:
                            wt_high(it, m)
                        if s in SCORE_SLOT:
                            sigmoids(it, SCORE_SLOT.index(s))
                        if not last:
                            if s in (4, 8):
                                if s == 4:
                                    act.wait_ge(gs_out, 16 * (NH * it + 1))
                                square(s // 4 - 1, g_uses(it))
                            if s in (12, 16):
                                square(s // 4 - 3, g_uses(it) + 2)
                                high_q(it + 1, s // 4 - 3)
                            if s in (15, 19):
                                high_k(it + 1, (s - 15) // 4, g_uses(it) + 4)
                            if s in (20, 24):
                                copy_vt((s - 20) // 4, g_uses(it) + 5)
                            if s == V_SLOT[1] + 1:
                                high_v(it + 1, 0, NWT * it + (NWT - 4) + 2)
                            if s == 28:
                                gate(it, 0, g_uses(it) + 6)
                        elif s - LAST_LATER in (4, 8, 12, 16, 20, 24):
                            i = (s - LAST_LATER - 4) // 4
                            gate(PAIRS - 1 + i // 2, i % 2, g_uses(it) + i // 2)
                        if 0 <= m - 1 < NWT and WEIGHT_STEPS[m - 1][2] == 4 * WEIGHT_STEPS[m - 1][1] + 3:
                            copy_o(it, *WEIGHT_STEPS[m - 1][:2])
                    if not last:
                        high_v(it + 1, 1, NWT * (it + 1) + 2)
                        gate(it, 1, g_uses(it) + 6)
                rounds(act, PAIRS, body)

            @block.vector
            def _(dve):
                chain = Chain(dve, dve_step)
                for sem_ in (g_free[0], g_free[1], lo_ready, o_free):
                    dve.sem_inc(sem_, 1)
                dve.sem_inc(ot_out, 16)
                nc.vector.memset(rest[:], 1.0)
                dve.wait_ge(g_loaded, 64)
                nc.vector.tensor_tensor(gains[:, 0:1], gains[:, 0:1], gains[:, 1:2], ALU.mult).then_inc(gains_made, 1)
                dve.wait_ge(gains_made, 1)

                def copy_k(prep, half, use):
                    dve.wait_ge(sq_ready, 4 * prep + half + 1)
                    nc.vector.tensor_copy(k_new[:, half * HALF:(half + 1) * HALF], G[half][:]
                                          ).then_inc(g_free[half], 1)

                def low_q(prep, half):
                    dve.wait_ge(q_high, NH * prep + half + 1)
                    at = slice(half * HALF, (half + 1) * HALF)
                    nc.vector.tensor_tensor(q_st[:, 1, at], G[half][:], q_st[:, 0, at], ALU.subtract
                                            ).then_inc(g_free[half], 1)

                def copy_ms(x, half, use):
                    dve.wait_ge(g_done[half], use + 1)
                    nc.vector.tensor_scalar(ms[:, x, TT * half:TT * (half + 1)], G[half][:, 0:TT], EPS, None,
                                            ALU.add).then_inc(g_free[half], 1)

                def k_root(prep, use, part):
                    if part == 0:
                        chain.enter(SB_CHAIN * prep)
                        for half in range(NH):
                            dve.wait_ge(g_free[half], use + 2)
                        rsqrt_guess(nc, chain, ms[:, 0, :], rms[:, 0, :])
                    rsqrt_newton(nc, chain, ms[:, 0, :], rms[:, 0, :], tmp[:])

                def repeat_k_rs():
                    nc.vector.tensor_copy(k_rs[:].rearrange("p t (e d) -> p (t e) d", e=2),
                                          rms[:, 0, :, None].to_broadcast([P, TT * 2, SB_DH])).then_inc(k_rs_ready, 1)

                def q_root(use):
                    for half in range(NH):
                        dve.wait_ge(g_free[half], use + 2)
                    rsqrt(nc, chain, ms[:, 1, :], rms[:, 1, :], tmp[:])
                    for x in range(2):
                        ins = nc.vector.tensor_scalar(q_scale[:, x, :], rms[:, 1, :], (-1, 1)[x] * SB_DH ** -0.5,
                                                      None, ALU.mult)
                    ins.then_inc(q_scale_ready, 1)
                    assert chain.n == SB_CHAIN

                def scale_k(half, use):
                    dve.wait_ge(g_done[half], use + 1)
                    at = slice(half * HALF, (half + 1) * HALF)
                    nc.vector.scalar_tensor_tensor(k_new[:, at], k_new[:, at], gains[:, 0:1], G[half][:],
                                                   ALU.mult, ALU.mult).then_inc(g_free[half], 1)

                def low_k(prep, half):
                    dve.wait_ge(k_high, NH * prep + half + 1)
                    at = slice(half * HALF, (half + 1) * HALF)
                    nc.vector.tensor_tensor(k_st[:, 1, at], k_new[:, at], k_st[:, 0, at], ALU.subtract
                                            ).then_inc(split_done, 1)

                def sum_o(it, e, g):
                    dve.wait_ge(half_copied, 4 * it + 2 * e + g + 1)
                    if e == 0 and g == 0:
                        dve.wait_ge(ot_out, 16 * (it + 1))
                    nc.vector.tensor_tensor(ot[e * SB_DH:(e + 1) * SB_DH, g * HALF:(g + 1) * HALF],
                                            O[0:SB_DH, :], o_low[:], ALU.add).then_inc(o_free, 1)

                def low_v(prep, part):
                    dve.wait_ge(v_high, 2 * prep + part + 1)
                    at = [v[:, 4 * part:4 * part + 4, :, x, :] for x in range(2)]
                    nc.vector.tensor_tensor(at[1], v_block(part), at[0], ALU.subtract).then_inc(v_ready, 1)

                for half in range(NH):
                    copy_k(0, half, 0)
                for half in range(NH):
                    copy_ms(0, half, 1)
                for part in range(3):
                    k_root(0, 1, part)
                repeat_k_rs()
                for half in range(NH):
                    low_q(0, half)
                for half in range(NH):
                    copy_ms(1, half, 3)
                for half in range(NH):
                    scale_k(half, 4)
                for half in range(NH):
                    low_k(0, half)
                q_root(3)
                for part in range(2):
                    low_v(0, part)

                def row(it, n):
                    e, tb = SCORE_STEPS[n]
                    width, b = (tb + 1) * P, n % 2
                    dve.wait_ge(z_free, 2 + NSC * it + n + 1)
                    back = rest[:, b, width - 1::-1] if width == S + 1 else rest[:, b, 0:width][:, ::-1]
                    nc.vector.tensor_tensor_scan(back, back, back, 1.0, ALU.mult, ALU.bypass).then_inc(scanned, 1)

                def wt_low(it, m):
                    e, g, j = WEIGHT_STEPS[m]
                    a = max(j - 4 * g, 0) * P
                    dve.wait_ge(hi_ready, t_uses(it) + m + 1)
                    nc.vector.tensor_tensor(wt_lo[:, m % 2, a:HALF], T[:, a:HALF], wt_hi[:, m % 2, a:HALF],
                                            ALU.subtract).then_inc(lo_ready, 1)

                def body(it, last):
                    for s in range(SLOTS):
                        m = s - WEIGHT_SLOT
                        if 0 <= m < NWT:
                            wt_low(it, m)
                        if s - 1 in SCORE_SLOT:
                            row(it, SCORE_SLOT.index(s - 1))
                        if not last:
                            if s in (4, 8):
                                copy_k(it + 1, s // 4 - 1, g_uses(it))
                            if s in (12, 16):
                                low_q(it + 1, s // 4 - 3)
                            if s in MS_SLOT:
                                i = MS_SLOT.index(s)
                                copy_ms(i // 2, i % 2, g_uses(it) + 2 * (i // 2) + 1)
                            if s in (10, 11, 12):
                                k_root(it + 1, g_uses(it) + 1, s - 10)
                            if s == 13:
                                repeat_k_rs()
                            if s in SPREAD_SLOT:
                                scale_k(SPREAD_SLOT.index(s), g_uses(it) + 4)
                            if s in (15, 19):
                                low_k(it + 1, (s - 15) // 4)
                            if s == V_SLOT[1] + 1:
                                low_v(it + 1, 0)
                            if s == 29:
                                q_root(g_uses(it) + 3)
                        if 0 <= m - 1 < NWT and WEIGHT_STEPS[m - 1][2] == 4 * WEIGHT_STEPS[m - 1][1] + 3:
                            sum_o(it, *WEIGHT_STEPS[m - 1][:2])
                    if not last:
                        low_v(it + 1, 1)
                rounds(dve, PAIRS, body)


GLA_SLOTS = 48
CHUNKS = S // P
LEVELS = 8
GLA_UNITS = 6
GLA_TILES = GLA_UNITS * (GLA_HEADS + 1)
GLA_TASKS = 9
GLA_T = CHUNKS + 8
GLA_CHAIN = 13
N_MADE = 3 + 3 * (LEVELS - 1) + 1


def linear_attention(nc, c, hT, w_in, w2, gate_b, out_gain, ogla_t, gates_t, W, following):
    with ExitStack() as ctx:
        sb = lambda n, shape, dt=F32: ctx.enter_context(nc.sbuf_tensor(f"gla_{n}", shape, dt))
        ps = lambda n, shape: ctx.enter_context(nc.psum_tensor(f"gla_{n}", shape, F32))
        sem = lambda n: ctx.enter_context(nc.semaphore(f"gla_{n}"))
        lr_raw, lr_hi, lr_lo = sb("lr_raw", [P, KT, LR]), sb("lr_hi", [P, KT, LR], F32R), sb("lr_lo", [P, KT, LR], F32R)
        lr_t = sb("lr_t", [LR, S])
        w2_all, w2_h = sb("w2_all", [LR, GLA_HEADS * GLA_DK]), sb("w2_h", [LR, GLA_DK])
        gb_all, gb_h = sb("gb_all", [P, GLA_HEADS]), sb("gb_h", [P, 1])
        og = sb("og", [P, 2])
        mask = sb("mask", [P, LEVELS, P])
        keep = sb("keep", [P, S], BF16)
        q_new, k_new = sb("q_new", [P, S]), sb("k_new", [P, S])
        q_diag, k_diag = sb("q_diag", [P, S]), sb("k_diag", [P, S])
        X = sb("x", [P, LEVELS - 1, S])
        q_in, k_out = sb("q_in", [P, S]), sb("k_out", [P, S])
        C = sb("c", [P, S])
        E = sb("e", [P, 2, S])
        dec = sb("dec", [P, CHUNKS])
        vt = sb("vt", [P, 2, S])
        V = sb("v", [P, CHUNKS, GLA_DV])
        RT = sb("rt", [P, 2, S])
        masked = E[:, 0, :].rearrange("p (l i) -> p l i", l=LEVELS)
        sc = sb("sc", [P, 2, P])
        kt = sb("kt", [P, 2, P])
        state = sb("state", [P, GLA_DV])
        obuf = sb("obuf", [P, CHUNKS, GLA_DV])
        junk = E[:, 1, 0:GLA_DV]
        ssq, stat = sb("ssq", [P, CHUNKS]), sb("stat", [P, 3, CHUNKS])
        G = [ps(f"g{h}", [P, HALF]) for h in range(NH)]
        SC = ps("s", [P, LEVELS, P])
        O = [ps(f"o{b}", [P, HALF]) for b in range(2)]
        ST = ps("st", [P, HALF])
        T = ps("t", [P, HALF])

        small_loaded = sem("small_loaded")
        made = sem("made")
        lr_split = sem("lr_split")
        g_done = [sem(f"g_done{h}") for h in range(NH)]
        g_free = [sem(f"g_free{h}") for h in range(NH)]
        r_sig = sem("r_sig")
        r_ready = sem("r_ready")
        w2_ready = sem("w2_ready")
        s_done, s_free = sem("s_done"), sem("s_free")
        abs_ready, log_ready = sem("abs_ready"), sem("log_ready")
        d_ready, e_ready = sem("d_ready"), sem("e_ready")
        f_ready = sem("f_ready")
        sc_ready = sem("sc_ready")
        t_done, t_free = sem("t_done"), sem("t_free")
        o_done, o_free = sem("o_done"), sem("o_free")
        ssq_ready = sem("ssq_ready")
        st_done, st_free = sem("st_done"), sem("st_free")
        on_ready = sem("on_ready")
        o_out = sem("o_out")
        gate_out = [sem(f"gate_out{h}") for h in range(NH)]
        dve_step = sem("dve_step")

        g_uses = lambda it: 7 + GLA_UNITS * it
        t_uses = lambda it: 4 + GLA_T * it
        s_uses = lambda it: 1 + (CHUNKS + 1) * it
        N_LAST_GATES = 6

        def blocks(t, half):
            return t.rearrange("p (b a h) -> p b a h", a=2, h=half)

        with nc.Block() as block:
            @block.sync
            def _(sp):
                sp.dma_start(lr_raw[:], w_in.rearrange("(k p) c -> p k c", p=P)[:, :, GLLR:GLLR + LR]
                             ).then_inc(small_loaded, 16)
                sp.dma_start(w2_all[:], w2).then_inc(small_loaded, 16)
                for dst, src in ((gb_all, gate_b), (og, out_gain)):
                    for n in range(dst.shape[1]):
                        sp.dma_start(dst[:, n:n + 1], src[:, n * P:(n + 1) * P].rearrange("a p -> p a")
                                     ).then_inc(small_loaded, 16)

                cols = [(GLQ, GLA_DK), (GLK, GLA_DK), (GLV, GLA_DV), (GLV + P, GLA_DV), (GLR, GLA_DV), (GLR + P, GLA_DV)]
                for n, (col, _) in enumerate(cols):
                    if n >= 2:
                        W.load(sp, 0, n, weight_cols(w_in, col))

                def body(it, last):
                    for n, (col, width) in enumerate(cols):
                        src = GATE + (10 + n) * P if last else it * width + (col + width)
                        W.load(sp, GLA_UNITS * it, GLA_UNITS + n, weight_cols(w_in, src))
                    for n in range(4):
                        d, cg = n // 2, n % 2
                        sp.wait_ge(t_free, t_uses(it) + CHUNKS + n + 1)
                        sp.dma_start(ogla_t[ds(it * GLA_DV + d * P, P), cg * HALF:(cg + 1) * HALF],
                                     RT[:, d, cg * HALF:(cg + 1) * HALF]).then_inc(o_out, 16)
                    if last:
                        for n in range(2):
                            W.load(sp, GLA_TILES, n, following[n])
                rounds(sp, GLA_HEADS, body)
                sp.wait_ge(o_out, 16 * 4 * GLA_HEADS)
                for half in range(NH):
                    sp.wait_ge(gate_out[half], 16 * N_LAST_GATES)

            @block.gpsimd
            def _(pool):
                chain = Chain(pool, made)
                chain.link(nc.gpsimd.memset(mask[:], 0.0))
                chain.link(nc.gpsimd.memset(keep[:], 1.0))
                chain.link(nc.gpsimd.memset(keep[:].rearrange("p (c t) -> p c t", t=P)[:, :, 0:1], 0.0))
                for lv in range(LEVELS - 1):
                    half = 1 << lv
                    second = blocks(mask[:, lv, :], half)[:, :, 1, :]
                    chain.link(nc.gpsimd.memset(second, 1.0))
                    pattern = lambda sign: [[sign * 2 * half, P // (2 * half)], [0, half]]
                    chain.link(nc.gpsimd.affine_select(out=second, in_=second, compare_op=ALU.is_ge, fill=0.0,
                                                       base=0, pattern=pattern(-1), channel_multiplier=1))
                    chain.link(nc.gpsimd.affine_select(out=second, in_=second, compare_op=ALU.is_ge, fill=0.0,
                                                       base=half - 1, pattern=pattern(1), channel_multiplier=-1))
                diag = mask[:, LEVELS - 1, :]
                chain.link(nc.gpsimd.affine_select(out=diag, in_=diag, compare_op=ALU.not_equal, fill=1.0,
                                                   base=0, pattern=[[-1, P]], channel_multiplier=1))
                assert chain.n == N_MADE
                for n in range(2, GLA_UNITS):
                    W.split(pool, 0, n, (g_done[1], n if n > 2 else 1))

                def body(it, last):
                    for n in range(GLA_UNITS):
                        W.split(pool, GLA_UNITS * it, GLA_UNITS + n, (g_done[1], GLA_UNITS * it + (GLA_UNITS + n)))
                rounds(pool, GLA_HEADS, body)
                W.split(pool, GLA_TILES, 0, (g_done[1], GLA_TILES))

            @block.tensor
            def _(pe):
                def fill(lot, step, eighth, use):
                    half, part = eighth // 4, eighth % 4
                    if eighth == 0:
                        W.take(pe, lot, step)
                    if part == 0:
                        pe.wait_ge(g_free[half], use + 1)
                    ins = project_part(nc, G[half][:], W.tile(step), hT, half, part, 4)
                    if part == 3:
                        ins.then_inc(g_done[half], 1)

                def transpose_v(n, use):
                    d, cg = n // 2, n % 2
                    need(pe, t_free, use)
                    for q in range(4):
                        j = 4 * cg + q
                        ins = nc.tensor.transpose(T[:, q * P:(q + 1) * P], vt[:, d, j * P:(j + 1) * P], c["ident"][:])
                    ins.then_inc(t_done, 1)

                def logits(prep, use):
                    pe.wait_ge(w2_ready, prep + 1)
                    pe.wait_ge(s_free, use + 1)
                    flat = SC[:].rearrange("p l i -> p (l i)")
                    for half in range(NH):
                        at = slice(half * HALF, (half + 1) * HALF)
                        ins = nc.tensor.matmul(flat[:, at], w2_h[:], lr_t[:, at], start=True, stop=True)
                    ins.then_inc(s_done, 1)

                def low_rank():
                    pe.wait_ge(lr_split, 2)
                    for half in range(NH):
                        pe.wait_ge(g_free[half], 2)
                        steps = [(a, b, k) for a, b in ((lr_hi, hT[0]), (lr_hi, hT[1]), (lr_lo, hT[0])) for k in range(KT)]
                        for n, (a, b, k) in enumerate(steps):
                            ins = nc.tensor.matmul(G[half][0:LR, :], a[:, k, :], b[:, k, half * HALF:(half + 1) * HALF],
                                                   start=(n == 0), stop=(n == len(steps) - 1))
                        ins.then_inc(g_done[half], 1)

                for n in range(GLA_UNITS):
                    for eighth in range(8):
                        fill(0, n, eighth, n + (n > 0))
                        if n == 5 and eighth % 2 == 0:
                            transpose_v(eighth // 2, eighth // 2)
                    if n == 0:
                        low_rank()
                    if n == 1:
                        for half in range(NH):
                            pe.wait_ge(g_free[half], 3)
                        logits(0, 0)
                def scores(it, ch):
                    if ch == 0:
                        pe.wait_ge(f_ready, GLA_TASKS * (it + 1))
                    at = slice(ch * P, (ch + 1) * P)
                    pe.wait_ge(t_free, t_uses(it) + ch)
                    nc.tensor.transpose(T[:, 0:P], k_out[:, at], c["ident"][:]).then_inc(t_done, 1)
                    pe.wait_ge(s_free, s_uses(it) + ch + 1)
                    for lv in range(LEVELS - 1):
                        nc.tensor.matmul(SC[:, lv, :], X[:, lv, at], X[:, lv, at], start=True, stop=True)
                    nc.tensor.matmul(SC[:, LEVELS - 1, :], k_diag[:, at], q_diag[:, at],
                                     start=True, stop=True).then_inc(s_done, 1)

                def outputs(it, ch):
                    at, o = slice(ch * P, (ch + 1) * P), O[ch % 2][:, 0:GLA_DV]
                    pe.wait_ge(o_free, CHUNKS * it + ch + 1)
                    if ch:
                        pe.wait_ge(st_free, (CHUNKS - 1) * it + ch + 1)
                        nc.tensor.matmul(o, q_in[:, at], state[:], start=True, stop=False)
                    pe.wait_ge(sc_ready, CHUNKS * it + ch + 1)
                    nc.tensor.matmul(o, sc[:, ch % 2, :], V[:, ch, :], start=(ch == 0), stop=True).then_inc(o_done, 1)
                    if ch < CHUNKS - 1:
                        pe.wait_ge(t_free, t_uses(it) + ch + 1)
                        pe.wait_ge(st_free, (CHUNKS - 1) * it + ch + 1)
                        nc.tensor.matmul(ST[:, 0:GLA_DV], kt[:, ch % 2, :], V[:, ch, :],
                                         start=True, stop=True).then_inc(st_done, 1)

                def transpose_o(it, n):
                    d, cg = n // 2, n % 2
                    if n == 0:
                        pe.wait_ge(on_ready, it + 1)
                    pe.wait_ge(t_free, t_uses(it) + CHUNKS + n)
                    for q in range(4):
                        ins = nc.tensor.transpose(T[:, q * P:(q + 1) * P], obuf[:, 4 * cg + q, d * P:(d + 1) * P],
                                                  c["ident"][:])
                    ins.then_inc(t_done, 1)

                def body(it, last):
                    for s in range(GLA_SLOTS):
                        if s < 3 * CHUNKS and s % 3 == 0:
                            scores(it, s // 3)
                        if s < 3 * CHUNKS and s % 3 == 2:
                            outputs(it, s // 3)
                        if s in (27, 28, 29, 30):
                            transpose_o(it, s - 27)
                        if not last:
                            if s == 25:
                                logits(it + 1, s_uses(it) + CHUNKS)
                            if s in (33, 34, 35, 36):
                                if s == 33:
                                    for half in range(NH):
                                        pe.wait_ge(g_free[half], g_uses(it) + 5)
                                transpose_v(s - 33, t_uses(it) + CHUNKS + 4 + s - 33)
                        fill(GLA_UNITS * it, GLA_UNITS + s // 8, s % 8, g_uses(it) + s // 8)
                rounds(pe, GLA_HEADS, body)

            @block.scalar
            def _(act):
                for sem_ in (o_free, o_free, ssq_ready):
                    act.sem_inc(sem_, 1)

                def copy_vt(d, half, use):
                    act.wait_ge(g_done[half], use + 1)
                    nc.scalar.copy(vt[:, d, half * HALF:(half + 1) * HALF], G[half][:]).then_inc(g_free[half], 1)

                def copy_r(d, half, use):
                    act.wait_ge(g_done[half], use + 1)
                    nc.scalar.copy(RT[:, d, half * HALF:(half + 1) * HALF], G[half][:]).then_inc(g_free[half], 1)

                def sigmoid_r(d):
                    nc.scalar.activation(vt[:, d, :], RT[:, d, :], ACT.Sigmoid).then_inc(r_sig, 1)

                def copy_v(n, use):
                    d, cg = n // 2, n % 2
                    act.wait_ge(t_done, use + 1)
                    nc.scalar.copy(V[:, 4 * cg:4 * cg + 4, d * P:(d + 1) * P],
                                   T[:].rearrange("p (j n) -> p j n", j=4)).then_inc(t_free, 1)

                def log_sigmoid(prep, use):
                    act.wait_ge(s_done, use + 1)
                    e, flat = E[:, 0, :], SC[:].rearrange("p l i -> p (l i)")
                    nc.scalar.activation(e, flat, ACT.Abs, bias=gb_h[:]).then_inc(abs_ready, 1)
                    act.wait_ge(abs_ready, 2 * prep + 1)
                    nc.scalar.activation(e, e, ACT.Exp, scale=-1.0).then_inc(abs_ready, 1)
                    act.wait_ge(abs_ready, 2 * prep + 2)
                    nc.scalar.activation(e, e, ACT.Ln, bias=1.0).then_inc(log_ready, 1)

                def exponential(prep, task):
                    act.wait_ge(d_ready, GLA_TASKS * prep + task + 1)
                    e = E[:, task % 2, :]
                    if task == 0:
                        nc.scalar.activation(dec[:], C[:].rearrange("p (c t) -> p c t", t=P)[:, :, P - 1],
                                             ACT.Exp, scale=1.0 / TAU)
                    nc.scalar.activation(e, C[:] if task == 0 else e, ACT.Exp,
                                         scale=1.0 / TAU).then_inc(e_ready, 1)

                for half in range(NH):
                    act.wait_ge(g_done[half], 2)
                    nc.scalar.copy(lr_t[:, half * HALF:(half + 1) * HALF], G[half][0:LR, :]).then_inc(g_free[half], 1)
                log_sigmoid(0, 0)
                for task in range(GLA_TASKS):
                    exponential(0, task)
                    if task in (0, 3):
                        for half in range(NH):
                            copy_vt(task // 3, half, 3 + task // 3)
                    if task == 6:
                        for half in range(NH):
                            copy_r(0, half, 5)
                    if task in (7, 8):
                        for n in range(2):
                            copy_v(2 * (task - 7) + n, 2 * (task - 7) + n)
                for half in range(NH):
                    copy_r(1, half, 6)

                def copy_kt(it, ch):
                    act.wait_ge(t_done, t_uses(it) + ch + 1)
                    nc.scalar.copy(kt[:, ch % 2, :], T[:, 0:P]).then_inc(t_free, 1)

                def copy_o(it, ch):
                    act.wait_ge(o_done, CHUNKS * it + ch + 1)
                    nc.scalar.copy(obuf[:, ch, :], O[ch % 2][:, 0:GLA_DV]).then_inc(o_free, 1)
                    act.wait_ge(o_free, CHUNKS * it + ch + 3)
                    act.wait_ge(ssq_ready, CHUNKS * it + ch + 1)
                    nc.scalar.activation(junk, obuf[:, ch, :], ACT.Square,
                                         accum_out=ssq[:, ch:ch + 1]).then_inc(ssq_ready, 1)

                def send_gate(n, half, use):
                    at = slice(half * HALF, (half + 1) * HALF)
                    act.wait_ge(g_done[half], use + 1)
                    need(act, gate_out[half], 16 * n)
                    nc.scalar.activation(q_new[:, at], G[half][:], ACT.Sigmoid).then_inc(g_free[half], 1)
                    act.wait_ge(g_free[half], use + 2)
                    act.dma_start(gates_t[(10 + n) * P:(11 + n) * P, at], q_new[:, at]).then_inc(gate_out[half], 16)

                def body(it, last):
                    for s in range(GLA_SLOTS):
                        if s < 3 * CHUNKS and s % 3 == 0:
                            copy_kt(it, s // 3)
                        if 3 <= s <= 3 * CHUNKS and s % 3 == 0:
                            copy_o(it, s // 3 - 1)
                        if s in (1, 4):
                            if s == 1:
                                for half in range(NH):
                                    act.wait_ge(g_free[half], g_uses(it) + 1)
                            sigmoid_r(s // 4)
                        if not last:
                            if s in (20, 24, 28, 32):
                                i = (s - 20) // 4
                                if i == 0:
                                    act.wait_ge(r_ready, 2 * (it + 1))
                                copy_vt(i // 2, i % 2, g_uses(it) + 2 + i // 2)
                            if s == 26:
                                log_sigmoid(it + 1, s_uses(it) + CHUNKS)
                            if s in (33, 34, 35, 36):
                                copy_v(s - 33, t_uses(it) + CHUNKS + 4 + s - 33)
                            if s in (31, 32, 34, 37, 38, 39, 41, 42, 43):
                                exponential(it + 1, (31, 32, 34, 37, 38, 39, 41, 42, 43).index(s))
                            if s in (36, 40, 44):
                                i = (s - 36) // 4
                                if i == 0:
                                    act.wait_ge(o_out, 16 * 4 * (it + 1))
                                copy_r(i // 2, i % 2, g_uses(it) + 4 + i // 2)
                        elif s >= 4 and s % 4 == 0:
                            i = s // 4 - 1
                            send_gate(i // 2, i % 2, g_uses(it) + i // 2)
                    if last:
                        send_gate(N_LAST_GATES - 1, 1, g_uses(it) + N_LAST_GATES - 1)
                    else:
                        copy_r(1, 1, g_uses(it) + 5)
                rounds(act, GLA_HEADS, body)

            @block.vector
            def _(dve):
                chain = Chain(dve, dve_step)
                for sem_ in (g_free[0], g_free[1], s_free, st_free):
                    dve.sem_inc(sem_, 1)
                dve.wait_ge(small_loaded, 16 * (2 + GLA_HEADS + 2))
                nc.vector.tensor_copy(lr_hi[:], lr_raw[:]).then_inc(lr_split, 1)
                dve.wait_ge(lr_split, 1)
                nc.vector.tensor_tensor(lr_lo[:], lr_raw[:], lr_hi[:], ALU.subtract).then_inc(lr_split, 1)
                def copy_q(half, use):
                    dve.wait_ge(g_done[half], use + 1)
                    nc.vector.tensor_scalar(q_new[:, half * HALF:(half + 1) * HALF], G[half][:], GLA_DK ** -0.5,
                                            None, ALU.mult).then_inc(g_free[half], 1)

                def copy_k(half, use):
                    dve.wait_ge(g_done[half], use + 1)
                    nc.vector.tensor_copy(k_new[:, half * HALF:(half + 1) * HALF], G[half][:]
                                          ).then_inc(g_free[half], 1)

                def head_gate(prep):
                    nc.vector.tensor_copy(w2_h[:], w2_all[:, ds(prep * GLA_DK, GLA_DK)])
                    nc.vector.tensor_copy(gb_h[:], gb_all[:, ds(prep, 1)]).then_inc(w2_ready, 1)

                def cumulate(prep, use):
                    dve.wait_ge(s_done, use + 1)
                    dve.wait_ge(abs_ready, 2 * prep + 1)
                    dve.wait_ge(w2_ready, prep + 1)
                    flat = SC[:].rearrange("p l i -> p (l i)")
                    e0, e1 = E[:, 0, :], E[:, 1, :]
                    nc.vector.tensor_scalar(e1, flat, gb_h[:], 0.0, ALU.add, ALU.min).then_inc(s_free, 1)
                    dve.wait_ge(log_ready, prep + 1)
                    dve.wait_ge(s_free, use + 2)
                    chain.link(nc.vector.tensor_tensor(e1, e1, e0, ALU.subtract))
                    nc.vector.tensor_tensor_scan(C[:], keep[:], e1, 0.0, ALU.mult, ALU.add).then_inc(d_ready, 1)
                    dve.wait_ge(d_ready, GLA_TASKS * prep + 1)

                def exponents(prep, task):
                    e = E[:, task % 2, :]
                    if task >= 2:
                        dve.wait_ge(f_ready, GLA_TASKS * prep + task - 1)
                    if task == 1:
                        view = lambda t: t.rearrange("p (c t) -> p c t", t=P)
                        nc.vector.tensor_tensor(view(e), view(C[:])[:, :, P - 1:P].to_broadcast([P, CHUNKS, P]),
                                                view(C[:]), ALU.subtract).then_inc(d_ready, 1)
                        return
                    half = 1 << (task - 2)
                    cb, eb = blocks(C[:], half), blocks(e, half)
                    mid = cb[:, :, 0, half - 1:half].to_broadcast([P, S // (2 * half), half])
                    nc.vector.tensor_tensor(eb[:, :, 0, :], mid, cb[:, :, 0, :], ALU.subtract)
                    nc.vector.tensor_tensor(eb[:, :, 1, :], cb[:, :, 1, :], mid, ALU.subtract).then_inc(d_ready, 1)

                def factors(prep, task):
                    dve.wait_ge(e_ready, GLA_TASKS * prep + task + 1)
                    e = E[:, task % 2, :]
                    if task == 0:
                        ins = nc.vector.tensor_tensor(q_in[:], q_new[:], e, ALU.mult)
                    elif task == 1:
                        ins = nc.vector.tensor_tensor(k_out[:], k_new[:], e, ALU.mult)
                    else:
                        half = 1 << (task - 2)
                        eb, xb = blocks(e, half), blocks(X[:, task - 2, :], half)
                        nc.vector.tensor_tensor(xb[:, :, 0, :], eb[:, :, 0, :], blocks(k_new[:], half)[:, :, 0, :], ALU.mult)
                        ins = nc.vector.tensor_tensor(xb[:, :, 1, :], eb[:, :, 1, :], blocks(q_new[:], half)[:, :, 1, :],
                                                      ALU.mult)
                    ins.then_inc(f_ready, 1)

                def diagonal():
                    nc.vector.tensor_copy(q_diag[:], q_new[:])
                    nc.vector.tensor_copy(k_diag[:], k_new[:])

                def gate_r(it, d):
                    dve.wait_ge(r_sig, 2 * it + d + 1)
                    nc.vector.scalar_tensor_tensor(RT[:, d, :], RT[:, d, :], og[:, d:d + 1], vt[:, d, :], ALU.mult,
                                                   ALU.mult).then_inc(r_ready, 1)

                head_gate(0)
                for half in range(NH):
                    copy_q(half, 0)
                for half in range(NH):
                    copy_k(half, 2)
                dve.wait_ge(made, N_MADE)
                chain.enter(0)
                cumulate(0, 0)
                diagonal()
                for task in range(GLA_TASKS):
                    if task + 1 < GLA_TASKS:
                        exponents(0, task + 1)
                    factors(0, task)
                first = chain.n

                def mask_scores(it, ch):
                    dve.wait_ge(s_done, s_uses(it) + ch + 1)
                    nc.vector.tensor_tensor(masked, SC[:], mask[:], ALU.mult).then_inc(s_free, 1)
                    dve.wait_ge(s_free, s_uses(it) + ch + 2)
                    nc.vector.tensor_reduce(sc[:, ch % 2, :], masked.rearrange("p l i -> p i l"), AX_X,
                                            ALU.add).then_inc(sc_ready, 1)

                def update(it, ch):
                    dve.wait_ge(st_done, (CHUNKS - 1) * it + ch + 1)
                    if ch == 0:
                        ins = nc.vector.tensor_copy(state[:], ST[:, 0:GLA_DV])
                    else:
                        dve.wait_ge(st_free, (CHUNKS - 1) * it + ch + 1)
                        ins = nc.vector.scalar_tensor_tensor(state[:], state[:], dec[:, ch:ch + 1], ST[:, 0:GLA_DV],
                                                             ALU.mult, ALU.add)
                    ins.then_inc(st_free, 1)

                def normalise(it):
                    dve.wait_ge(ssq_ready, CHUNKS * (it + 1) + 1)
                    ms, y, u = stat[:, 0, :], stat[:, 1, :], stat[:, 2, :]
                    chain.link(nc.vector.tensor_scalar(ms, ssq[:], 1.0 / GLA_DV, EPS, ALU.mult, ALU.add))
                    rsqrt(nc, chain, ms, y, u)
                    for ch in range(CHUNKS):
                        ins = nc.vector.tensor_scalar(obuf[:, ch, :], obuf[:, ch, :], y[:, ch:ch + 1], None, ALU.mult)
                    ins.then_inc(on_ready, 1)

                def gate_o(it, n):
                    d, cg = n // 2, n % 2
                    dve.wait_ge(t_done, t_uses(it) + CHUNKS + n + 1)
                    r = RT[:, d, cg * HALF:(cg + 1) * HALF]
                    dve.wait_ge(r_ready, 2 * (it + 1))
                    nc.vector.tensor_tensor(r, T[:], r, ALU.mult).then_inc(t_free, 1)

                def body(it, last):
                    chain.enter(GLA_CHAIN * it + first)
                    for s in range(GLA_SLOTS):
                        if s < 3 * (CHUNKS - 1) + 1 and s % 3 == 0 and s:
                            update(it, s // 3 - 1)
                        if s < 3 * CHUNKS and s % 3 == 0:
                            mask_scores(it, s // 3)
                        if s in (2, 5):
                            gate_r(it, s // 3)
                        if s == 25:
                            normalise(it)
                        if s in (27, 28, 29, 30):
                            gate_o(it, s - 27)
                        if not last:
                            if s in (4, 8):
                                copy_q(s // 4 - 1, g_uses(it))
                            if s in (12, 16):
                                copy_k(s // 4 - 3, g_uses(it) + 1)
                            if s == 24:
                                head_gate(it + 1)
                            if s == 31:
                                cumulate(it + 1, s_uses(it) + CHUNKS)
                                exponents(it + 1, 1)
                                diagonal()
                            if s == 32:
                                factors(it + 1, 0)
                                exponents(it + 1, 2)
                            if s in (34, 37, 38, 39, 41, 42, 43):
                                task = (34, 37, 38, 39, 41, 42, 43).index(s) + 1
                                factors(it + 1, task)
                                if task + 2 < GLA_TASKS:
                                    exponents(it + 1, task + 2)
                    if not last:
                        factors(it + 1, GLA_TASKS - 1)
                        assert chain.n == GLA_CHAIN, chain.n
                rounds(dve, GLA_HEADS, body)


def merge_and_project(nc, o_t, osb_out, gates_t, weights, w_out, x, y, W, merged, ssq):
    OUTS = TT * NH
    ROUND = 2 * NH + OUTS
    with ExitStack() as ctx:
        sb = lambda n, shape, dt=F32: ctx.enter_context(nc.sbuf_tensor(f"mp_{n}", shape, dt))
        sem = lambda n: ctx.enter_context(nc.semaphore(f"mp_{n}"))
        parts = [[sb(f"o{b}_{part}", [P, KT, S], F32R) for part in ("hi", "lo")] for b in range(2)]
        sig = sb("sig", [P, 2, S])
        m_hi, m_lo = sb("m_hi", [P, S], F32R), sb("m_lo", [P, S], F32R)
        ps = lambda n: ctx.enter_context(nc.psum_tensor(f"mp_{n}", [P, HALF], F32))
        acc = [[ps(f"acc{b}{h}") for h in range(NH)] for b in range(2)]
        outs = [ps(f"out{i}") for i in range(4)]
        o_loaded = [sem(f"o_loaded{i}") for i in range(TT)]
        hi_done, lo_done = sem("hi_done"), sem("lo_done")
        x_loaded = sem("x_loaded")
        sq_done = sem("sq_done")
        sig_loaded = [sem(f"sig_loaded{b}") for b in range(2)]
        pe_done = sem("pe_done")
        acc_free = sem("acc_free")
        m_ready = sem("m_ready")
        m_high, m_split = sem("m_high"), sem("m_split")
        out_free = sem("out_free")
        base = lambda j: 2 * NH + ROUND * j
        row_tiles = [(b, k) for b in range(2) for k in range(KT)]

        def steps(eng, prologue, step):
            prologue()
            with eng.Fori(0, (KT - 1) // 2, 1) as i:
                for u in range(2):
                    step(i, u, False)
            step((KT - 1) // 2, 0, False)
            step((KT - 1) // 2, 1, True)

        with nc.Block() as block:
            @block.sync
            def _(sp):
                def load_sig(b, row, used=None):
                    src = gates_t[ds(row + b * D, P), :]
                    if used is not None:
                        sp.wait_ge(*used)
                    sp.dma_start(sig[:, b, :], src).then_inc(sig_loaded[b], 16)

                def prologue():
                    for n, (b, k) in enumerate(row_tiles):
                        if n == TT - 1:
                            sp.wait_ge(osb_out, 16 * (PAIRS + 1))
                        if n >= TT:
                            sp.wait_ge(lo_done, n - TT + 1)
                        sp.dma_start(y[:, n % TT, :], o_t[b][k * P:(k + 1) * P, :]).then_inc(o_loaded[n % TT], 16)
                        if n == TT + 1:
                            W.load(sp, 0, 2, weight_cols(weights[0], P))
                        if n == TT + 5:
                            W.load(sp, 0, 3, w_out[0:P, :].rearrange("p (k c) -> p k c", k=KT))
                    for b in range(2):
                        load_sig(b, 0)
                    for i in range(TT):
                        sp.wait_ge(lo_done, TT + i + 1)
                        sp.dma_start(y[:, i, :], x[i * P:(i + 1) * P, :]).then_inc(x_loaded, 16)

                def step(i, u, last):
                    if last:
                        return
                    j, lot, n = 2 * i + u, 6 * i, 4 + 3 * u
                    row = lambda ahead: i * (2 * P) + (u + ahead) * P
                    W.load(sp, lot, n, weight_cols(weights[1], row(1)))
                    load_sig(0, row(1), (acc_free, 4 + 4 * j + NH))
                    load_sig(1, row(1), (m_ready, NH * (j + 1)))
                    if not (isinstance(j, int) and j == KT - 2):
                        W.load(sp, lot, n + 1, weight_cols(weights[0], row(2)))
                        n += 1
                    W.load(sp, lot, n + 1, w_out[ds(row(1), P), :].rearrange("p (k c) -> p k c", k=KT))
                steps(sp, prologue, step)

            @block.gpsimd
            def _(pool):
                def step(i, u, last):
                    j = 2 * i + u
                    for n, done in enumerate((base(j) - 2, base(j), base(j) + NH)[:1 if last else 3]):
                        W.split(pool, 6 * i, 2 + 3 * u + n, (pe_done, done))
                steps(pool, lambda: None, step)

            @block.scalar
            def _(act):
                def high_m(j):
                    for half in range(NH):
                        at = slice(half * HALF, (half + 1) * HALF)
                        act.wait_ge(m_ready, NH * j + half + 1)
                        nc.scalar.copy(m_hi[:, at], merged[:, at]).then_inc(m_high, 1)

                def prologue():
                    for n, (b, k) in enumerate(row_tiles):
                        act.wait_ge(o_loaded[n % TT], 16 * (n // TT + 1))
                        nc.scalar.copy(parts[b][0][:, k, :], y[:, n % TT, :]).then_inc(hi_done, 1)
                    high_m(0)

                def square(t):
                    act.wait_ge(out_free, 4 + OUTS * (KT - 1) + NH * (t + 1))
                    act.wait_ge(*((sq_done, t) if t else (m_split, NH * KT)))
                    nc.scalar.activation(merged[:], y[:, t, :], ACT.Square, accum_out=ssq[:, t:t + 1]).then_inc(sq_done, 1)

                def step(i, u, last):
                    if not last:
                        high_m(2 * i + (u + 1))
                        return
                    for t in range(TT):
                        square(t)
                steps(act, prologue, step)

            @block.vector
            def _(dve):
                for sem_ in (acc_free, out_free):
                    dve.sem_inc(sem_, 4)

                def sb_term(at, j, first=False):
                    dve.wait_ge(sig_loaded[0], 16 * (j + 1))
                    if not first:
                        dve.wait_ge(m_split, NH * j)
                    for half in range(NH):
                        cols = slice(half * HALF, (half + 1) * HALF)
                        dve.wait_ge(pe_done, at + half + 1)
                        nc.vector.tensor_tensor(merged[:, cols], acc[0][half][:], sig[:, 0, cols], ALU.mult
                                                ).then_inc(acc_free, 1)

                def merge(at, j):
                    dve.wait_ge(sig_loaded[1], 16 * (j + 1))
                    for half in range(NH):
                        cols = slice(half * HALF, (half + 1) * HALF)
                        dve.wait_ge(pe_done, at + half + 1)
                        nc.vector.tensor_tensor(sig[:, 1, cols], acc[1][half][:], sig[:, 1, cols], ALU.mult
                                                ).then_inc(acc_free, 1)
                        dve.wait_ge(acc_free, 4 + 4 * j + NH + half + 1)
                        nc.vector.tensor_tensor(merged[:, cols], merged[:, cols], sig[:, 1, cols], ALU.add
                                                ).then_inc(m_ready, 1)
                    for half in range(NH):
                        cols = slice(half * HALF, (half + 1) * HALF)
                        dve.wait_ge(m_high, NH * j + half + 1)
                        nc.vector.tensor_tensor(m_lo[:, cols], merged[:, cols], m_hi[:, cols], ALU.subtract
                                                ).then_inc(m_split, 1)

                def prologue():
                    for n, (b, k) in enumerate(row_tiles):
                        dve.wait_ge(hi_done, n + 1)
                        nc.vector.tensor_tensor(parts[b][1][:, k, :], y[:, n % TT, :], parts[b][0][:, k, :],
                                                ALU.subtract).then_inc(lo_done, 1)
                    sb_term(0, 0, first=True)
                    merge(NH, 0)
                    dve.wait_ge(x_loaded, 16 * TT)

                def step(i, u, last):
                    j = 2 * i + u
                    first = base(j) + (0 if last else NH)
                    if not last:
                        sb_term(base(j), j + 1)
                    for o in range(OUTS):
                        at = y[:, o // NH, (o % NH) * HALF:(o % NH + 1) * HALF]
                        dve.wait_ge(pe_done, first + o + 1)
                        nc.vector.tensor_tensor(at, outs[o % 4][:], at, ALU.add).then_inc(out_free, 1)
                    if not last:
                        merge(base(j) + NH + OUTS, j + 1)
                steps(dve, prologue, step)

            @block.tensor
            def _(pe):
                def unit(b, lot, n, j):
                    W.take(pe, lot, n)
                    for half in range(NH):
                        pe.wait_ge(acc_free, 4 * j + NH * b + half + 1)
                        project_part(nc, acc[b][half][:], W.tile(n), parts[b], half, 0, 1).then_inc(pe_done, 1)

                def first_unit(b):
                    W.take(pe, 0, b)
                    pe.wait_ge(acc_free, NH * b + NH)
                    w = W.tile(b)
                    for k in range(KT):
                        pe.wait_ge(lo_done, KT * b + k + 1)
                        for half in range(NH):
                            for n, (wp, xp) in enumerate(((0, 0), (0, 1), (1, 0))):
                                ins = nc.tensor.matmul(acc[b][half][:], w[wp][:, k, :],
                                                       parts[b][xp][:, k, half * HALF:(half + 1) * HALF],
                                                       start=(k == 0 and n == 0), stop=(k == KT - 1 and n == 2))
                            if k == KT - 1:
                                ins.then_inc(pe_done, 1)

                def prologue():
                    for b in range(2):
                        first_unit(b)

                def step(i, u, last):
                    j, lot, n = 2 * i + u, 6 * i, 2 + 3 * u
                    if not last:
                        unit(0, lot, n, j + 1)
                        n += 1
                    W.take(pe, lot, n)
                    pe.wait_ge(m_split, NH * (j + 1))
                    hi, lo = W.hi[:, n % 2, :], W.lo[:, n % 2, :]
                    for o in range(OUTS):
                        rows, cols = slice(o // NH * P, (o // NH + 1) * P), slice((o % NH) * HALF, (o % NH + 1) * HALF)
                        pe.wait_ge(out_free, OUTS * j + o + 1)
                        for q, (m, w) in enumerate(((m_hi, hi), (m_hi, lo), (m_lo, hi))):
                            ins = nc.tensor.matmul(outs[o % 4][:], m[:, rows], w[:, cols], start=(q == 0), stop=(q == 2))
                        ins.then_inc(pe_done, 1)
                    if not last:
                        unit(1, lot, n + 1, j + 1)
                steps(pe, prologue, step)


def feed_forward(nc, hT, w_gate, w_up, w_down, y, out, W):
    CHUNK = 2
    N = FF // P // CHUNK
    OUTS = TT * NH
    ROUND = 4 * CHUNK + OUTS
    with ExitStack() as ctx:
        sb = lambda n, shape, dt=F32: ctx.enter_context(nc.sbuf_tensor(f"ff_{n}", shape, dt))
        sem = lambda n: ctx.enter_context(nc.semaphore(f"ff_{n}"))
        hid_hi = sb("hid_hi", [P, 2, CHUNK, S], F32R)
        hid_lo = sb("hid_lo", [P, 2, CHUNK, S], F32R)
        act_buf = sb("act", [P, NH, HALF])
        ps = lambda n: ctx.enter_context(nc.psum_tensor(f"ff_{n}", [P, HALF], F32))
        gate, up = [ps(f"gate{h}") for h in range(NH)], [ps(f"up{h}") for h in range(NH)]
        down = [ps(f"down{i}") for i in range(4)]
        pe_done = sem("pe_done")
        sig_done = sem("sig_done")
        silu_done = sem("silu_done")
        gu_free = sem("gu_free")
        hi_done, lo_done = sem("hi_done"), sem("lo_done")
        d_free = sem("d_free")
        out_done = sem("out_done")
        base = lambda c: 8 + ROUND * c
        tiles = lambda k: 12 * k

        def steps(eng, prologue, step):
            prologue()
            with eng.Fori(0, (N - 1) // 2, 1) as k:
                for j in range(2):
                    step(k, j, False)
            step((N - 1) // 2, 0, True)

        with nc.Block() as block:
            @block.sync
            def _(sp):
                def units(k, first, col, skip=0):
                    for n, w in list(enumerate((w_gate, w_up, w_gate, w_up)))[skip:]:
                        W.load(sp, tiles(k), first + n, weight_cols(w, col + (n // 2) * P))

                def step(k, j, last):
                    if not last:
                        units(k, 4 + 6 * j, k * (4 * P) + (j + 1) * 2 * P)
                    for f in range(CHUNK):
                        row = k * (4 * P) + (2 * j + f) * P
                        W.load(sp, tiles(k), 4 + 6 * j + f + (0 if last else 4),
                               w_down[ds(row, P), :].rearrange("p (k c) -> p k c", k=KT))
                steps(sp, lambda: units(0, 0, 0, skip=3), step)
                for t in range(TT):
                    sp.wait_ge(d_free, 4 + OUTS * (N - 1) + NH * (t + 1))
                    sp.dma_start(out[t * P:(t + 1) * P, :], y[:, t, :]).then_inc(out_done, 16)
                sp.wait_ge(out_done, 16 * TT)

            @block.gpsimd
            def _(pool):
                def prologue():
                    W.split(pool, 0, 3, (pe_done, 2))

                def step(k, j, last):
                    c = 2 * k + j
                    done = [base(c) - 4, base(c), base(c), base(c) + 2, base(c) + 4, base(c) + 6]
                    for n in range(2 if last else 6):
                        W.split(pool, tiles(k), 4 + 6 * j + n, (pe_done, done[n]))
                steps(pool, prologue, step)

            @block.tensor
            def _(pe):
                def units(k, first, chunk):
                    for n in range(4):
                        W.take(pe, tiles(k), first + n)
                        for half in range(NH):
                            f = n // 2
                            if n % 2 == 0:
                                pe.wait_ge(gu_free, 2 * (2 * chunk + f) + half + 1)
                            acc = (gate, up)[n % 2][half]
                            project_part(nc, acc[:], W.tile(first + n), hT, half, 0, 1).then_inc(pe_done, 1)

                def step(k, j, last):
                    c = 2 * k + j
                    if not last:
                        units(k, 4 + 6 * j, c + 1)
                    first = 4 + 6 * j + (0 if last else 4)
                    for f in range(CHUNK):
                        W.take(pe, tiles(k), first + f)
                    pe.wait_ge(lo_done, 2 * CHUNK * (c + 1))
                    w = [(W.hi[:, (first + f) % 3, :], W.lo[:, (first + f) % 3, :]) for f in range(CHUNK)]
                    for o in range(OUTS):
                        t, nh = o // NH, o % NH
                        pe.wait_ge(d_free, OUTS * c + o + 1)
                        rows, cols = slice(t * P, (t + 1) * P), slice(nh * HALF, (nh + 1) * HALF)
                        for n in range(3 * CHUNK):
                            f, kind = n // 3, n % 3
                            h = (hid_hi, hid_hi, hid_lo)[kind][:, j, f, rows]
                            ins = nc.tensor.matmul(down[o % 4][:], h, w[f][(0, 1, 0)[kind]][:, cols],
                                                   start=(n == 0), stop=(n == 3 * CHUNK - 1))
                        ins.then_inc(pe_done, 1)
                steps(pe, lambda: units(0, 0, 0), step)

            @block.scalar
            def _(act):
                def units(at, chunk, buf):
                    for f in range(CHUNK):
                        for half in range(NH):
                            num = 2 * CHUNK * chunk + 2 * f + half
                            act.wait_ge(pe_done, at + 4 * f + half + 1)
                            need(act, lo_done, num - 1)
                            nc.scalar.activation(act_buf[:, half, :], gate[half][:], ACT.Sigmoid).then_inc(sig_done, 1)
                            act.wait_ge(gu_free, num + 3)
                            nc.scalar.copy(hid_hi[:, buf, f, half * HALF:(half + 1) * HALF], act_buf[:, half, :]
                                           ).then_inc(hi_done, 1)

                def step(k, j, last):
                    if not last:
                        units(base(2 * k + j), 2 * k + (j + 1), (j + 1) % 2)
                steps(act, lambda: units(0, 0, 0), step)

            @block.vector
            def _(dve):
                dve.sem_inc(gu_free, 2)
                dve.sem_inc(d_free, 4)

                def units(at, chunk, buf):
                    for f in range(CHUNK):
                        for half in range(NH):
                            num, a = 2 * CHUNK * chunk + 2 * f + half, act_buf[:, half, :]
                            dve.wait_ge(sig_done, num + 1)
                            nc.vector.tensor_tensor(a, gate[half][:], a, ALU.mult).then_inc(silu_done, 1)
                            dve.wait_ge(silu_done, num + 1)
                            dve.wait_ge(pe_done, at + 4 * f + 2 + half + 1)
                            nc.vector.tensor_tensor(a, up[half][:], a, ALU.mult).then_inc(gu_free, 1)
                            dve.wait_ge(hi_done, num + 1)
                            cols = slice(half * HALF, (half + 1) * HALF)
                            nc.vector.tensor_tensor(hid_lo[:, buf, f, cols], a, hid_hi[:, buf, f, cols],
                                                    ALU.subtract).then_inc(lo_done, 1)

                def step(k, j, last):
                    c = 2 * k + j
                    if not last:
                        units(base(c), 2 * k + (j + 1), (j + 1) % 2)
                    first = base(c) + (0 if last else 4 * CHUNK)
                    for o in range(OUTS):
                        t, nh = o // NH, o % NH
                        at = y[:, t, nh * HALF:(nh + 1) * HALF]
                        dve.wait_ge(pe_done, first + o + 1)
                        nc.vector.tensor_tensor(at, down[o % 4][:], at, ALU.add).then_inc(d_free, 1)
                steps(dve, lambda: units(0, 0, 0), step)


def layer(nc, x, norm1_g, w_in, sb_q_norm_g, sb_k_norm_g, gla_gate_w2, gla_gate_b, gla_out_norm_g,
          w_branch_sb, w_branch_gla, w_out, norm2_g, w_ffn_gate, w_ffn_up, w_ffn_down, out):
    scratch = lambda n, rows: nc.dram_tensor(n, [rows, S], F32, kind="Internal").ap()
    osb_t, ogla_t = scratch("osb_t", D), scratch("ogla_t", D)
    gates_t = scratch("gates_t", 2 * D)
    with ExitStack() as ctx:
        c = constants(nc, ctx)
        W = Weights(nc, ctx, "w", 2)
        sb = lambda stack, n, shape, dt=F32: stack.enter_context(nc.sbuf_tensor(n, shape, dt))
        g_all, ssq = sb(ctx, "g_all", [P, D]), sb(ctx, "ssq", [P, TT])
        ot = g_all
        ot_out = ctx.enter_context(nc.semaphore("sb_ot_out"))
        with ExitStack() as heads:
            hT = [sb(heads, f"h1_{n}", [P, KT, S], F32R) for n in ("hi", "lo")]
            with ExitStack() as first:
                x_sb = sb(first, "x_sb", [P, TT, D])
                norm_transposed(nc, c, "norm1", x[0], x_sb, g_all, ssq, norm1_g, hT, W,
                                [weight_cols(w_in[0], col) for col in (GLQ, GLK)])
            linear_attention(nc, c, hT, w_in[0], gla_gate_w2[0], gla_gate_b, gla_out_norm_g, ogla_t, gates_t, W,
                             [weight_cols(w_in[0], col) for col in (SBK, SBQ)])
            W.next_phase(GLA_TILES)
            branch_weights = w_branch_sb[0], w_branch_gla[0]
            stick_breaking(nc, c, hT, w_in[0], (sb_q_norm_g, sb_k_norm_g), osb_t, gates_t, W,
                           [weight_cols(w, 0) for w in branch_weights], ot, ot_out)
            W.next_phase(SB_TILES)
        y = sb(ctx, "y", [P, TT, D])
        merge_and_project(nc, (osb_t, ogla_t), ot_out, gates_t, branch_weights, w_out[0], x[0], y, W,
                          ot, ssq)
        W = Weights(nc, ctx, "ffw", 3)
        hT = [sb(ctx, f"h2_{n}", [P, KT, S], F32R) for n in ("hi", "lo")]
        norm_transposed(nc, c, "norm2", None, y, g_all, ssq, norm2_g, hT, W,
                        [weight_cols(w_ffn_gate[0], 0), weight_cols(w_ffn_up[0], 0), weight_cols(w_ffn_gate[0], P)])
        feed_forward(nc, hT, w_ffn_gate[0], w_ffn_up[0], w_ffn_down[0], y, out[0], W)


_INS = ["x", "norm1_g", "w_in", "sb_q_norm_g", "sb_k_norm_g", "gla_gate_w2", "gla_gate_b", "gla_out_norm_g",
        "w_branch_sb", "w_branch_gla", "w_out", "norm2_g", "w_ffn_gate", "w_ffn_up", "w_ffn_down"]


def kernel(**inputs):
    import concourse.bacc as bacc
    from concourse.bass_utils import run_bass_kernel_spmd

    nc = bacc.Bacc("TRN2", target_bir_lowering=False, num_devices=1)
    arrays = {n: np.ascontiguousarray(inputs[n]) for n in _INS}
    args = [nc.dram_tensor(n, a.shape, mybir.dt.from_np(a.dtype), kind="ExternalInput").ap()
            for n, a in arrays.items()]
    out = nc.dram_tensor("out", [1, S, D], F32, kind="ExternalOutput").ap()
    layer(nc, *args, out)
    result = run_bass_kernel_spmd(nc, [arrays], core_ids=[0])
    return result.results[0]["out"]
```
